# Optimizing a Trainium2 kernel written in Bass

```python
import jax, jax.numpy as jnp
from jax import lax
import numpy as np

D_MODEL = 1024
BATCH = 1
SEQ = 2048
DEPTH = 1

CHUNK = 64
N_META = 16
HEAD_DIM = 64
A_HEADS = 8
A_KV_HEADS = 2
A_WINDOW = 128
A_WINDOW_CHUNKS = A_WINDOW // CHUNK
B_HEADS = 8
B_KV_RANK = 128
IDX_HEADS = 8
IDX_DIM = 64
TOPK_MAX = 256
B_Q_BLOCK = 64
D_FF = -(-8 * D_MODEL // (3 * 256)) * 256
DEEPNORM_ALPHA = (2 * DEPTH) ** 0.25
DEEPNORM_BETA = (8 * DEPTH) ** -0.25
A_Q = A_HEADS * HEAD_DIM
A_KV = A_KV_HEADS * HEAD_DIM
B_Q = B_HEADS * HEAD_DIM
IN_COLS = (A_Q, A_KV, A_KV, B_Q, B_KV_RANK, IDX_HEADS * IDX_DIM, IDX_DIM, IDX_HEADS, 2 * D_MODEL)
IN_WIDTH = sum(IN_COLS)

kernel_name = "hybrid_swa_sink_dsa_gated_deepnorm"

def layer_norm(x, g, b, eps=1e-5):
    xf = x.astype(jnp.float32)
    mu = jnp.mean(xf, axis=-1, keepdims=True)
    xc = xf - mu
    var = jnp.mean(xc * xc, axis=-1, keepdims=True)
    return (xc * lax.rsqrt(var + eps) * g.astype(jnp.float32) + b.astype(jnp.float32)).astype(x.dtype)

def rms_norm(x, g, eps=1e-6):
    xf = x.astype(jnp.float32)
    ms = jnp.mean(xf * xf, axis=-1, keepdims=True)
    return (xf * lax.rsqrt(ms + eps) * g.astype(jnp.float32)).astype(x.dtype)

def alibi_slopes(n):
    return 2.0 ** (-8.0 * jnp.arange(1, n + 1, dtype=jnp.float32) / n)

def chunk_index(pos):
    return jnp.where(pos < N_META, 0, 1 + (pos - N_META) // CHUNK)

def softmax_with_sink(logits, sink):
    sink_col = jnp.broadcast_to(sink, logits.shape[:-1] + (1,))
    p = jax.nn.softmax(jnp.concatenate([logits, sink_col], axis=-1), axis=-1)
    return p[..., :-1]

def swa_sink_attention(q, k, v, sinks):
    B, L, _ = q.shape
    S = L - N_META
    NC = S // CHUNK
    G = A_HEADS // A_KV_HEADS
    WC = A_WINDOW_CHUNKS * CHUNK
    q = q.reshape(B, L, A_KV_HEADS, G, HEAD_DIM) * (HEAD_DIM ** -0.5)
    k = k.reshape(B, L, A_KV_HEADS, HEAD_DIM)
    v = v.reshape(B, L, A_KV_HEADS, HEAD_DIM)
    slopes = alibi_slopes(A_HEADS).reshape(A_KV_HEADS, G)
    sink = sinks.astype(jnp.float32).reshape(A_KV_HEADS, G)[:, :, None, None]
    qm, km, vm = q[:, :N_META], k[:, :N_META], v[:, :N_META]

    pm = jnp.arange(N_META)
    dist_mm = jnp.abs(pm[:, None] - pm[None, :]).astype(jnp.float32)
    s_mm = jnp.einsum('bqkgd,bskd->bkgqs', qm, km).astype(jnp.float32) - slopes[:, :, None, None] * dist_mm
    p_mm = softmax_with_sink(s_mm, sink).astype(v.dtype)
    o_m = jnp.einsum('bkgqs,bskd->bqkgd', p_mm, vm).reshape(B, N_META, A_Q)

    qr = q[:, N_META:].reshape(B, NC, CHUNK, A_KV_HEADS, G, HEAD_DIM)
    kr = k[:, N_META:].reshape(B, NC, CHUNK, A_KV_HEADS, HEAD_DIM)
    vr = v[:, N_META:].reshape(B, NC, CHUNK, A_KV_HEADS, HEAD_DIM)

    def band(t):
        pad = ((0, 0), (A_WINDOW_CHUNKS - 1, 0), (0, 0), (0, 0), (0, 0))
        tp = jnp.pad(t, pad)
        parts = [tp[:, A_WINDOW_CHUNKS - 1 - w: A_WINDOW_CHUNKS - 1 - w + NC] for w in range(A_WINDOW_CHUNKS - 1, -1, -1)]
        return jnp.concatenate(parts, axis=2)

    kb, vb = band(kr), band(vr)
    c_ids = jnp.arange(NC)
    q_off = jnp.arange(CHUNK)
    j_off = jnp.arange(WC)
    m_ids = jnp.arange(N_META)
    dist_meta = (N_META + c_ids[:, None, None] * CHUNK + q_off[None, :, None] - m_ids[None, None, :]).astype(jnp.float32)
    dist_band = jnp.abs((A_WINDOW_CHUNKS - 1) * CHUNK + q_off[:, None] - j_off[None, :]).astype(jnp.float32)
    band_valid = (c_ids[:, None] - (A_WINDOW_CHUNKS - 1) + j_off[None, :] // CHUNK) >= 0

    s_meta = jnp.einsum('bcqkgd,bmkd->bckgqm', qr, km).astype(jnp.float32)
    s_meta = s_meta - slopes[None, :, :, None, None] * dist_meta[:, None, None]
    s_band = jnp.einsum('bcqkgd,bcskd->bckgqs', qr, kb).astype(jnp.float32)
    s_band = s_band - slopes[:, :, None, None] * dist_band
    s_band = jnp.where(band_valid[:, None, None, None, :], s_band, -jnp.inf)
    p = softmax_with_sink(jnp.concatenate([s_meta, s_band], axis=-1), sink).astype(v.dtype)
    o_r = (jnp.einsum('bckgqm,bmkd->bcqkgd', p[..., :N_META], vm)
           + jnp.einsum('bckgqs,bcskd->bcqkgd', p[..., N_META:], vb)).reshape(B, S, A_Q)
    return jnp.concatenate([o_m, o_r], axis=1)

def dsa_mla_attention(q, c_kv, q_idx, k_idx, w_idx, w_uk, w_uv, topk):
    B, L, _ = q.shape
    n_blk = -(-L // B_Q_BLOCK)
    L_pad = n_blk * B_Q_BLOCK
    q_pos = jnp.arange(L_pad)
    q_chunk = chunk_index(q_pos)
    k_chunk = chunk_index(jnp.arange(L))
    slopes = alibi_slopes(B_HEADS)
    k_idx32 = k_idx.astype(jnp.float32)

    def to_blocks(t):
        t = jnp.pad(t, [(0, 0), (0, L_pad - L)] + [(0, 0)] * (t.ndim - 2))
        return jnp.moveaxis(t.reshape((B, n_blk, B_Q_BLOCK) + t.shape[2:]), 1, 0)

    xs = (to_blocks(q.reshape(B, L, B_HEADS, HEAD_DIM)),
          to_blocks(q_idx.reshape(B, L, IDX_HEADS, IDX_DIM)),
          to_blocks(w_idx),
          q_pos.reshape(n_blk, B_Q_BLOCK),
          q_chunk.reshape(n_blk, B_Q_BLOCK))

    def block(args):
        qb, qib, wb, tpos, tchunk = args
        visible = k_chunk[None, :] <= tchunk[:, None]
        rel = jax.nn.relu(jnp.einsum('bqhd,bsd->bqhs', qib.astype(jnp.float32), k_idx32))
        score = jnp.einsum('bqh,bqhs->bqs', wb.astype(jnp.float32), rel)
        score = jnp.where(visible[None], score, -jnp.inf)
        top_val, top_idx = lax.top_k(score, topk)
        valid = top_val > -jnp.inf
        c_sel = jax.vmap(lambda c, i: c[i])(c_kv, top_idx)
        q_lat = jnp.einsum('bqhd,hrd->bqhr', qb, w_uk)
        logits = jnp.einsum('bqhr,bqkr->bhqk', q_lat, c_sel).astype(jnp.float32) * (HEAD_DIM ** -0.5)
        dist = jnp.abs(tpos[None, :, None] - top_idx).astype(jnp.float32)
        logits = logits - slopes[None, :, None, None] * dist[:, None]
        logits = jnp.where(valid[:, None], logits, -jnp.inf)
        p = jax.nn.softmax(logits, axis=-1).astype(c_sel.dtype)
        ctx = jnp.einsum('bhqk,bqkr->bqhr', p, c_sel)
        o = jnp.einsum('bqhr,hrd->bqhd', ctx, w_uv)
        return o.reshape(B, B_Q_BLOCK, B_Q)

    out = lax.map(block, xs)
    return jnp.moveaxis(out, 0, 1).reshape(B, L_pad, B_Q)[:, :L]

def hybrid_layer(h, w_in, b_gate, kv_norm_g, w_uk, w_uv, k_idx_g, k_idx_b, sinks, w_o_a, w_o_b, w_out,
                 ln1_g, ln1_b, w_ff_gate, w_ff_up, w_ff_down, ln2_g, ln2_b, topk):
    proj = h @ w_in
    split_points = np.cumsum(IN_COLS)[:-1].tolist()
    qa, ka, va, qb, cb, qi, ki, wi, gates = jnp.split(proj, split_points, axis=-1)
    y_a = swa_sink_attention(qa, ka, va, sinks) @ w_o_a
    c_kv = rms_norm(cb, kv_norm_g)
    k_idx = layer_norm(ki, k_idx_g, k_idx_b)
    w_idx = wi * (IDX_HEADS ** -0.5 * IDX_DIM ** -0.5)
    y_b = dsa_mla_attention(qb, c_kv, qi, k_idx, w_idx, w_uk, w_uv, topk) @ w_o_b
    g = jax.nn.sigmoid(gates + b_gate)
    g_a, g_b = g[..., :D_MODEL], g[..., D_MODEL:]
    mix = (g_a * y_a + g_b * y_b) @ w_out
    h = layer_norm(DEEPNORM_ALPHA * h + mix, ln1_g, ln1_b)
    ff = (jax.nn.silu(h @ w_ff_gate) * (h @ w_ff_up)) @ w_ff_down
    return layer_norm(DEEPNORM_ALPHA * h + ff, ln2_g, ln2_b)

def setup_inputs(seed: int = 0) -> dict:
    key = jax.random.key(seed)
    ks = jax.random.split(key, 24)

    def nrm(k, shape, scale):
        return jax.random.normal(k, shape, jnp.float32) * scale

    beta = DEEPNORM_BETA
    return {
        "x": nrm(ks[0], (BATCH, SEQ, D_MODEL), 1.0),
        "meta_tokens": nrm(ks[1], (N_META, D_MODEL), 1.0),
        "ln0_g": 1.0 + nrm(ks[2], (D_MODEL,), 0.02),
        "ln0_b": nrm(ks[3], (D_MODEL,), 0.02),
        "w_in": nrm(ks[4], (DEPTH, D_MODEL, IN_WIDTH), D_MODEL ** -0.5),
        "b_gate": nrm(ks[5], (DEPTH, 2 * D_MODEL), 0.02),
        "kv_norm_g": 1.0 + nrm(ks[6], (DEPTH, B_KV_RANK), 0.02),
        "w_uk": nrm(ks[7], (DEPTH, B_HEADS, B_KV_RANK, HEAD_DIM), B_KV_RANK ** -0.5),
        "w_uv": nrm(ks[8], (DEPTH, B_HEADS, B_KV_RANK, HEAD_DIM), B_KV_RANK ** -0.5),
        "k_idx_g": 1.0 + nrm(ks[9], (DEPTH, IDX_DIM), 0.02),
        "k_idx_b": nrm(ks[10], (DEPTH, IDX_DIM), 0.02),
        "sinks": nrm(ks[11], (DEPTH, A_HEADS), 0.5),
        "w_o_a": nrm(ks[12], (DEPTH, A_Q, D_MODEL), A_Q ** -0.5 * beta),
        "w_o_b": nrm(ks[13], (DEPTH, B_Q, D_MODEL), B_Q ** -0.5 * beta),
        "w_out": nrm(ks[14], (DEPTH, D_MODEL, D_MODEL), D_MODEL ** -0.5 * beta),
        "ln1_g": 1.0 + nrm(ks[15], (DEPTH, D_MODEL), 0.02),
        "ln1_b": nrm(ks[16], (DEPTH, D_MODEL), 0.02),
        "w_ff_gate": nrm(ks[17], (DEPTH, D_MODEL, D_FF), D_MODEL ** -0.5),
        "w_ff_up": nrm(ks[18], (DEPTH, D_MODEL, D_FF), D_MODEL ** -0.5),
        "w_ff_down": nrm(ks[19], (DEPTH, D_FF, D_MODEL), D_FF ** -0.5 * beta),
        "ln2_g": 1.0 + nrm(ks[20], (DEPTH, D_MODEL), 0.02),
        "ln2_b": nrm(ks[21], (DEPTH, D_MODEL), 0.02),
    }

def reference(x, meta_tokens, ln0_g, ln0_b, w_in, b_gate, kv_norm_g, w_uk, w_uv, k_idx_g, k_idx_b, sinks,
              w_o_a, w_o_b, w_out, ln1_g, ln1_b, w_ff_gate, w_ff_up, w_ff_down, ln2_g, ln2_b):
    B, S, D = x.shape
    topk = min(TOPK_MAX, S // 4)
    meta = jnp.broadcast_to(meta_tokens[None].astype(x.dtype), (B, N_META, D))
    h = layer_norm(jnp.concatenate([meta, x], axis=1), ln0_g, ln0_b)
    for l in range(DEPTH):
        h = hybrid_layer(h, w_in[l], b_gate[l], kv_norm_g[l], w_uk[l], w_uv[l], k_idx_g[l], k_idx_b[l], sinks[l],
                         w_o_a[l], w_o_b[l], w_out[l], ln1_g[l], ln1_b[l], w_ff_gate[l], w_ff_up[l], w_ff_down[l],
                         ln2_g[l], ln2_b[l], topk)
    return h[:, N_META:]


_drawn_inputs = setup_inputs


def setup_inputs(seed=0):
    import zlib

    import numpy as np

    out = dict(_drawn_inputs(seed))
    spreads = {}
    factors = {'meta_tokens': 8.0,
     'b_gate': 8.0,
     'kv_norm_g': 8.0,
     'k_idx_g': 5.134,
     'k_idx_b': 6.364,
     'sinks': 8.0,
     'ln1_g': 2.748,
     'ln1_b': 2.729,
     'ln2_g': 2.953,
     'ln2_b': 2.749}
    for name, (base, spread) in spreads.items():
        noise = np.random.default_rng([zlib.crc32(name.encode()), seed]).standard_normal(out[name].shape)
        drawn = base * np.exp(spread * noise) if base else spread * noise
        out[name] = __import__('jax').numpy.asarray(drawn.astype(out[name].dtype))
    for name, factor in factors.items():
        out[name] = (out[name] * factor).astype(out[name].dtype)
    return out
```

```python
from contextlib import ExitStack

import concourse.bass as bass
from concourse import mybir

ALU = mybir.AluOpType
ACT = mybir.ActivationFunctionType
AX = mybir.AxisListType.X
F32 = mybir.dt.float32
F32R = mybir.dt.float32r
I32 = mybir.dt.int32

P = 128
D = 1024
KT = D // P
SEQ = 2048
META = 16
L = SEQ + META
CHUNK = 64
HEADS = 8
DH = 64
TOPK = 256
DFF = 2816
FT = DFF // P
GROUP = 512
NG = SEQ // GROUP
TPG = GROUP // P
ALPHA = 2.0 ** 0.25
PAD = CHUNK
LP = L + PAD
BIG = 1e37
START = 1
MARK = -3e38
R_QA, R_KA, R_VA, R_QB, R_CB, R_QI, R_KI, R_WI, R_GATE = 0, 512, 640, 768, 1280, 1408, 1920, 1984, 2048
SPLIT_CHUNKS = 16
GATE_COL = 1992
WIN = 2 * CHUNK + CHUNK
WA = META + WIN
WH = WA // 2


def f32(ap):
    return ap.bitcast(F32)


class Scope(ExitStack):

    def __init__(self, nc, tag):
        super().__init__()
        self.nc, self.tag, self.all_sems = nc, tag, []

    def sb(self, name, shape, dt=F32):
        return self.enter_context(self.nc.sbuf_tensor(f"{self.tag}_{name}", shape, dt))

    def ps(self, name, shape):
        return self.enter_context(self.nc.psum_tensor(f"{self.tag}_{name}", shape, F32))

    def sem(self, name):
        self.all_sems.append(self.enter_context(self.nc.semaphore(f"{self.tag}_{name}")))
        return self.all_sems[-1]

    def begin(self, sp):
        for sem in self.all_sems:
            sp.sem_inc(sem, START)

    def sems(self, name, n=2):
        return [self.sem(f"{name}{i}") for i in range(n)]


def matmul3(pe, out, lhs_hi, lhs_lo, rhs_hi, rhs_lo, start, stop):
    pe.matmul(out, lhs_lo, rhs_hi, start=start, stop=False)
    pe.matmul(out, lhs_hi, rhs_hi, start=False, stop=False)
    return pe.matmul(out, lhs_hi, rhs_lo, start=False, stop=stop)


def make_identity(nc, pool, ident, ready):
    pool.memset(ident[:, :], 0.0)
    pool.drain()
    pool.affine_select(out=ident[:, :], in_=ident[:, :], compare_op=ALU.not_equal, fill=1.0, base=0,
                       pattern=[[-1, P]], channel_multiplier=1).then_inc(ready, 1)


def project(nc, x, meta_tokens, ln0_g, ln0_b, w_in, b_gate, h0, proj, v_nat):
    with Scope(nc, "pj") as s:
        h_hi, h_lo = s.sb("h_hi", [P, KT, L], F32R), s.sb("h_lo", [P, KT, L], F32R)
        ident = s.sb("ident", [P, P])
        zeros = s.sb("zeros", [P, PAD])
        half = s.sb("half", [P, 1])
        id_ready, zero_ready, zero_stored = s.sem("id_ready"), s.sem("zero_ready"), s.sem("zero_stored")
        with Scope(nc, "ln") as a:
            xt = [a.sb(f"x{u}", [P, D]) for u in range(2)]
            hb = [a.sb(f"h{u}", [P, D]) for u in range(2)]
            gain, shift = a.sb("gain", [P, D]), a.sb("shift", [P, D])
            stats = [a.sb(f"stats{u}", [P, 2, 6]) for u in range(2)]
            mean_var = [a.sb(f"mv{u}", [P, 2]) for u in range(2)]
            var_eps = [a.sb(f"ve{u}", [P, 1]) for u in range(2)]
            rstd = [a.sb(f"rstd{u}", [P, 1]) for u in range(2)]
            turned = [a.ps(f"turned{u}", [P, KT, P]) for u in range(2)]
            gb_loaded = a.sem("gb_loaded")
            x_loaded, x_free = a.sems("x_loaded"), a.sems("x_free")
            var_ready, rstd_ready = a.sems("var_ready"), a.sems("rstd_ready")
            h_ready, h_stored = a.sems("h_ready"), a.sems("h_stored")
            turned_ready, hi_ready, turned_free = a.sems("turned_ready"), a.sems("hi_ready"), a.sems("turned_free")

            def tiles(eng, step):
                step(0, 0, META, None)
                with eng.Fori(0, SEQ // P // 2) as i:
                    step(1, i, P, 2 * P * i)
                    step(0, i + 1, P, 2 * P * i + P)

            with nc.Block() as block:
                @block.sync
                def _(sp):
                    s.begin(sp)
                    a.begin(sp)
                    sp.dma_start(gain[:, :], ln0_g.rearrange("(a d) -> a d", a=1).to_broadcast([P, D])).then_inc(gb_loaded, 16)
                    sp.dma_start(shift[:, :], ln0_b.rearrange("(a d) -> a d", a=1).to_broadcast([P, D])).then_inc(gb_loaded, 16)

                    def load(u, k, n, r):
                        sp.wait_ge(x_free[u], k + START)
                        src = meta_tokens if r is None else x[0, bass.ds(r, P), :]
                        sp.dma_start(xt[u][0:n, :], src).then_inc(x_loaded[u], 16)

                    tiles(sp, load)
                    sp.wait_ge(zero_ready, 1 + START)
                    sp.dma_start(proj[R_KA:R_KA + P, 0:PAD], zeros[:, :]).then_inc(zero_stored, 16)
                    for half_cols in range(2):
                        sp.dma_start(v_nat[0:PAD, half_cols * 64:half_cols * 64 + 64], zeros[0:PAD, :]).then_inc(zero_stored, 16)
                    sp.wait_ge(zero_stored, 48 + START)

                @block.gpsimd
                def _(pool):
                    make_identity(nc, pool, ident, id_ready)
                    pool.memset(half[:, :], -0.5)
                    pool.memset(zeros[:, :], 0.0).then_inc(zero_ready, 1)
                    pool.drain()

                    def inverse_root(u, k, n, r):
                        pool.wait_ge(var_ready[u], k + 1 + START)
                        pool.tensor_tensor(rstd[u][0:n, :], var_eps[u][0:n, :], half[0:n, :], ALU.pow).then_inc(rstd_ready[u], 1)

                    tiles(pool, inverse_root)

                @block.vector
                def _(dve):
                    def normalise(u, k, n, r=None):
                        dve.wait_ge(x_loaded[u], 16 * (k + 1) + START)
                        for c in range(2):
                            dve.bn_stats(stats[u][0:n, c, :], xt[u][0:n, c * 512:c * 512 + 512])
                        dve.drain()
                        dve.bn_aggr(mean_var[u][0:n, :], stats[u][0:n, :, :])
                        dve.drain()
                        dve.tensor_scalar(var_eps[u][0:n, :], mean_var[u][0:n, 1:2], 1e-5, None, ALU.add).then_inc(var_ready[u], 1)
                        dve.wait_ge(rstd_ready[u], k + 1 + START)
                        dve.wait_ge(turned_ready[u], k + START)
                        dve.wait_ge(h_stored[u], 16 * k + START)
                        dve.tensor_scalar(hb[u][0:n, :], xt[u][0:n, :], mean_var[u][0:n, 0:1], rstd[u][0:n, :],
                                          ALU.subtract, ALU.mult).then_inc(x_free[u], 1)
                        dve.drain()
                        dve.tensor_tensor(hb[u][0:n, :], hb[u][0:n, :], gain[0:n, :], ALU.mult)
                        dve.drain()
                        dve.tensor_tensor(hb[u][0:n, :], hb[u][0:n, :], shift[0:n, :], ALU.add).then_inc(h_ready[u], 1)

                    def low_part(u, k, n, col):
                        dve.wait_ge(hi_ready[u], k + 1 + START)
                        dve.tensor_tensor(h_lo[:, :, bass.ds(col, n)], turned[u][:, :, 0:n],
                                          f32(h_hi[:, :, bass.ds(col, n)]), ALU.subtract).then_inc(turned_free[u], 1)

                    dve.wait_ge(gb_loaded, 32 + START)
                    normalise(0, 0, META)
                    normalise(1, 0, P)
                    low_part(0, 0, META, 0)
                    with dve.Fori(0, SEQ // P // 2 - 1) as i:
                        normalise(0, i + 1, P)
                        low_part(1, i, P, META + 2 * P * i)
                        normalise(1, i + 1, P)
                        low_part(0, i + 1, P, META + 2 * P * i + P)
                    last = SEQ // P // 2
                    normalise(0, last, P)
                    low_part(1, last - 1, P, L - 2 * P)
                    low_part(0, last, P, L - P)

                @block.tensor
                def _(pe):
                    pe.wait_ge(id_ready, 1 + START)

                    def turn(u, k, n, r):
                        pe.wait_ge(h_ready[u], k + 1 + START)
                        pe.wait_ge(turned_free[u], k + START)
                        for c in range(KT):
                            last = pe.transpose(turned[u][:, c, 0:n], hb[u][0:n, c * P:c * P + P], ident[0:n, 0:n])
                        last.then_inc(turned_ready[u], 1)

                    tiles(pe, turn)

                @block.scalar
                def _(act):
                    def high_part(u, k, n, r):
                        act.wait_ge(h_ready[u], k + 1 + START)
                        dst = h0[0:META, :] if r is None else h0[bass.ds(r + META, P), :]
                        act.dma_start(dst, hb[u][0:n, :]).then_inc(h_stored[u], 16)
                        act.wait_ge(turned_ready[u], k + 1 + START)
                        col = 0 if r is None else r + META
                        act.activation(h_hi[:, :, bass.ds(col, n)], turned[u][:, :, 0:n], ACT.Copy).then_inc(hi_ready[u], 1)

                    tiles(act, high_part)
                    act.wait_ge(h_stored[0], 16 * 9 + START)
                    act.wait_ge(h_stored[1], 16 * 8 + START)

        with Scope(nc, "in") as a:
            raw = [a.sb(f"raw{u}", [P, KT, P]) for u in range(2)]
            w_hi = [a.sb(f"w_hi{u}", [P, KT, P], F32R) for u in range(2)]
            w_lo = [a.sb(f"w_lo{u}", [P, KT, P], F32R) for u in range(2)]
            row = [a.sb(f"row{u}", [P, L]) for u in range(2)]
            bias = [a.sb(f"bias{u}", [P, 1]) for u in range(2)]
            acc = [a.ps(f"acc{g}", [P, GROUP]) for g in range(NG)]
            acc_meta = [a.ps(f"acc_meta{u}", [P, GROUP]) for u in range(2)]
            w_loaded, hi_ready, lo_ready, w_free = a.sems("w_loaded"), a.sems("hi_ready"), a.sems("lo_ready"), a.sems("w_free")
            acc_ready = a.sems("acc_ready", NG)
            acc_free = a.sems("acc_free", NG + 1)
            stored = a.sems("stored")
            half_plain, half_all = SPLIT_CHUNKS // 2, SPLIT_CHUNKS

            with nc.Block() as block:
                @block.sync
                def _(sp):
                    a.begin(sp)
                    def load(u, k, gates):
                        sp.wait_ge(lo_ready[u], k + START)
                        first = (2 * k + u) * P
                        if gates:
                            first = first - (R_GATE - GATE_COL)
                        sp.dma_start(raw[u][:, :, :], w_in[0].rearrange("(k p) c -> p k c", p=P)[:, :, bass.ds(first, P)]).then_inc(w_loaded[u], 16)
                        if gates:
                            sp.wait_ge(acc_free[NG], 2 * k + u - 1 + START)
                            sp.dma_start(bias[u][:, :], b_gate[0].rearrange("(a b) -> a b", b=1)[bass.ds((2 * k + u) * P - R_GATE, P), :]).then_inc(w_loaded[u], 16)

                    def store(u, k):
                        for n in range(NG + 1):
                            sp.wait_ge(acc_free[n], 2 * k + u + 1 + START)
                        sp.dma_start(proj[bass.ds((2 * k + u) * P, P), PAD:LP], row[u][:, :]).then_inc(stored[u], 16)

                    load(0, 0, False)
                    load(1, 0, False)
                    with sp.Fori(0, half_plain - 1) as k:
                        for u in range(2):
                            store(u, k)
                            load(u, k + 1, False)
                    with sp.Fori(half_plain - 1, half_all - 1) as k:
                        for u in range(2):
                            store(u, k)
                            load(u, k + 1, True)
                    for u in range(2):
                        store(u, half_all - 1)
                    for u in range(2):
                        sp.wait_ge(stored[u], 16 * half_all + START)

                def loaded(eng, u, k, gates):
                    eng.wait_ge(w_loaded[u], (32 * (k + 1) - 16 * half_plain if gates else 16 * (k + 1)) + START)

                @block.gpsimd
                def _(pool):
                    with pool.Fori(0, half_all) as k:
                        for u in range(2):
                            pool.wait_ge(hi_ready[u], k + 1 + START)
                            pool.tensor_tensor(w_lo[u][:, :, :], raw[u][:, :, :], f32(w_hi[u][:, :, :]), ALU.subtract).then_inc(lo_ready[u], 1)

                @block.scalar
                def _(act):
                    def high_part(u, k, gates):
                        loaded(act, u, k, gates)
                        act.wait_ge(w_free[u], k + START)
                        act.activation(w_hi[u][:, :, :], raw[u][:, :, :], ACT.Copy).then_inc(hi_ready[u], 1)

                    def evacuate(u, k):
                        act.wait_ge(stored[u], 16 * k + START)
                        for g in (1, 3):
                            act.wait_ge(acc_ready[g], 2 * k + u + 1 + START)
                            act.activation(row[u][:, META + g * GROUP:META + (g + 1) * GROUP], acc[g][:, :], ACT.Copy).then_inc(acc_free[g], 1)

                    def gate(u, k):
                        act.wait_ge(stored[u], 16 * k + START)
                        for g in range(NG):
                            act.wait_ge(acc_ready[g], 2 * k + u + 1 + START)
                            act.activation(row[u][:, META + g * GROUP:META + (g + 1) * GROUP], acc[g][:, :], ACT.Sigmoid,
                                           bias=bias[u][:, :]).then_inc(acc_free[g], 1)
                        act.wait_ge(w_free[u], k + 1 + START)
                        act.activation(row[u][:, 0:META], acc_meta[u][:, 0:META], ACT.Sigmoid, bias=bias[u][:, :]).then_inc(acc_free[NG], 1)

                    high_part(0, 0, False)
                    with act.Fori(0, half_plain - 1) as k:
                        high_part(1, k, False)
                        evacuate(0, k)
                        high_part(0, k + 1, False)
                        evacuate(1, k)
                    high_part(1, half_plain - 1, False)
                    evacuate(0, half_plain - 1)
                    high_part(0, half_plain, True)
                    evacuate(1, half_plain - 1)
                    with act.Fori(half_plain, half_all - 1) as k:
                        high_part(1, k, True)
                        gate(0, k)
                        high_part(0, k + 1, True)
                        gate(1, k)
                    high_part(1, half_all - 1, True)
                    gate(0, half_all - 1)
                    gate(1, half_all - 1)

                @block.vector
                def _(dve):
                    with dve.Fori(0, half_plain) as k:
                        for u in range(2):
                            dve.wait_ge(stored[u], 16 * k + START)
                            for g in (0, 2):
                                dve.wait_ge(acc_ready[g], 2 * k + u + 1 + START)
                                dve.tensor_copy(row[u][:, META + g * GROUP:META + (g + 1) * GROUP], acc[g][:, :]).then_inc(acc_free[g], 1)
                            dve.wait_ge(w_free[u], k + 1 + START)
                            dve.tensor_copy(row[u][:, 0:META], acc_meta[u][:, 0:META]).then_inc(acc_free[NG], 1)

                @block.tensor
                def _(pe):
                    with pe.Fori(0, half_all) as k:
                        for u in range(2):
                            pe.wait_ge(hi_ready[u], k + 1 + START)
                            pe.wait_ge(lo_ready[u], k + 1 + START)
                            for g in range(NG + 1):
                                pe.wait_ge(acc_free[g], 2 * k + u + START)
                                out = acc[g][:, :] if g < NG else acc_meta[u][:, 0:META]
                                c0, c1 = (META + g * GROUP, META + (g + 1) * GROUP) if g < NG else (0, META)
                                for c in range(KT):
                                    last = matmul3(pe, out, w_hi[u][:, c, :], w_lo[u][:, c, :], h_hi[:, c, c0:c1],
                                                   h_lo[:, c, c0:c1], c == 0, c == KT - 1)
                                last.then_inc(acc_ready[g] if g < NG else w_free[u], 1)


def prepare_keys(nc, proj, kv_norm_g, k_idx_g, k_idx_b, v_nat, keys):
    c_nat, c_hi, c_lo, ki_hi, ki_lo = keys
    with Scope(nc, "ky") as s:
        ident, half = s.sb("ident", [P, P]), s.sb("half", [P, 2])
        cg, kg, kb = s.sb("cg", [P, P]), s.sb("kg", [P, DH]), s.sb("kb", [P, DH])
        cin = [s.sb(f"cin{u}", [P, P]) for u in range(2)]
        kin = [s.sb(f"kin{u}", [DH, P]) for u in range(2)]
        vin = [s.sb(f"vin{u}", [P, P]) for u in range(2)]
        junk = s.sb("junk", [P, P])
        stats = [s.sb(f"stats{u}", [P, 6]) for u in range(2)]
        mean_var = [s.sb(f"mv{u}", [P, 2]) for u in range(2)]
        square = [s.sb(f"square{u}", [P, 1]) for u in range(2)]
        var_eps = [s.sb(f"ve{u}", [P, 2]) for u in range(2)]
        rstd = [s.sb(f"rstd{u}", [P, 2]) for u in range(2)]
        cn = [s.sb(f"cn{u}", [P, P]) for u in range(2)]
        kn = [s.sb(f"kn{u}", [P, 2, DH]) for u in range(2)]
        vn = [s.sb(f"vn{u}", [P, P]) for u in range(2)]
        nat = [s.ps(f"nat{u}", [P, 512]) for u in range(2)]
        nat_k = [s.ps(f"nat_k{u}", [P, 512]) for u in range(2)]
        back = [s.ps(f"back{u}", [P, 512]) for u in range(2)]
        const_ready, g_loaded = s.sem("const_ready"), s.sem("g_loaded")
        loaded, nat_ready, square_ready = s.sems("loaded"), s.sems("nat_ready"), s.sems("square_ready")
        var_ready, rstd_ready, norm_ready, copied = s.sems("var_ready"), s.sems("rstd_ready"), s.sems("norm_ready"), s.sems("copied")
        back_ready, hi_ready, lo_ready, v_stored = s.sems("back_ready"), s.sems("hi_ready"), s.sems("lo_ready"), s.sems("v_stored")

        def tiles(eng, step):
            with eng.Fori(0, L // P // 2) as i:
                for u in range(2):
                    step(u, i, P, (2 * i + u) * P)
            step(0, L // P // 2, L % P, L - L % P)

        with nc.Block() as block:
            @block.sync
            def _(sp):
                s.begin(sp)
                sp.dma_start(cg[:, :], kv_norm_g.to_broadcast([P, P])).then_inc(g_loaded, 16)
                sp.dma_start(kg[:, :], k_idx_g.to_broadcast([P, DH])).then_inc(g_loaded, 16)
                sp.dma_start(kb[:, :], k_idx_b.to_broadcast([P, DH])).then_inc(g_loaded, 16)

                def load(u, k, n, j):
                    sp.wait_ge(nat_ready[u], k + START)
                    for dst, row, rows in ((cin, R_CB, P), (kin, R_KI, DH), (vin, R_VA, P)):
                        sp.dma_start(dst[u][0:rows, 0:n], proj[row:row + rows, bass.ds(j + PAD, n)]).then_inc(loaded[u], 16)

                tiles(sp, load)

            @block.gpsimd
            def _(pool):
                pool.memset(half[:, :], -0.5)
                make_identity(nc, pool, ident, const_ready)
                pool.drain()

                def step(u, k, n, j):
                    pool.wait_ge(var_ready[u], k + 1 + START)
                    pool.tensor_tensor(rstd[u][0:n, :], var_eps[u][0:n, :], half[0:n, :], ALU.pow).then_inc(rstd_ready[u], 1)
                    pool.wait_ge(norm_ready[u], k + 1 + START)
                    pool.tensor_copy(c_nat[0:n, bass.ds(j, P)], cn[u][0:n, :]).then_inc(copied[u], 1)

                tiles(pool, step)

            @block.tensor
            def _(pe):
                pe.wait_ge(const_ready, 1 + START)

                def step(u, k, n, j):
                    pe.wait_ge(loaded[u], 48 * (k + 1) + START)
                    pe.wait_ge(norm_ready[u], k + START)
                    pe.transpose(nat[u][0:n, 0:P], cin[u][:, 0:n], ident[:, :])
                    pe.transpose(nat_k[u][0:n, 0:DH], kin[u][:, 0:n], ident[0:DH, 0:DH])
                    pe.transpose(nat[u][0:n, P:2 * P], vin[u][:, 0:n], ident[:, :]).then_inc(nat_ready[u], 1)
                    pe.wait_ge(norm_ready[u], k + 1 + START)
                    pe.wait_ge(lo_ready[u], k + START)
                    pe.transpose(back[u][:, 0:n], cn[u][0:n, :], ident[0:n, 0:n])
                    pe.transpose(back[u][:, P:P + n], kn[u][0:n, :, :].rearrange("p a d -> p (a d)"), ident[0:n, 0:n]).then_inc(back_ready[u], 1)

                tiles(pe, step)

            @block.scalar
            def _(act):
                def step(u, k, n, j):
                    act.wait_ge(nat_ready[u], k + 1 + START)
                    act.wait_ge(v_stored[u], 16 * k + START)
                    act.activation(junk[0:n, :], nat[u][0:n, 0:P], ACT.Square, accum_out=square[u][0:n, :])
                    act.activation(vn[u][0:n, :], nat[u][0:n, P:2 * P], ACT.Copy).then_inc(square_ready[u], 1)
                    act.drain()
                    act.dma_start(v_nat[bass.ds(j + PAD, n), :], vn[u][0:n, :]).then_inc(v_stored[u], 16)
                    act.wait_ge(back_ready[u], k + 1 + START)
                    act.activation(c_hi[:, bass.ds(j, n)], back[u][:, 0:n], ACT.Copy)
                    act.activation(ki_hi[:, bass.ds(j, n)], back[u][:, P:P + n], ACT.Copy).then_inc(hi_ready[u], 1)

                tiles(act, step)
                act.wait_ge(v_stored[0], 16 * 9 + START)
                act.wait_ge(v_stored[1], 16 * 8 + START)

            @block.vector
            def _(dve):
                dve.wait_ge(g_loaded, 48 + START)

                def step(u, k, n, j):
                    dve.wait_ge(nat_ready[u], k + 1 + START)
                    dve.bn_stats(stats[u][0:n, :], nat_k[u][0:n, 0:DH])
                    dve.drain()
                    dve.bn_aggr(mean_var[u][0:n, :], stats[u][0:n, :])
                    dve.drain()
                    dve.tensor_scalar(var_eps[u][0:n, 1:2], mean_var[u][0:n, 1:2], 1e-5, None, ALU.add)
                    dve.wait_ge(square_ready[u], k + 1 + START)
                    dve.tensor_scalar(var_eps[u][0:n, 0:1], square[u][0:n, :], 1.0 / P, 1e-6, ALU.mult, ALU.add).then_inc(var_ready[u], 1)
                    dve.wait_ge(rstd_ready[u], k + 1 + START)
                    dve.wait_ge(back_ready[u], k + START)
                    dve.wait_ge(copied[u], k + START)
                    dve.scalar_tensor_tensor(out=cn[u][0:n, :], in0=nat[u][0:n, 0:P], scalar=rstd[u][0:n, 0:1], in1=cg[0:n, :], op0=ALU.mult, op1=ALU.mult)
                    dve.tensor_scalar(kn[u][0:n, 1, :], nat_k[u][0:n, 0:DH], mean_var[u][0:n, 0:1], rstd[u][0:n, 1:2], ALU.subtract, ALU.mult)
                    dve.drain()
                    dve.tensor_tensor(kn[u][0:n, 1, :], kn[u][0:n, 1, :], kg[0:n, :], ALU.mult)
                    dve.drain()
                    dve.tensor_tensor(kn[u][0:n, 0, :], kn[u][0:n, 1, :], kb[0:n, :], ALU.add)
                    dve.drain()
                    dve.tensor_copy(kn[u][0:n, 1, :], kn[u][0:n, 0, :]).then_inc(norm_ready[u], 1)
                    dve.wait_ge(hi_ready[u], k + 1 + START)
                    dve.tensor_tensor(c_lo[:, bass.ds(j, n)], back[u][:, 0:n], f32(c_hi[:, bass.ds(j, n)]), ALU.subtract)
                    dve.tensor_tensor(ki_lo[:, bass.ds(j, n)], back[u][:, P:P + n], f32(ki_hi[:, bass.ds(j, n)]), ALU.subtract).then_inc(lo_ready[u], 1)

                tiles(dve, step)


def attention(nc, proj, v_nat, w_uk, w_uv, sinks, attn, keys):
    c_nat, c_hi, c_lo, ki_hi, ki_lo = keys
    with Scope(nc, "at") as s:
        ident = s.sb("ident", [P, P])
        wuk = s.sb("wuk", [P, HEADS, DH])
        wuk_t = s.sb("wuk_t", [P, HEADS // 2, P])
        wuv = s.sb("wuv", [P, HEADS, DH])
        query_key = s.sb("query_key", [P, L])
        limit = s.sb("limit", [P, L])
        ints = s.sb("ints", [P, L], I32)
        base_a = s.sb("base_a", [P, WA])
        dist_a = s.sb("dist_a", [P, WA])
        pair_scale = s.sb("pair_scale", [P, HEADS // 2])
        slope, neg_slope, inv_slope = s.sb("slope", [P, HEADS]), s.sb("neg_slope", [P, HEADS]), s.sb("inv_slope", [P, HEADS])
        sink_u = s.sb("sink_u", [P, HEADS])
        minus_one = s.sb("minus_one", [P, HEADS])
        t_col, first_col = s.sb("t_col", [P, 1]), s.sb("first_col", [P, 1])
        qa, qb = s.sb("qa", [P, HEADS // 2, P]), s.sb("qb", [P, HEADS // 2, P])
        qa_s, qb_s = s.sb("qa_s", [P, HEADS // 2, P]), s.sb("qb_s", [P, HEADS // 2, P])
        qi = s.sb("qi", [P, HEADS, P])
        qi_2 = s.sb("qi_2", [P, HEADS, P], F32R)
        wi = s.sb("wi", [HEADS, P])
        w_idx = s.sb("w_idx", [P, HEADS])
        k_win = s.sb("k_win", [P, 2, WA])
        v_win = s.sb("v_win", [WH, 2, P])
        ql_hi, ql_lo = s.sb("ql_hi", [P, HEADS, P], F32R), s.sb("ql_lo", [P, HEADS, P], F32R)
        hidden = s.sb("hidden", [P, L])
        dist = s.sb("dist", [P, L])
        score = s.sb("score", [P, L])
        rel = [s.sb(f"rel{u}", [P, 1024]) for u in range(2)]
        rel_meta = s.sb("rel_meta", [P, HEADS, META])
        best = s.sb("best", [P, 8])
        u_a = s.sb("u_a", [P, HEADS, WA])
        max_a, bias_a, sink_e = s.sb("max_a", [P, HEADS]), s.sb("bias_a", [P, HEADS]), s.sb("sink_e", [P, HEADS])
        den_a, rden_a = s.sb("den_a", [P, HEADS]), s.sb("rden_a", [P, HEADS])
        u_meta = s.sb("u_meta", [P, HEADS, META])
        u_b = [s.sb(f"u_b{u}", [P, L]) for u in range(2)]
        max_b, max_1, bias_b = s.sb("max_b", [P, HEADS, 4]), s.sb("max_1", [P, HEADS]), s.sb("bias_b", [P, HEADS])
        den_b, rden_b = s.sb("den_b", [P, HEADS]), s.sb("rden_b", [P, HEADS])
        p_t = [s.sb(f"p_t{u}", [P, 4, P]) for u in range(2)]
        ctx_t = s.sb("ctx_t", [P, HEADS, P])
        o_nat = [s.sb(f"o_nat{b}", [P, HEADS * DH]) for b in range(2)]
        o_t = [s.sb(f"o_t{b}", [P, 4, P]) for b in range(2)]

        big = [s.ps(f"big{u}", [P, 1024]) for u in range(2)]
        turn = [s.ps(f"turn{u}", [P, 512]) for u in range(2)]
        misc, ctx = s.ps("misc", [P, 512]), s.ps("ctx", [P, 512])

        id_ready, const_ready, w_loaded = s.sem("id_ready"), s.sem("const_ready"), s.sem("w_loaded")
        iota_ready, iota_used, wukt_ready = s.sem("iota_ready"), s.sem("iota_used"), s.sem("wukt_ready")
        q_loaded, q_scaled, qi_hi, qi_lo = s.sem("q_loaded"), s.sem("q_scaled"), s.sem("qi_hi"), s.sem("qi_lo")
        win_done = s.sem("win_done")
        t_ready, dist_ready, dist_full = s.sem("t_ready"), s.sem("dist_ready"), s.sem("dist_full")
        big_ready, big_free = s.sems("big_ready"), s.sems("big_free")
        turn_ready, turn_free = s.sems("turn_ready"), s.sems("turn_free")
        pt_ready, pt_free = s.sems("pt_ready"), s.sems("pt_free")
        rel_ready, rel_free = s.sems("rel_ready"), s.sems("rel_free")
        misc_ready, misc_free = s.sem("misc_ready"), s.sem("misc_free")
        relm_ready, ql_hi_ready, ql_lo_ready = s.sem("relm_ready"), s.sem("ql_hi_ready"), s.sem("ql_lo_ready")
        stats_a, exp_a, rden_ready = s.sem("stats_a"), s.sem("exp_a"), s.sem("rden_ready")
        u_ready, p_ready, u_free = s.sem("u_ready"), s.sem("p_ready"), s.sems("u_free")
        ctx_ready, ctx_free = s.sem("ctx_ready"), s.sem("ctx_free")
        logits_seen = s.sem("logits_seen")
        o_ready, attn_stored = s.sem("o_ready"), s.sem("attn_stored")

        class Group:

            def __init__(self, g):
                self.g = g
                self.real = GROUP * (g + 1)
                self.width = META + self.real
                self.blocks = [(b, min(1024, self.real - b)) for b in range(0, self.real, 1024)]
                self.key_tiles = [(a, min(P, self.width - a)) for a in range(0, self.width, P)]
                self.key_fours = [self.key_tiles[a:a + 4] for a in range(0, len(self.key_tiles), 4)]
                nb, nf = len(self.blocks), len(self.key_fours)
                self.per_tile = {"big": 1 + HEADS * nb, "rel": HEADS * nb // 2,
                                 "turn": (2 + 4 + 1 + HEADS * nf + 1) // 2, "pt": (4 + HEADS * nf) // 2}
                self.at_start = {r: sum(Group(e).per_tile[r] * TPG for e in range(g)) for r in self.per_tile}

            def use(self, ring, n):
                return n % 2, self.i * self.per_tile[ring] + (self.at_start[ring] + n // 2)

        groups = [Group(g) for g in range(NG)]
        MISC_IDX, MISC_OA, MISC_META, MISC_OB = 0, 1, 2, 3

        def of_parity(tile, n):
            return tile[:, :, :].rearrange("p (j e) q -> p j e q", e=2)[:, :, n, :]

        def for_tiles(eng, body):
            for grp in groups:
                with eng.Fori(0, TPG) as i:
                    grp.i = i
                    body(grp, i + TPG * grp.g)

        with nc.Block() as block:
            @block.sync
            def _(sp):
                s.begin(sp)
                sp.dma_start(wuk[:, :, :], w_uk[0].rearrange("h r d -> r h d")).then_inc(w_loaded, 16)
                sp.dma_start(wuv[:, :, :], w_uv[0].rearrange("h r d -> r h d")).then_inc(w_loaded, 16)
                sp.dma_start(sink_u[:, :], sinks.to_broadcast([P, HEADS])).then_inc(w_loaded, 16)
                for half in range(2):
                    sp.dma_start(k_win[half * DH:half * DH + DH, :, 0:META],
                                 proj[R_KA:R_KA + P, PAD:PAD + META].rearrange("(k d) c -> d k c", d=DH)).then_inc(w_loaded, 16)
                sp.dma_start(v_win[0:META, 0, :], v_nat[PAD:PAD + META, :]).then_inc(w_loaded, 16)

                def load(grp, t):
                    sp.wait_ge(win_done, t + START)
                    q0 = t * P + (PAD + META)
                    w0 = t * P + META
                    cols = bass.ds(q0, P)
                    win = bass.ds(w0, WIN)
                    sp.dma_start(qi[0:DH, :, :], proj[R_QI:R_QI + 512, cols].rearrange("(h d) c -> d h c", d=DH)).then_inc(q_loaded, 16)
                    sp.dma_start(qi[DH:P, :, :], proj[R_QI:R_QI + 512, cols].rearrange("(h d) c -> d h c", d=DH)).then_inc(q_loaded, 16)
                    sp.dma_start(qa[:, :, :], proj[R_QA:R_QA + 512, cols].rearrange("(j p) c -> p j c", p=P)).then_inc(q_loaded, 16)
                    sp.dma_start(qb[:, :, :], proj[R_QB:R_QB + 512, cols].rearrange("(j p) c -> p j c", p=P)).then_inc(q_loaded, 16)
                    sp.dma_start(wi[:, :], proj[R_WI:R_WI + HEADS, cols]).then_inc(q_loaded, 16)
                    for half in range(2):
                        sp.dma_start(k_win[half * DH:half * DH + DH, :, META:WA],
                                     proj[R_KA:R_KA + P, win].rearrange("(k d) c -> d k c", d=DH)).then_inc(q_loaded, 16)
                    sp.dma_start(v_win[META:WH, 0, :], v_nat[bass.ds(w0, WH - META), :]).then_inc(q_loaded, 16)
                    sp.dma_start(v_win[:, 1, :], v_nat[bass.ds(w0 + (WH - META), WH), :]).then_inc(q_loaded, 16)

                for_tiles(sp, load)
            q_dmas = 9

            @block.gpsimd
            def _(pool):
                make_identity(nc, pool, ident, id_ready)
                pool.iota(ints[:, :], pattern=[[-1, L]], base=META, channel_multiplier=1).then_inc(iota_ready, 1)
                pool.memset(minus_one[:, :], -1.0)
                for h in range(HEADS):
                    pool.memset(slope[:, h:h + 1], 2.0 ** -(h + 1))
                    pool.memset(neg_slope[:, h:h + 1], -2.0 ** -(h + 1))
                    pool.memset(inv_slope[:, h:h + 1], 2.0 ** (h + 1))
                pool.wait_ge(iota_used, 1 + START)
                for half in range(2):
                    pool.drain()
                    last = pool.iota(ints[half * DH:half * DH + DH, :], pattern=[[1, L]], base=-(META + CHUNK) - CHUNK * half,
                                     channel_multiplier=0)
                last.then_inc(iota_ready, 1)
                pool.drain()
                pool.wait_ge(iota_used, 2 + START)
                pool.iota(ints[:, 0:WIN], pattern=[[-1, WIN]], base=CHUNK, channel_multiplier=1).then_inc(iota_ready, 1)
                pool.drain()
                pool.wait_ge(const_ready, 1 + START)

                def body(grp, t):
                    w = grp.width
                    pool.wait_ge(q_loaded, 16 * q_dmas * (t + 1) + START)
                    scale = pair_scale[:, :].rearrange("p (j a) -> p j a", a=1).to_broadcast([P, HEADS // 2, P])
                    pool.tensor_tensor(qa_s[:, :, :], qa[:, :, :], scale, ALU.mult).then_inc(q_scaled, 1)
                    pool.tensor_tensor(qb_s[:, :, :], qb[:, :, :], scale, ALU.mult).then_inc(q_scaled, 1)
                    pool.drain()
                    pool.wait_ge(qi_hi, t + 1 + START)
                    pool.tensor_tensor(qi_2[DH:P, :, :], qi[DH:P, :, :], f32(qi_2[DH:P, :, :]), ALU.subtract).then_inc(qi_lo, 1)
                    pool.drain()
                    pool.wait_ge(dist_ready, t + 1 + START)
                    pool.tensor_tensor(dist[:, 0:w], dist[:, 0:w], hidden[:, 0:w], ALU.add).then_inc(dist_full, 1)
                    pool.wait_ge(exp_a, t + 1 + START)
                    pool.tensor_tensor(rden_a[:, :], den_a[:, :], sink_e[:, :], ALU.add)
                    pool.drain()
                    pool.tensor_tensor(rden_a[:, :], rden_a[:, :], minus_one[:, :], ALU.pow).then_inc(rden_ready, 1)
                    pool.wait_ge(p_ready, HEADS * (t + 1) + START)
                    pool.tensor_tensor(rden_b[:, :], den_b[:, :], minus_one[:, :], ALU.pow).then_inc(rden_ready, 1)

                for_tiles(pool, body)

            @block.tensor
            def _(pe):
                pe.wait_ge(id_ready, 1 + START)
                pe.wait_ge(w_loaded, 96 + START)
                for j in range(HEADS // 2):
                    last = pe.transpose(ctx[:, j * P:j * P + P], wuk[:, 2 * j:2 * j + 2, :].rearrange("r a d -> r (a d)"), ident[:, :])
                last.then_inc(wukt_ready, 1)
                pe.wait_ge(wukt_ready, 2 + START)
                pe.wait_ge(const_ready, 1 + START)

                def body(grp, t):
                    w = grp.width
                    nb, nf = len(grp.blocks), len(grp.key_fours)

                    pe.wait_ge(q_loaded, 16 * q_dmas * (t + 1) + START)
                    pe.wait_ge(q_scaled, 2 * t + 1 + START)
                    for n in range(2):
                        u, k = grp.use("big", n)
                        pe.wait_ge(big_free[u], k + START)
                        for h in range(4 * n, 4 * n + 4):
                            r = slice(h % 2 * DH, h % 2 * DH + DH)
                            at = h % 2 * 512 + h // 2 % 2 * 256
                            last = pe.matmul(big[u][:, at:at + WA], qa_s[r, h // 2, :], k_win[r, n, :],
                                             start=True, stop=True)
                        last.then_inc(big_ready[u], 1)

                    pe.wait_ge(misc_free, 4 * t + START)
                    pe.wait_ge(qi_lo, t + 1 + START)
                    for h in range(HEADS):
                        out = misc[:, h * META:h * META + META]
                        pe.matmul(out, qi_2[:, h, :], ki_hi[:, 0:META], start=True, stop=False)
                        pe.matmul(out, qi_2[:, h, :], ki_lo[:, 0:META], start=False, stop=True)
                    pe.drain()
                    pe.transpose(misc[:, 128:128 + HEADS], wi[:, :], ident[0:HEADS, 0:HEADS]).then_inc(misc_ready, 1)

                    pe.wait_ge(q_scaled, 2 * t + 2 + START)
                    for n in range(2):
                        u, k = grp.use("turn", n)
                        pe.wait_ge(turn_free[u], k + START)
                        r = slice(n * DH, n * DH + DH)
                        for j in range(HEADS // 2):
                            last = pe.matmul(turn[u][:, j * P:j * P + P], wuk_t[r, j, :], qb_s[r, j, :],
                                             start=True, stop=True)
                        last.then_inc(turn_ready[u], 1)

                    for h in range(HEADS):
                        for b, (a0, wb) in enumerate(grp.blocks):
                            u, k = grp.use("big", 2 + h * nb + b)
                            pe.wait_ge(big_free[u], k + START)
                            for a in range(0, wb, 512):
                                cols = slice(META + a0 + a, META + a0 + a + 512)
                                pe.matmul(big[u][:, a:a + 512], qi_2[:, h, :], ki_hi[:, cols], start=True, stop=False)
                                last = pe.matmul(big[u][:, a:a + 512], qi_2[:, h, :], ki_lo[:, cols], start=False, stop=True)
                            last.then_inc(big_ready[u], 1)

                    def turn_a(n):
                        u, k = grp.use("turn", 2 + n)
                        pe.wait_ge(turn_free[u], k + START)
                        for m in range(4):
                            h, b = 2 * n + m // 2, m % 2
                            last = pe.transpose(turn[u][0:WH, m * P:m * P + P], u_a[:, h, b * WH:b * WH + WH], ident[:, :])
                        last.then_inc(turn_ready[u], 1)

                    pe.wait_ge(exp_a, t + 1 + START)
                    turn_a(0)
                    pe.wait_ge(misc_free, 4 * t + MISC_OA + START)
                    for n in range(4):
                        if n < 3:
                            turn_a(n + 1)
                        u, k = grp.use("pt", n)
                        pe.wait_ge(pt_ready[u], k + 1 + START)
                        for m in range(4):
                            h, b = 2 * n + m // 2, m % 2
                            kv = h // 4
                            last = pe.matmul(misc[:, h * DH:h * DH + DH], p_t[u][0:WH, m, :], v_win[:, b, kv * DH:kv * DH + DH],
                                             start=(b == 0), stop=(b == 1))
                        last.then_inc(pt_free[u], 1)
                    pe.drain()
                    pe.sem_inc(misc_ready, 1)
                    pe.sem_inc(win_done, 1)

                    def turn_output(branch, n):
                        u, k = grp.use("turn", n)
                        pe.wait_ge(o_ready, 2 * t + 1 + branch + START)
                        pe.wait_ge(turn_free[u], k + START)
                        for j in range(4):
                            last = pe.transpose(turn[u][:, j * P:j * P + P], o_nat[branch][:, j * P:j * P + P], ident[:, :])
                        last.then_inc(turn_ready[u], 1)

                    turn_output(0, 6)

                    pe.wait_ge(misc_free, 4 * t + MISC_META + START)
                    pe.wait_ge(ql_lo_ready, 2 * t + 2 + START)
                    for h in range(HEADS):
                        last = matmul3(pe, misc[:, h * META:h * META + META], ql_hi[:, h, :], ql_lo[:, h, :], c_hi[:, 0:META],
                                       c_lo[:, 0:META], True, True)
                    last.then_inc(misc_ready, 1)

                    def logits(h):
                        for b, (a0, wb) in enumerate(grp.blocks):
                            u, k = grp.use("big", 2 + (HEADS + h) * nb + b)
                            pe.wait_ge(big_free[u], k + START)
                            for a in range(0, wb, 512):
                                cols = slice(META + a0 + a, META + a0 + a + 512)
                                last = matmul3(pe, big[u][:, a:a + 512], ql_hi[:, h, :], ql_lo[:, h, :], c_hi[:, cols], c_lo[:, cols], True, True)
                            last.then_inc(big_ready[u], 1)

                    def turn_b(h, f):
                        u, k = grp.use("turn", 7 + h * nf + f)
                        pe.wait_ge(turn_free[u], k + START)
                        for m, (a, n) in enumerate(grp.key_fours[f]):
                            last = pe.transpose(turn[u][0:n, m * P:m * P + P], u_b[h % 2][:, a:a + n], ident[:, :])
                        last.then_inc(turn_ready[u], 1)

                    def weigh(h):
                        pe.wait_ge(p_ready, HEADS * t + h + 1 + START)
                        turn_b(h, 0)
                        pe.wait_ge(ctx_free, HEADS * t + h + START)
                        for f in range(nf):
                            if f + 1 < nf:
                                turn_b(h, f + 1)
                                if f + 2 == nf:
                                    pe.drain()
                                    pe.sem_inc(u_free[h % 2], 1)
                            u, k = grp.use("pt", 4 + h * nf + f)
                            pe.wait_ge(pt_ready[u], k + 1 + START)
                            for m, (a, n) in enumerate(grp.key_fours[f]):
                                last = pe.matmul(ctx[:, 0:P], c_nat[0:n, a:a + P], p_t[u][0:n, m, :],
                                                 start=(a == 0), stop=(a + n == w))
                            last.then_inc(pt_free[u], 1)
                        pe.drain()
                        pe.sem_inc(ctx_ready, 1)

                    logits(0)
                    for h in range(HEADS):
                        if h + 1 < HEADS:
                            logits(h + 1)
                        weigh(h)
                    pe.wait_ge(misc_free, 4 * t + MISC_OB + START)
                    pe.wait_ge(ctx_free, HEADS * (t + 1) + START)
                    for h in range(HEADS):
                        last = pe.matmul(misc[:, h * DH:h * DH + DH], ctx_t[:, h, :], wuv[:, h, :], start=True, stop=True)
                    last.then_inc(misc_ready, 1)
                    turn_output(1, 7 + HEADS * nf)

                for_tiles(pe, body)

            @block.scalar
            def _(act):
                act.wait_ge(wukt_ready, 1 + START)
                act.activation(wuk_t[:, :, :], ctx[:, :].rearrange("p (j r) -> p j r", j=4), ACT.Copy).then_inc(wukt_ready, 1)
                act.wait_ge(iota_ready, 3 + START)
                act.activation(base_a[:, META:WA], ints[:, 0:WIN], ACT.Abs).then_inc(iota_used, 1)
                act.wait_ge(const_ready, 1 + START)

                def body(grp, t):
                    w = grp.width
                    nb, nf = len(grp.blocks), len(grp.key_fours)
                    act.wait_ge(q_loaded, 16 * q_dmas * (t + 1) + START)
                    act.activation(qi_2[:, :, :], qi[:, :, :], ACT.Copy).then_inc(qi_hi, 1)
                    act.wait_ge(t_ready, t + 1 + START)
                    act.activation(dist[:, 0:w], query_key[:, 0:w], ACT.Abs, bias=t_col[:, :]).then_inc(dist_ready, 1)
                    act.wait_ge(misc_ready, 4 * t + 1 + START)
                    act.activation(w_idx[:, :], misc[:, 128:128 + HEADS], ACT.Copy, scale=HEADS ** -0.5 * DH ** -0.5)
                    act.activation(rel_meta[:, :, :], misc[:, 0:128].rearrange("p (h m) -> p h m", h=HEADS), ACT.Relu)
                    act.drain()
                    act.sem_inc(relm_ready, 1)
                    act.sem_inc(misc_free, 1)
                    for n in range(2):
                        u, k = grp.use("turn", n)
                        act.wait_ge(turn_ready[u], k + 1 + START)
                        act.activation(of_parity(ql_hi, n), turn[u][:, :].rearrange("p (j q) -> p j q", j=4), ACT.Copy).then_inc(ql_hi_ready, 1)
                    for h in range(HEADS):
                        for b, (a0, wb) in enumerate(grp.blocks):
                            u, k = grp.use("big", 2 + h * nb + b)
                            v, kv = grp.use("rel", h * nb + b)
                            act.wait_ge(big_ready[u], k + 1 + START)
                            act.wait_ge(rel_free[v], kv + START)
                            act.activation(rel[v][:, 0:wb], big[u][:, 0:wb], ACT.Relu)
                            act.drain()
                            act.sem_inc(rel_ready[v], 1)
                            act.sem_inc(big_free[u], 1)
                    act.wait_ge(stats_a, t + 1 + START)
                    for h in range(HEADS):
                        act.activation(u_a[:, h, :], u_a[:, h, :], ACT.Exp, bias=bias_a[:, h:h + 1], scale=2.0 ** -(h + 1),
                                       accum_out=den_a[:, h:h + 1])
                    act.activation(sink_e[:, :], sink_e[:, :], ACT.Exp).then_inc(exp_a, 1)

                    def evacuate(n, m, rows, count):
                        u, k = grp.use("turn", n)
                        v, kv = grp.use("pt", m)
                        act.wait_ge(turn_ready[u], k + 1 + START)
                        act.wait_ge(pt_free[v], kv + START)
                        act.activation(p_t[v][0:rows, 0:count, :], turn[u][0:rows, 0:count * P].rearrange("p (m q) -> p m q", m=count), ACT.Copy)
                        act.drain()
                        act.sem_inc(pt_ready[v], 1)
                        act.sem_inc(turn_free[u], 1)

                    def output(branch, use_misc, n):
                        act.wait_ge(rden_ready, 2 * t + 1 + branch + START)
                        act.wait_ge(misc_ready, 4 * t + use_misc + 1 + START)
                        rden = rden_a if branch == 0 else rden_b
                        for h in range(HEADS):
                            act.activation(o_nat[branch][:, h * DH:h * DH + DH], misc[:, h * DH:h * DH + DH], ACT.Copy, scale=rden[:, h:h + 1])
                        act.drain()
                        act.sem_inc(o_ready, 1)
                        act.sem_inc(misc_free, 1)
                        u, k = grp.use("turn", n)
                        act.wait_ge(turn_ready[u], k + 1 + START)
                        act.wait_ge(attn_stored, 32 * t + START)
                        act.activation(o_t[branch][:, :, :], turn[u][:, :].rearrange("p (j q) -> p j q", j=4), ACT.Copy).then_inc(turn_free[u], 1)
                        act.drain()
                        act.dma_start(attn[branch * 512:branch * 512 + 512, bass.ds(t * P, P)].rearrange("(j p) c -> p j c", p=P),
                                      o_t[branch][:, :, :]).then_inc(attn_stored, 16)

                    for n in range(4):
                        evacuate(2 + n, n, WH, 4)
                    output(0, MISC_OA, 6)
                    for h in range(HEADS):
                        act.wait_ge(u_ready, HEADS * t + h + 1 + START)
                        act.activation(u_b[h % 2][:, 0:w], u_b[h % 2][:, 0:w], ACT.Exp, bias=bias_b[:, h:h + 1], scale=2.0 ** -(h + 1),
                                       accum_out=den_b[:, h:h + 1]).then_inc(p_ready, 1)
                        for f in range(nf):
                            four = grp.key_fours[f]
                            evacuate(7 + h * nf + f, 4 + h * nf + f, four[0][1], len(four))
                        act.wait_ge(ctx_ready, HEADS * t + h + 1 + START)
                        act.activation(ctx_t[:, h, :], ctx[:, 0:P], ACT.Copy).then_inc(ctx_free, 1)
                    output(1, MISC_OB, 7 + HEADS * nf)

                for_tiles(act, body)
                act.wait_ge(attn_stored, 32 * SEQ // P + START)

            @block.vector
            def _(dve):
                dve.wait_ge(iota_ready, 1 + START)
                dve.tensor_copy(query_key[:, :], ints[:, :]).then_inc(iota_used, 1)
                dve.wait_ge(iota_ready, 2 + START)
                dve.tensor_copy(limit[:, :], ints[:, :]).then_inc(iota_used, 1)
                dve.memset(t_col[:, :], -float(P))
                for h in range(HEADS):
                    dve.memset(pair_scale[h % 2 * DH:h % 2 * DH + DH, h // 2:h // 2 + 1], DH ** -0.5 * 2.0 ** (h + 1))
                dve.wait_ge(iota_used, 3 + START)
                dve.wait_ge(w_loaded, 96 + START)
                dve.memset(base_a[0:DH, META + 2 * CHUNK:WA], BIG)
                dve.memset(base_a[DH:P, META:META + CHUNK], BIG)
                dve.drain()
                dve.tensor_copy(dist_a[:, META:WA], base_a[:, META:WA])
                dve.tensor_tensor(sink_u[:, :], sink_u[:, :], inv_slope[:, :], ALU.mult)
                dve.drain()
                dve.sem_inc(const_ready, 1)

                def body(grp, t):
                    w = grp.width
                    nb = len(grp.blocks)
                    dve.tensor_scalar(t_col[:, :], t_col[:, :], float(P), None, ALU.add)
                    dve.drain()
                    dve.tensor_scalar(hidden[:, 0:w], limit[:, 0:w], t_col[:, :], BIG, ALU.is_ge, ALU.mult)
                    dve.tensor_scalar(first_col[:, :], t_col[:, :], 1.0, BIG, ALU.is_lt, ALU.mult)
                    dve.tensor_scalar(dist_a[:, 0:META], query_key[:, 0:META], t_col[:, :], None, ALU.add)
                    dve.drain()
                    dve.tensor_scalar(dist_a[:, META:META + CHUNK], base_a[:, META:META + CHUNK], first_col[:, :], None, ALU.max)
                    dve.drain()
                    dve.sem_inc(t_ready, 1)
                    for n in range(2):
                        u, k = grp.use("big", n)
                        dve.wait_ge(big_ready[u], k + 1 + START)
                        dve.tensor_tensor(u_a[:, 4 * n:4 * n + 4, :].rearrange("p (j e) c -> p e j c", e=2),
                                          big[u][:, :].rearrange("p (e j c) -> p e j c", e=2, j=2)[:, :, :, 0:WA],
                                          dist_a[:, :].rearrange("p (a b c) -> p a b c", a=1, b=1).to_broadcast([P, 2, 2, WA]),
                                          ALU.subtract).then_inc(big_free[u], 1)
                    dve.drain()
                    dve.tensor_reduce(max_a[:, :], u_a[:, :, :], AX, ALU.max)
                    dve.drain()
                    dve.tensor_tensor(max_a[:, :], max_a[:, :], sink_u[:, :], ALU.max)
                    dve.drain()
                    dve.tensor_tensor(bias_a[:, :], max_a[:, :], neg_slope[:, :], ALU.mult)
                    dve.tensor_tensor(sink_e[:, :], sink_u[:, :], max_a[:, :], ALU.subtract)
                    dve.drain()
                    dve.tensor_tensor(sink_e[:, :], sink_e[:, :], slope[:, :], ALU.mult).then_inc(stats_a, 1)
                    for n in range(2):
                        u, k = grp.use("turn", n)
                        dve.wait_ge(ql_hi_ready, 2 * t + n + 1 + START)
                        dve.tensor_tensor(of_parity(ql_lo, n), turn[u][:, :].rearrange("p (j q) -> p j q", j=4),
                                          f32(of_parity(ql_hi, n)), ALU.subtract)
                        dve.drain()
                        dve.sem_inc(turn_free[u], 1)
                        dve.sem_inc(ql_lo_ready, 1)

                    for h in range(HEADS):
                        def add(dst, src, prev, op, free=None):
                            ins = dve.scalar_tensor_tensor(out=dst, in0=src, scalar=w_idx[:, h:h + 1], in1=prev, op0=ALU.mult, op1=op)
                            if free is not None:
                                ins.then_inc(free, 1)
                        op = ALU.add if h else ALU.subtract
                        prev = score if h else hidden
                        dve.drain()
                        if h == 0:
                            dve.wait_ge(relm_ready, t + 1 + START)
                        add(score[:, 0:META], rel_meta[:, h, :], prev[:, 0:META], op)
                        for b, (a0, wb) in enumerate(grp.blocks):
                            v, kv = grp.use("rel", h * nb + b)
                            dve.wait_ge(rel_ready[v], kv + 1 + START)
                            cols = slice(META + a0, META + a0 + wb)
                            add(score[:, cols], rel[v][:, 0:wb], prev[:, cols], op, rel_free[v])
                    dve.drain()

                    with dve.Fori(0, TOPK // 8 // 2) as _:
                        for _ in range(2):
                            dve.max(best[:, :], score[:, 0:w])
                            dve.drain()
                            dve.match_replace(score[:, 0:w], best[:, :], score[:, 0:w], MARK)
                            dve.drain()
                    dve.tensor_scalar(score[:, 0:w], score[:, 0:w], MARK / 2, BIG, ALU.is_gt, ALU.mult)
                    dve.drain()
                    dve.wait_ge(dist_full, t + 1 + START)
                    dve.tensor_tensor(dist[:, 0:w], dist[:, 0:w], score[:, 0:w], ALU.max)
                    dve.drain()

                    dve.wait_ge(misc_ready, 4 * t + MISC_META + 1 + START)
                    dve.tensor_tensor(u_meta[:, :, :], misc[:, 0:128].rearrange("p (h m) -> p h m", h=HEADS),
                                      dist[:, 0:META].rearrange("p (a m) -> p a m", a=1).to_broadcast([P, HEADS, META]), ALU.subtract).then_inc(misc_free, 1)
                    dve.drain()
                    for h in range(HEADS):
                        dve.wait_ge(u_free[h % 2], HEADS // 2 * t + h // 2 + START)
                        dve.tensor_scalar(u_b[h % 2][:, 0:META], u_meta[:, h, :], 1.0, None, ALU.mult, ALU.max, accum_out=max_b[:, h, 0:1])
                        for b, (a0, wb) in enumerate(grp.blocks):
                            u, k = grp.use("big", 2 + (HEADS + h) * nb + b)
                            dve.wait_ge(big_ready[u], k + 1 + START)
                            dve.sem_inc(logits_seen, 1)
                            cols = slice(META + a0, META + a0 + wb)
                            dve.tensor_tensor_reduce(u_b[h % 2][:, cols], big[u][:, 0:wb], dist[:, cols], 1.0, MARK,
                                                     ALU.subtract, ALU.max, max_b[:, h, b + 1:b + 2]).then_inc(big_free[u], 1)
                        dve.drain()
                        dve.tensor_reduce(max_1[:, h:h + 1], max_b[:, h, 0:nb + 1], AX, ALU.max)
                        dve.drain()
                        dve.tensor_scalar(bias_b[:, h:h + 1], max_1[:, h:h + 1], -2.0 ** -(h + 1), None, ALU.mult).then_inc(u_ready, 1)

                for_tiles(dve, body)


def mix_and_ffn(nc, proj, attn, h0, w_o_a, w_o_b, w_out, ln1_g, ln1_b, w_gate, w_up, w_down, ln2_g, ln2_b, out):
    with Scope(nc, "ff") as s:
        ident, half = s.sb("ident", [P, P]), s.sb("half", [P, 1])
        ln = [s.sb(f"ln{n}", [P, D]) for n in range(4)]
        raw = [s.sb(f"raw{u}", [P, D]) for u in range(2)]
        w_hi, w_lo = [s.sb(f"w_hi{u}", [P, D], F32R) for u in range(2)], [s.sb(f"w_lo{u}", [P, D], F32R) for u in range(2)]
        resid = s.sb("resid", [P, TPG, D])
        h1_hi, h1_lo = s.sb("h1_hi", [P, KT, GROUP], F32R), s.sb("h1_lo", [P, KT, GROUP], F32R)
        f_hi, f_lo = s.sb("f_hi", [P, FT, GROUP], F32R), s.sb("f_lo", [P, FT, GROUP], F32R)
        gates = [s.sb(f"gates{u}", [P, 2, GROUP]) for u in range(2)]
        part_a, part_b, mixed = s.sb("part_a", [P, GROUP]), s.sb("part_b", [P, GROUP]), s.sb("mixed", [P, GROUP])
        silu = s.sb("silu", [P, GROUP])
        feature = s.sb("feature", [P, GROUP])
        stats, mean_var, var_eps, rstd = s.sb("stats", [P, 2, 6]), s.sb("mv", [P, 2]), s.sb("ve", [P, 1]), s.sb("rstd", [P, 1])
        bank = s.ps("bank", [P, 8, GROUP])

        const_ready, ln_loaded = s.sem("const_ready"), s.sem("ln_loaded")
        w_loaded, hi_ready, lo_ready, w_used = s.sems("w_loaded"), s.sems("hi_ready"), s.sems("lo_ready"), s.sems("w_used")
        att_loaded, att_hi, att_lo, h0_loaded = s.sem("att_loaded"), s.sem("att_hi"), s.sem("att_lo"), s.sem("h0_loaded")
        gates_loaded, gates_used = s.sems("gates_loaded"), s.sems("gates_used")
        mix_ready, mix_hi, mix_lo = s.sem("mix_ready"), s.sem("mix_hi"), s.sem("mix_lo")
        acc_free = s.sem("acc_free")
        var_ready, rstd_ready = s.sem("var_ready"), s.sem("rstd_ready")
        h1_ready, h1_turned, h1_hi_ready, h1_lo_ready = s.sem("h1_ready"), s.sem("h1_turned"), s.sem("h1_hi_ready"), s.sem("h1_lo_ready")
        silu_ready, feat_ready, feat_hi, feat_lo = s.sem("silu_ready"), s.sem("feat_ready"), s.sem("feat_hi"), s.sem("feat_lo")
        h2_ready, out_stored = s.sem("h2_ready"), s.sem("out_stored")

        Y, M, F, Z = 0, 4, 8, 8 + FT
        PAIRS = Z + FT // 2

        with nc.Block() as block:
            @block.sync
            def _(sp):
                s.begin(sp)
                for n, v in enumerate((ln1_g, ln1_b, ln2_g, ln2_b)):
                    sp.dma_start(ln[n][:, :], v.to_broadcast([P, D])).then_inc(ln_loaded, 16)
                cols = lambda w, c: w.rearrange("(k p) c -> p k c", p=P)[:, :, bass.ds(c * P, P)]
                rows = lambda w, c: w[bass.ds(c * P, P), :]
                as_k = lambda t: t[:, :].rearrange("p (k c) -> p k c", c=P)
                with sp.Fori(0, NG) as g:
                    sp.wait_ge(out_stored, 16 * TPG * g + START)
                    sp.dma_start(resid[:, :, :].rearrange("p a (b c) -> p (a b) c", c=GROUP),
                                 attn.rearrange("(k p) c -> p k c", p=P)[:, :, bass.ds(g * GROUP, GROUP)]).then_inc(att_loaded, 16)

                    def chunk(u, k, parts):
                        sp.wait_ge(lo_ready[u], g * PAIRS + k + START)
                        for dst, src in parts:
                            sp.dma_start(dst, src).then_inc(w_loaded[u], 16)

                    with sp.Fori(0, 4) as i:
                        for u in range(2):
                            c = 2 * i + u
                            chunk(u, Y + i, [(as_k(raw[u])[:, 0:4, :], cols(w_o_a, c)), (as_k(raw[u])[:, 4:8, :], cols(w_o_b, c))])
                            sp.wait_ge(gates_used[u], 4 * g + i + START)
                            for b in range(2):
                                sp.dma_start(gates[u][:, b, :], proj[bass.ds(c * P + R_GATE + b * D, P), bass.ds(g * GROUP + PAD + META, GROUP)]).then_inc(gates_loaded[u], 16)
                    sp.wait_ge(att_lo, g + 1 + START)
                    sp.dma_start(resid[:, :, :], h0[bass.ds(g * GROUP + META, GROUP), :].rearrange("(a p) d -> p a d", p=P)).then_inc(h0_loaded, 16)
                    with sp.Fori(0, 4) as i:
                        for u in range(2):
                            chunk(u, M + i, [(raw[u][:, :], rows(w_out, 2 * i + u))])
                    with sp.Fori(0, FT) as i:
                        chunk(0, F + i, [(as_k(raw[0]), cols(w_gate, i))])
                        chunk(1, F + i, [(as_k(raw[1]), cols(w_up, i))])
                    with sp.Fori(0, FT // 2) as i:
                        for u in range(2):
                            chunk(u, Z + i, [(raw[u][:, :], rows(w_down, 2 * i + u))])

            @block.gpsimd
            def _(pool):
                pool.memset(half[:, :], -0.5)
                make_identity(nc, pool, ident, const_ready)
                pool.drain()
                with pool.Fori(0, NG) as g:
                    def low_part(u, k):
                        pool.wait_ge(hi_ready[u], g * PAIRS + k + 1 + START)
                        pool.tensor_tensor(w_lo[u][:, :], raw[u][:, :], f32(w_hi[u][:, :]), ALU.subtract).then_inc(lo_ready[u], 1)

                    def inverse_roots(n):
                        with pool.Fori(0, TPG) as a:
                            pool.wait_ge(var_ready, 2 * TPG * g + n * TPG + a + 1 + START)
                            pool.tensor_tensor(rstd[:, :], var_eps[:, :], half[:, :], ALU.pow).then_inc(rstd_ready, 1)

                    pool.wait_ge(att_hi, g + 1 + START)
                    pool.tensor_tensor(f_lo[:, 0:8, :], resid[:, :, :].rearrange("p a (b c) -> p (a b) c", c=GROUP), f32(f_hi[:, 0:8, :]),
                                       ALU.subtract).then_inc(att_lo, 1)
                    with pool.Fori(0, F) as i:
                        for u in range(2):
                            low_part(u, i)
                    inverse_roots(0)
                    with pool.Fori(F, PAIRS) as i:
                        for u in range(2):
                            low_part(u, i)
                    inverse_roots(1)

            @block.scalar
            def _(act):
                with act.Fori(0, NG) as g:
                    def high_part(u, k, double=False):
                        act.wait_ge(w_loaded[u], (16 * (PAIRS + 4) * g + (32 * (k + 1) if double else 16 * (k + 1) + 64)) + START)
                        act.wait_ge(w_used[u], g * PAIRS + k + START)
                        act.activation(w_hi[u][:, :], raw[u][:, :], ACT.Copy).then_inc(hi_ready[u], 1)

                    act.wait_ge(att_loaded, 16 * (g + 1) + START)
                    act.wait_ge(w_used[1], g * PAIRS + START)
                    act.activation(f_hi[:, 0:8, :], resid[:, :, :].rearrange("p a (b c) -> p (a b) c", c=GROUP), ACT.Copy).then_inc(att_hi, 1)
                    with act.Fori(0, 4) as i:
                        for u in range(2):
                            high_part(u, Y + i, True)
                            act.wait_ge(mix_ready, 8 * g + 2 * i + u + 1 + START)
                            act.activation(f_hi[:, bass.ds(8 + 2 * i + u, 1), :], mixed[:, :].rearrange("p (a c) -> p a c", a=1), ACT.Copy).then_inc(mix_hi, 1)
                    with act.Fori(0, 4) as i:
                        for u in range(2):
                            high_part(u, M + i)
                    with act.Fori(0, TPG) as a:
                        for b in range(2):
                            act.wait_ge(h1_turned, 2 * TPG * g + 2 * a + b + 1 + START)
                            act.activation(h1_hi[:, 4 * b:4 * b + 4, bass.ds(a * P, P)], bank[:, b, :].rearrange("p (k c) -> p k c", c=P),
                                           ACT.Copy).then_inc(h1_hi_ready, 1)

                    def gate(n, i):
                        act.wait_ge(w_used[0], g * PAIRS + F + i + 1 + START)
                        act.wait_ge(feat_ready, FT * g + i + START)
                        act.activation(silu[:, :], bank[:, 4 * n, :], ACT.Silu).then_inc(silu_ready, 1)
                        act.wait_ge(feat_ready, FT * g + i + 1 + START)
                        act.activation(f_hi[:, bass.ds(i, 1), :], feature[:, :].rearrange("p (a c) -> p a c", a=1), ACT.Copy).then_inc(feat_hi, 1)

                    high_part(0, F)
                    high_part(1, F)
                    with act.Fori(0, FT // 2 - 1) as i:
                        for n in range(2):
                            high_part(0, F + 2 * i + n + 1)
                            gate(n, 2 * i + n)
                            high_part(1, F + 2 * i + n + 1)
                    high_part(0, F + FT - 1)
                    gate(0, FT - 2)
                    high_part(1, F + FT - 1)
                    high_part(0, Z)
                    gate(1, FT - 1)
                    high_part(1, Z)
                    with act.Fori(1, FT // 2) as i:
                        for u in range(2):
                            high_part(u, Z + i)
                    with act.Fori(0, TPG) as a:
                        act.wait_ge(h2_ready, TPG * g + a + 1 + START)
                        act.dma_start(out[0, bass.ds(g * GROUP + a * P, P), :], resid[:, bass.ds(a, 1), :].rearrange("p a d -> p (a d)")).then_inc(out_stored, 16)
                act.wait_ge(out_stored, 16 * TPG * NG + START)

            @block.vector
            def _(dve):
                dve.wait_ge(ln_loaded, 64 + START)

                with dve.Fori(0, NG) as g:
                    def one(ap):
                        return ap.rearrange("p a c -> p (a c)")

                    with dve.Fori(0, 4) as i:
                        for u in range(2):
                            n = 2 * i + u
                            dve.wait_ge(gates_loaded[u], 32 * (4 * g + i + 1) + START)
                            dve.wait_ge(w_used[u], g * PAIRS + Y + i + 1 + START)
                            dve.tensor_tensor(part_a[:, :], bank[:, 2 * u, :], gates[u][:, 0, :], ALU.mult)
                            dve.tensor_tensor(part_b[:, :], bank[:, 2 * u + 1, :], gates[u][:, 1, :], ALU.mult)
                            dve.drain()
                            dve.sem_inc(gates_used[u], 1)
                            dve.sem_inc(acc_free, 1)
                            dve.tensor_tensor(mixed[:, :], part_a[:, :], part_b[:, :], ALU.add).then_inc(mix_ready, 1)
                            dve.wait_ge(mix_hi, 8 * g + n + 1 + START)
                            dve.tensor_tensor(one(f_lo[:, bass.ds(8 + n, 1), :]), mixed[:, :], f32(one(f_hi[:, bass.ds(8 + n, 1), :])), ALU.subtract).then_inc(mix_lo, 1)
                            dve.drain()

                    def layer_norm(stage, n, done):
                        for a in range(TPG):
                            x = resid[:, a, :]
                            for b in range(2):
                                dve.scalar_tensor_tensor(out=resid[:, a, b * 512:b * 512 + 512], in0=resid[:, a, b * 512:b * 512 + 512],
                                                         scalar=ALPHA, in1=bank[:, 2 * a + b, :], op0=ALU.mult, op1=ALU.add)
                            dve.drain()
                            dve.sem_inc(acc_free, 1)
                            for b in range(2):
                                dve.bn_stats(stats[:, b, :], resid[:, a, b * 512:b * 512 + 512])
                            dve.drain()
                            dve.bn_aggr(mean_var[:, :], stats[:, :, :])
                            dve.drain()
                            dve.tensor_scalar(var_eps[:, :], mean_var[:, 1:2], 1e-5, None, ALU.add).then_inc(var_ready, 1)
                            dve.wait_ge(rstd_ready, 2 * TPG * g + TPG * stage + a + 1 + START)
                            dve.tensor_scalar(x, x, mean_var[:, 0:1], rstd[:, :], ALU.subtract, ALU.mult)
                            dve.drain()
                            dve.tensor_tensor(x, x, ln[n][:, :], ALU.mult)
                            dve.drain()
                            dve.tensor_tensor(x, x, ln[n + 1][:, :], ALU.add).then_inc(done, 1)

                    dve.wait_ge(h0_loaded, 16 * (g + 1) + START)
                    dve.wait_ge(w_used[1], g * PAIRS + F + START)
                    layer_norm(0, 0, h1_ready)
                    with dve.Fori(0, TPG) as a:
                        for b in range(2):
                            dve.wait_ge(h1_hi_ready, 2 * TPG * g + 2 * a + b + 1 + START)
                            dve.tensor_tensor(h1_lo[:, 4 * b:4 * b + 4, bass.ds(a * P, P)], bank[:, b, :].rearrange("p (k c) -> p k c", c=P),
                                              f32(h1_hi[:, 4 * b:4 * b + 4, bass.ds(a * P, P)]), ALU.subtract).then_inc(h1_lo_ready, 1)
                    with dve.Fori(0, FT // 2) as i:
                        for n in range(2):
                            t = 2 * i + n
                            dve.wait_ge(silu_ready, FT * g + t + 1 + START)
                            dve.wait_ge(w_used[1], g * PAIRS + F + t + 1 + START)
                            dve.tensor_tensor(feature[:, :], silu[:, :], bank[:, 4 * n + 1, :], ALU.mult).then_inc(feat_ready, 1)
                            dve.wait_ge(feat_hi, FT * g + t + 1 + START)
                            dve.tensor_tensor(one(f_lo[:, bass.ds(t, 1), :]), feature[:, :], f32(one(f_hi[:, bass.ds(t, 1), :])), ALU.subtract).then_inc(feat_lo, 1)
                            dve.drain()
                    dve.wait_ge(w_used[1], g * PAIRS + PAIRS + START)
                    layer_norm(1, 2, h2_ready)

            @block.tensor
            def _(pe):
                pe.wait_ge(const_ready, 1 + START)
                ACC = 8 + 2 * TPG
                with pe.Fori(0, NG) as g:
                    def weights(u, k):
                        pe.wait_ge(hi_ready[u], g * PAIRS + k + 1 + START)
                        pe.wait_ge(lo_ready[u], g * PAIRS + k + 1 + START)

                    def turned(dst, u, first, count, hi, lo, hi_first):
                        for c in range(count):
                            w = slice((first + c) * P, (first + c) * P + P)
                            last = matmul3(pe, dst, w_hi[u][:, w], w_lo[u][:, w], hi[:, hi_first + c, :], lo[:, hi_first + c, :],
                                           c == 0, c == count - 1)
                        return last

                    with pe.Fori(0, 4) as i:
                        for u in range(2):
                            pe.wait_ge(att_lo, g + 1 + START)
                            pe.wait_ge(acc_free, ACC * g + START)
                            weights(u, Y + i)
                            pe.wait_ge(mix_ready, 8 * g + 2 * i + START)
                            turned(bank[:, 2 * u, :], u, 0, 4, f_hi, f_lo, 0)
                            turned(bank[:, 2 * u + 1, :], u, 4, 4, f_hi, f_lo, 4).then_inc(w_used[u], 1)

                    def natural(u, first, last_one, hi, lo, at):
                        for a in range(TPG):
                            for b in range(2):
                                q, c = slice(a * P, a * P + P), slice(b * 512, b * 512 + 512)
                                last = matmul3(pe, bank[:, 2 * a + b, :], hi[:, at, q], lo[:, at, q], w_hi[u][:, c], w_lo[u][:, c],
                                               first, last_one)
                        last.then_inc(w_used[u], 1)

                    pe.wait_ge(acc_free, ACC * g + 8 + START)
                    for c in range(8):
                        weights(c % 2, M + c // 2)
                        pe.wait_ge(mix_lo, 8 * g + 8 + START)
                        natural(c % 2, c == 0, c == 7, f_hi, f_lo, 8 + c)
                    pe.wait_ge(acc_free, ACC * g + 8 + TPG + START)
                    for a in range(TPG):
                        pe.wait_ge(h1_ready, TPG * g + a + 1 + START)
                        for b in range(2):
                            if a:
                                pe.wait_ge(h1_lo_ready, 2 * TPG * g + 2 * (a - 1) + b + 1 + START)
                            for c in range(4):
                                last = pe.transpose(bank[:, b, c * P:c * P + P], resid[:, a, (4 * b + c) * P:(4 * b + c) * P + P], ident[:, :])
                            last.then_inc(h1_turned, 1)
                    with pe.Fori(0, FT // 2) as i:
                        for n in range(2):
                            pe.wait_ge(h1_lo_ready, 2 * TPG * (g + 1) + START)
                            pe.wait_ge(feat_ready, FT * g + 2 * i + START)
                            for u in range(2):
                                weights(u, F + 2 * i + n)
                                turned(bank[:, 4 * n + u, :], u, 0, 8, h1_hi, h1_lo, 0).then_inc(w_used[u], 1)
                    pe.wait_ge(feat_lo, FT * (g + 1) + START)
                    for c in range(FT):
                        weights(c % 2, Z + c // 2)
                        natural(c % 2, c == 0, c == FT - 1, f_hi, f_lo, c)


def build(nc, x, meta_tokens, ln0_g, ln0_b, w_in, b_gate, kv_norm_g, w_uk, w_uv, k_idx_g, k_idx_b, sinks, w_o_a, w_o_b,
          w_out, ln1_g, ln1_b, w_ff_gate, w_ff_up, w_ff_down, ln2_g, ln2_b, out, phases=4):
    h0 = nc.dram_tensor("h0", (L, D), F32, kind="Internal").ap()
    proj = nc.dram_tensor("proj", (4096, LP), F32, kind="Internal").ap()
    v_nat = nc.dram_tensor("v_nat", (LP, P), F32, kind="Internal").ap()
    attn = nc.dram_tensor("attn", (D, SEQ), F32, kind="Internal").ap()
    project(nc, x, meta_tokens, ln0_g, ln0_b, w_in, b_gate, h0, proj, v_nat)
    if phases > 1:
        with Scope(nc, "keys") as s:
            keys = (s.sb("c_nat", [P, 17 * P]), s.sb("c_hi", [P, L], F32R), s.sb("c_lo", [P, L], F32R),
                    s.sb("ki_hi", [P, L], F32R), s.sb("ki_lo", [P, L], F32R))
            prepare_keys(nc, proj, kv_norm_g, k_idx_g, k_idx_b, v_nat, keys)
            if phases > 2:
                attention(nc, proj, v_nat, w_uk, w_uv, sinks, attn, keys)
    if phases > 3:
        mix_and_ffn(nc, proj, attn, h0, w_o_a[0], w_o_b[0], w_out[0], ln1_g, ln1_b, w_ff_gate[0], w_ff_up[0], w_ff_down[0],
                    ln2_g, ln2_b, out)


_INS = ["x", "meta_tokens", "ln0_g", "ln0_b", "w_in", "b_gate", "kv_norm_g", "w_uk", "w_uv", "k_idx_g", "k_idx_b", "sinks",
        "w_o_a", "w_o_b", "w_out", "ln1_g", "ln1_b", "w_ff_gate", "w_ff_up", "w_ff_down", "ln2_g", "ln2_b"]


def kernel(**inputs):
    import numpy as np
    import concourse.bacc as bacc
    from concourse.bass_utils import run_bass_kernel_spmd

    nc = bacc.Bacc("TRN2", target_bir_lowering=False, num_devices=1)
    arrays, args = {}, []
    for name in _INS:
        a = np.ascontiguousarray(inputs[name])
        arrays[f"in_{name}"] = a
        args.append(nc.dram_tensor(f"in_{name}", a.shape, mybir.dt.from_np(a.dtype), kind="ExternalInput").ap())
    args.append(nc.dram_tensor("out_0", (1, SEQ, D), F32, kind="ExternalOutput").ap())
    build(nc, *args)
    r = run_bass_kernel_spmd(nc, [arrays], core_ids=[0])
    return r.results[0]["out_0"]
```

```python
from contextlib import ExitStack

import concourse.bass as bass
from concourse import mybir

ALU = mybir.AluOpType
ACT = mybir.ActivationFunctionType
AX = mybir.AxisListType.X
F32 = mybir.dt.float32
F32R = mybir.dt.float32r
I32 = mybir.dt.int32
BF16 = mybir.dt.bfloat16

P = 128
D = 1024
KT = D // P
SEQ = 2048
META = 16
L = SEQ + META
CHUNK = 64
HEADS = 8
DH = 64
TOPK = 256
DFF = 2816
FT = DFF // P
GROUP = 512
NG = SEQ // GROUP
TPG = GROUP // P
ALPHA = 2.0 ** 0.25
PAD = CHUNK
LP = L + PAD
BIG = 1e37
START = 1
MARK = -3e38
R_QA, R_KA, R_VA, R_QB, R_CB, R_QI, R_KI, R_WI, R_GATE = 0, 512, 640, 768, 1280, 1408, 1920, 1984, 2048
SPLIT_CHUNKS = 16
GATE_COL = 1992
WIN = 2 * CHUNK + CHUNK
WA = META + WIN
TINY, TOP = 2.0 ** -126, 3e38
MANTISSA = 23
ROUNDS = 1 + 8 + MANTISSA
DVE_TILES = 2
ORDER = (0, 2, 1, 3)
WH = WA // 2


def f32(ap):
    return ap.bitcast(F32)


class Scope(ExitStack):

    def __init__(self, nc, tag):
        super().__init__()
        self.nc, self.tag, self.all_sems = nc, tag, []

    def sb(self, name, shape, dt=F32):
        return self.enter_context(self.nc.sbuf_tensor(f"{self.tag}_{name}", shape, dt))

    def ps(self, name, shape):
        return self.enter_context(self.nc.psum_tensor(f"{self.tag}_{name}", shape, F32))

    def sem(self, name):
        self.all_sems.append(self.enter_context(self.nc.semaphore(f"{self.tag}_{name}")))
        return self.all_sems[-1]

    def begin(self, sp):
        for sem in self.all_sems:
            sp.sem_inc(sem, START)

    def sems(self, name, n=2):
        return [self.sem(f"{name}{i}") for i in range(n)]


def matmul3(pe, out, lhs_hi, lhs_lo, rhs_hi, rhs_lo, start, stop):
    pe.matmul(out, lhs_lo, rhs_hi, start=start, stop=False)
    pe.matmul(out, lhs_hi, rhs_hi, start=False, stop=False)
    return pe.matmul(out, lhs_hi, rhs_lo, start=False, stop=stop)


def make_identity(nc, pool, ident, ready):
    pool.memset(ident[:, :], 0.0)
    pool.drain()
    pool.affine_select(out=ident[:, :], in_=ident[:, :], compare_op=ALU.not_equal, fill=1.0, base=0,
                       pattern=[[-1, P]], channel_multiplier=1).then_inc(ready, 1)


def project(nc, x, meta_tokens, ln0_g, ln0_b, w_in, b_gate, h0, proj, v_nat):
    with Scope(nc, "pj") as s:
        h_hi, h_lo = s.sb("h_hi", [P, KT, L], F32R), s.sb("h_lo", [P, KT, L], F32R)
        ident = s.sb("ident", [P, P])
        zeros = s.sb("zeros", [P, PAD])
        half = s.sb("half", [P, 1])
        id_ready, zero_ready, zero_stored = s.sem("id_ready"), s.sem("zero_ready"), s.sem("zero_stored")
        with Scope(nc, "ln") as a:
            xt = [a.sb(f"x{u}", [P, D]) for u in range(2)]
            hb = [a.sb(f"h{u}", [P, D]) for u in range(2)]
            gain, shift = a.sb("gain", [P, D]), a.sb("shift", [P, D])
            stats = [a.sb(f"stats{u}", [P, 2, 6]) for u in range(2)]
            mean_var = [a.sb(f"mv{u}", [P, 2]) for u in range(2)]
            var_eps = [a.sb(f"ve{u}", [P, 1]) for u in range(2)]
            rstd = [a.sb(f"rstd{u}", [P, 1]) for u in range(2)]
            turned = [a.ps(f"turned{u}", [P, KT, P]) for u in range(2)]
            gb_loaded = a.sem("gb_loaded")
            x_loaded, x_free = a.sems("x_loaded"), a.sems("x_free")
            var_ready, rstd_ready = a.sem("var_ready"), a.sem("rstd_ready")
            h_ready, h_stored = a.sems("h_ready"), a.sems("h_stored")
            turned_ready, hi_ready, turned_free = a.sems("turned_ready"), a.sems("hi_ready"), a.sems("turned_free")

            def tiles(eng, step):
                step(0, 0, META, None)
                with eng.Fori(0, SEQ // P // 2) as i:
                    step(1, i, P, 2 * P * i)
                    step(0, i + 1, P, 2 * P * i + P)

            with nc.Block() as block:
                @block.sync
                def _(sp):
                    s.begin(sp)
                    a.begin(sp)
                    sp.dma_start(gain[:, :], ln0_g.rearrange("(a d) -> a d", a=1).to_broadcast([P, D])).then_inc(gb_loaded, 16)
                    sp.dma_start(shift[:, :], ln0_b.rearrange("(a d) -> a d", a=1).to_broadcast([P, D])).then_inc(gb_loaded, 16)

                    def load(u, k, n, r):
                        sp.wait_ge(x_free[u], k + START)
                        src = meta_tokens if r is None else x[0, bass.ds(r, P), :]
                        sp.dma_start(xt[u][0:n, :], src).then_inc(x_loaded[u], 16)

                    tiles(sp, load)
                    sp.wait_ge(zero_ready, 1 + START)
                    sp.dma_start(proj[R_KA:R_KA + P, 0:PAD], zeros[:, :]).then_inc(zero_stored, 16)
                    for half_cols in range(2):
                        sp.dma_start(v_nat[0:PAD, half_cols * 64:half_cols * 64 + 64], zeros[0:PAD, :]).then_inc(zero_stored, 16)
                    sp.wait_ge(zero_stored, 48 + START)

                @block.gpsimd
                def _(pool):
                    make_identity(nc, pool, ident, id_ready)
                    pool.memset(half[:, :], -0.5)
                    pool.memset(zeros[:, :], 0.0).then_inc(zero_ready, 1)
                    pool.drain()

                    def inverse_root(u, k, n, r):
                        pool.wait_ge(var_ready, 2 * k + u + 1 + START)
                        pool.tensor_tensor(rstd[u][0:n, :], var_eps[u][0:n, :], half[0:n, :], ALU.pow).then_inc(rstd_ready, 1)

                    tiles(pool, inverse_root)

                @block.vector
                def _(dve):
                    def normalise(u, k, n, r=None):
                        dve.wait_ge(x_loaded[u], 16 * (k + 1) + START)
                        for c in range(2):
                            dve.bn_stats(stats[u][0:n, c, :], xt[u][0:n, c * 512:c * 512 + 512])
                        dve.drain()
                        dve.bn_aggr(mean_var[u][0:n, :], stats[u][0:n, :, :])
                        dve.drain()
                        dve.tensor_scalar(var_eps[u][0:n, :], mean_var[u][0:n, 1:2], 1e-5, None, ALU.add).then_inc(var_ready, 1)
                        dve.wait_ge(rstd_ready, 2 * k + u + 1 + START)
                        dve.wait_ge(turned_ready[u], k + START)
                        dve.wait_ge(h_stored[u], 16 * k + START)
                        dve.tensor_scalar(hb[u][0:n, :], xt[u][0:n, :], mean_var[u][0:n, 0:1], rstd[u][0:n, :],
                                          ALU.subtract, ALU.mult).then_inc(x_free[u], 1)
                        dve.drain()
                        dve.tensor_tensor(hb[u][0:n, :], hb[u][0:n, :], gain[0:n, :], ALU.mult)
                        dve.drain()
                        dve.tensor_tensor(hb[u][0:n, :], hb[u][0:n, :], shift[0:n, :], ALU.add).then_inc(h_ready[u], 1)

                    def low_part(u, k, n, col):
                        dve.wait_ge(hi_ready[u], k + 1 + START)
                        dve.tensor_tensor(h_lo[:, :, bass.ds(col, n)], turned[u][:, :, 0:n],
                                          f32(h_hi[:, :, bass.ds(col, n)]), ALU.subtract).then_inc(turned_free[u], 1)

                    dve.wait_ge(gb_loaded, 32 + START)
                    normalise(0, 0, META)
                    normalise(1, 0, P)
                    low_part(0, 0, META, 0)
                    with dve.Fori(0, SEQ // P // 2 - 1) as i:
                        normalise(0, i + 1, P)
                        low_part(1, i, P, META + 2 * P * i)
                        normalise(1, i + 1, P)
                        low_part(0, i + 1, P, META + 2 * P * i + P)
                    last = SEQ // P // 2
                    normalise(0, last, P)
                    low_part(1, last - 1, P, L - 2 * P)
                    low_part(0, last, P, L - P)

                @block.tensor
                def _(pe):
                    pe.wait_ge(id_ready, 1 + START)

                    def turn(u, k, n, r):
                        pe.wait_ge(h_ready[u], k + 1 + START)
                        pe.wait_ge(turned_free[u], k + START)
                        for c in range(KT):
                            last = pe.transpose(turned[u][:, c, 0:n], hb[u][0:n, c * P:c * P + P], ident[0:n, 0:n])
                        last.then_inc(turned_ready[u], 1)

                    tiles(pe, turn)

                @block.scalar
                def _(act):
                    def high_part(u, k, n, r):
                        act.wait_ge(h_ready[u], k + 1 + START)
                        dst = h0[0:META, :] if r is None else h0[bass.ds(r + META, P), :]
                        act.dma_start(dst, hb[u][0:n, :]).then_inc(h_stored[u], 16)
                        act.wait_ge(turned_ready[u], k + 1 + START)
                        col = 0 if r is None else r + META
                        act.activation(h_hi[:, :, bass.ds(col, n)], turned[u][:, :, 0:n], ACT.Copy).then_inc(hi_ready[u], 1)

                    tiles(act, high_part)
                    act.wait_ge(h_stored[0], 16 * 9 + START)
                    act.wait_ge(h_stored[1], 16 * 8 + START)

        with Scope(nc, "in") as a:
            raw = [a.sb(f"raw{u}", [P, KT, P]) for u in range(2)]
            w_hi = [a.sb(f"w_hi{u}", [P, KT, P], F32R) for u in range(2)]
            w_lo = [a.sb(f"w_lo{u}", [P, KT, P], F32R) for u in range(2)]
            row = [a.sb(f"row{u}", [P, L]) for u in range(2)]
            bias = [a.sb(f"bias{u}", [P, 1]) for u in range(2)]
            acc = [a.ps(f"acc{g}", [P, GROUP]) for g in range(NG)]
            acc_meta = [a.ps(f"acc_meta{u}", [P, GROUP]) for u in range(2)]
            w_loaded, hi_ready, lo_ready, w_free = a.sems("w_loaded"), a.sems("hi_ready"), a.sems("lo_ready"), a.sems("w_free")
            acc_ready = a.sems("acc_ready", NG)
            acc_free = a.sems("acc_free", NG + 1)
            stored = a.sems("stored")
            half_plain, half_all = SPLIT_CHUNKS // 2, SPLIT_CHUNKS

            with nc.Block() as block:
                @block.sync
                def _(sp):
                    a.begin(sp)
                    def load(u, k, gates):
                        sp.wait_ge(lo_ready[u], k + START)
                        first = (2 * k + u) * P
                        if gates:
                            first = first - (R_GATE - GATE_COL)
                        sp.dma_start(raw[u][:, :, :], w_in[0].rearrange("(k p) c -> p k c", p=P)[:, :, bass.ds(first, P)]).then_inc(w_loaded[u], 16)
                        if gates:
                            sp.wait_ge(acc_free[NG], 2 * k + u - 1 + START)
                            sp.dma_start(bias[u][:, :], b_gate[0].rearrange("(a b) -> a b", b=1)[bass.ds((2 * k + u) * P - R_GATE, P), :]).then_inc(w_loaded[u], 16)

                    def store(u, k):
                        for n in range(NG + 1):
                            sp.wait_ge(acc_free[n], 2 * k + u + 1 + START)
                        sp.dma_start(proj[bass.ds((2 * k + u) * P, P), PAD:LP], row[u][:, :]).then_inc(stored[u], 16)

                    load(0, 0, False)
                    load(1, 0, False)
                    with sp.Fori(0, half_plain - 1) as k:
                        for u in range(2):
                            store(u, k)
                            load(u, k + 1, False)
                    with sp.Fori(half_plain - 1, half_all - 1) as k:
                        for u in range(2):
                            store(u, k)
                            load(u, k + 1, True)
                    for u in range(2):
                        store(u, half_all - 1)
                    for u in range(2):
                        sp.wait_ge(stored[u], 16 * half_all + START)

                def loaded(eng, u, k, gates):
                    eng.wait_ge(w_loaded[u], (32 * (k + 1) - 16 * half_plain if gates else 16 * (k + 1)) + START)

                @block.gpsimd
                def _(pool):
                    with pool.Fori(0, half_all) as k:
                        for u in range(2):
                            pool.wait_ge(hi_ready[u], k + 1 + START)
                            pool.tensor_tensor(w_lo[u][:, :, :], raw[u][:, :, :], f32(w_hi[u][:, :, :]), ALU.subtract).then_inc(lo_ready[u], 1)

                @block.scalar
                def _(act):
                    def high_part(u, k, gates):
                        loaded(act, u, k, gates)
                        act.wait_ge(w_free[u], k + START)
                        act.activation(w_hi[u][:, :, :], raw[u][:, :, :], ACT.Copy).then_inc(hi_ready[u], 1)

                    def evacuate(u, k):
                        act.wait_ge(stored[u], 16 * k + START)
                        for g in (1, 3):
                            act.wait_ge(acc_ready[g], 2 * k + u + 1 + START)
                            act.activation(row[u][:, META + g * GROUP:META + (g + 1) * GROUP], acc[g][:, :], ACT.Copy).then_inc(acc_free[g], 1)

                    def gate(u, k):
                        act.wait_ge(stored[u], 16 * k + START)
                        for g in range(NG):
                            act.wait_ge(acc_ready[g], 2 * k + u + 1 + START)
                            act.activation(row[u][:, META + g * GROUP:META + (g + 1) * GROUP], acc[g][:, :], ACT.Sigmoid,
                                           bias=bias[u][:, :]).then_inc(acc_free[g], 1)
                        act.wait_ge(w_free[u], k + 1 + START)
                        act.activation(row[u][:, 0:META], acc_meta[u][:, 0:META], ACT.Sigmoid, bias=bias[u][:, :]).then_inc(acc_free[NG], 1)

                    high_part(0, 0, False)
                    with act.Fori(0, half_plain - 1) as k:
                        high_part(1, k, False)
                        evacuate(0, k)
                        high_part(0, k + 1, False)
                        evacuate(1, k)
                    high_part(1, half_plain - 1, False)
                    evacuate(0, half_plain - 1)
                    high_part(0, half_plain, True)
                    evacuate(1, half_plain - 1)
                    with act.Fori(half_plain, half_all - 1) as k:
                        high_part(1, k, True)
                        gate(0, k)
                        high_part(0, k + 1, True)
                        gate(1, k)
                    high_part(1, half_all - 1, True)
                    gate(0, half_all - 1)
                    gate(1, half_all - 1)

                @block.vector
                def _(dve):
                    with dve.Fori(0, half_plain) as k:
                        for u in range(2):
                            dve.wait_ge(stored[u], 16 * k + START)
                            for g in (0, 2):
                                dve.wait_ge(acc_ready[g], 2 * k + u + 1 + START)
                                dve.tensor_copy(row[u][:, META + g * GROUP:META + (g + 1) * GROUP], acc[g][:, :]).then_inc(acc_free[g], 1)
                            dve.wait_ge(w_free[u], k + 1 + START)
                            dve.tensor_copy(row[u][:, 0:META], acc_meta[u][:, 0:META]).then_inc(acc_free[NG], 1)

                @block.tensor
                def _(pe):
                    with pe.Fori(0, half_all) as k:
                        for u in range(2):
                            pe.wait_ge(hi_ready[u], k + 1 + START)
                            pe.wait_ge(lo_ready[u], k + 1 + START)
                            for g in range(NG + 1):
                                pe.wait_ge(acc_free[g], 2 * k + u + START)
                                out = acc[g][:, :] if g < NG else acc_meta[u][:, 0:META]
                                c0, c1 = (META + g * GROUP, META + (g + 1) * GROUP) if g < NG else (0, META)
                                for c in range(KT):
                                    last = matmul3(pe, out, w_hi[u][:, c, :], w_lo[u][:, c, :], h_hi[:, c, c0:c1],
                                                   h_lo[:, c, c0:c1], c == 0, c == KT - 1)
                                last.then_inc(acc_ready[g] if g < NG else w_free[u], 1)


def prepare_keys(nc, proj, kv_norm_g, k_idx_g, k_idx_b, v_nat, keys):
    c_nat, c_hi, c_lo, ki_hi, ki_lo = keys
    with Scope(nc, "ky") as s:
        ident, half = s.sb("ident", [P, P]), s.sb("half", [P, 2])
        cg, kg, kb = s.sb("cg", [P, P]), s.sb("kg", [P, DH]), s.sb("kb", [P, DH])
        cin = [s.sb(f"cin{u}", [P, P]) for u in range(2)]
        kin = [s.sb(f"kin{u}", [DH, P]) for u in range(2)]
        vin = [s.sb(f"vin{u}", [P, P]) for u in range(2)]
        junk = s.sb("junk", [P, P])
        stats = [s.sb(f"stats{u}", [P, 6]) for u in range(2)]
        mean_var = [s.sb(f"mv{u}", [P, 2]) for u in range(2)]
        square = [s.sb(f"square{u}", [P, 1]) for u in range(2)]
        var_eps = [s.sb(f"ve{u}", [P, 2]) for u in range(2)]
        rstd = [s.sb(f"rstd{u}", [P, 2]) for u in range(2)]
        cn = [s.sb(f"cn{u}", [P, P]) for u in range(2)]
        kn = [s.sb(f"kn{u}", [P, 2, DH]) for u in range(2)]
        vn = [s.sb(f"vn{u}", [P, P]) for u in range(2)]
        nat = [s.ps(f"nat{u}", [P, 512]) for u in range(2)]
        nat_k = [s.ps(f"nat_k{u}", [P, 512]) for u in range(2)]
        back = [s.ps(f"back{u}", [P, 512]) for u in range(2)]
        const_ready, g_loaded = s.sem("const_ready"), s.sem("g_loaded")
        loaded, nat_ready, square_ready = s.sems("loaded"), s.sems("nat_ready"), s.sems("square_ready")
        var_ready, rstd_ready, norm_ready, copied = s.sems("var_ready"), s.sems("rstd_ready"), s.sems("norm_ready"), s.sems("copied")
        back_ready, hi_ready, lo_ready, v_stored = s.sems("back_ready"), s.sems("hi_ready"), s.sems("lo_ready"), s.sems("v_stored")

        def tiles(eng, step):
            with eng.Fori(0, L // P // 2) as i:
                for u in range(2):
                    step(u, i, P, (2 * i + u) * P)
            step(0, L // P // 2, L % P, L - L % P)

        with nc.Block() as block:
            @block.sync
            def _(sp):
                s.begin(sp)
                sp.dma_start(cg[:, :], kv_norm_g.to_broadcast([P, P])).then_inc(g_loaded, 16)
                sp.dma_start(kg[:, :], k_idx_g.to_broadcast([P, DH])).then_inc(g_loaded, 16)
                sp.dma_start(kb[:, :], k_idx_b.to_broadcast([P, DH])).then_inc(g_loaded, 16)

                def load(u, k, n, j):
                    sp.wait_ge(nat_ready[u], k + START)
                    for dst, row, rows in ((cin, R_CB, P), (kin, R_KI, DH), (vin, R_VA, P)):
                        sp.dma_start(dst[u][0:rows, 0:n], proj[row:row + rows, bass.ds(j + PAD, n)]).then_inc(loaded[u], 16)

                tiles(sp, load)

            @block.gpsimd
            def _(pool):
                pool.memset(half[:, :], -0.5)
                make_identity(nc, pool, ident, const_ready)
                pool.drain()

                def step(u, k, n, j):
                    pool.wait_ge(var_ready[u], k + 1 + START)
                    pool.tensor_tensor(rstd[u][0:n, :], var_eps[u][0:n, :], half[0:n, :], ALU.pow).then_inc(rstd_ready[u], 1)
                    pool.wait_ge(norm_ready[u], k + 1 + START)
                    pool.tensor_copy(c_nat[0:n, bass.ds(j, P)], cn[u][0:n, :]).then_inc(copied[u], 1)

                tiles(pool, step)

            @block.tensor
            def _(pe):
                pe.wait_ge(const_ready, 1 + START)

                def step(u, k, n, j):
                    pe.wait_ge(loaded[u], 48 * (k + 1) + START)
                    pe.wait_ge(norm_ready[u], k + START)
                    pe.transpose(nat[u][0:n, 0:P], cin[u][:, 0:n], ident[:, :])
                    pe.transpose(nat_k[u][0:n, 0:DH], kin[u][:, 0:n], ident[0:DH, 0:DH])
                    pe.transpose(nat[u][0:n, P:2 * P], vin[u][:, 0:n], ident[:, :]).then_inc(nat_ready[u], 1)
                    pe.wait_ge(norm_ready[u], k + 1 + START)
                    pe.wait_ge(lo_ready[u], k + START)
                    pe.transpose(back[u][:, 0:n], cn[u][0:n, :], ident[0:n, 0:n])
                    pe.transpose(back[u][:, P:P + n], kn[u][0:n, :, :].rearrange("p a d -> p (a d)"), ident[0:n, 0:n]).then_inc(back_ready[u], 1)

                tiles(pe, step)

            @block.scalar
            def _(act):
                def step(u, k, n, j):
                    act.wait_ge(nat_ready[u], k + 1 + START)
                    act.wait_ge(v_stored[u], 16 * k + START)
                    act.activation(junk[0:n, :], nat[u][0:n, 0:P], ACT.Square, accum_out=square[u][0:n, :])
                    act.activation(vn[u][0:n, :], nat[u][0:n, P:2 * P], ACT.Copy).then_inc(square_ready[u], 1)
                    act.drain()
                    act.dma_start(v_nat[bass.ds(j + PAD, n), :], vn[u][0:n, :]).then_inc(v_stored[u], 16)
                    act.wait_ge(back_ready[u], k + 1 + START)
                    act.activation(c_hi[:, bass.ds(j, n)], back[u][:, 0:n], ACT.Copy)
                    act.activation(ki_hi[:, bass.ds(j, n)], back[u][:, P:P + n], ACT.Copy).then_inc(hi_ready[u], 1)

                tiles(act, step)
                act.wait_ge(v_stored[0], 16 * 9 + START)
                act.wait_ge(v_stored[1], 16 * 8 + START)

            @block.vector
            def _(dve):
                dve.wait_ge(g_loaded, 48 + START)

                def step(u, k, n, j):
                    dve.wait_ge(nat_ready[u], k + 1 + START)
                    dve.bn_stats(stats[u][0:n, :], nat_k[u][0:n, 0:DH])
                    dve.drain()
                    dve.bn_aggr(mean_var[u][0:n, :], stats[u][0:n, :])
                    dve.drain()
                    dve.tensor_scalar(var_eps[u][0:n, 1:2], mean_var[u][0:n, 1:2], 1e-5, None, ALU.add)
                    dve.wait_ge(square_ready[u], k + 1 + START)
                    dve.tensor_scalar(var_eps[u][0:n, 0:1], square[u][0:n, :], 1.0 / P, 1e-6, ALU.mult, ALU.add).then_inc(var_ready[u], 1)
                    dve.wait_ge(rstd_ready[u], k + 1 + START)
                    dve.wait_ge(back_ready[u], k + START)
                    dve.wait_ge(copied[u], k + START)
                    dve.scalar_tensor_tensor(out=cn[u][0:n, :], in0=nat[u][0:n, 0:P], scalar=rstd[u][0:n, 0:1], in1=cg[0:n, :], op0=ALU.mult, op1=ALU.mult)
                    dve.tensor_scalar(kn[u][0:n, 1, :], nat_k[u][0:n, 0:DH], mean_var[u][0:n, 0:1], rstd[u][0:n, 1:2], ALU.subtract, ALU.mult)
                    dve.drain()
                    dve.tensor_tensor(kn[u][0:n, 1, :], kn[u][0:n, 1, :], kg[0:n, :], ALU.mult)
                    dve.drain()
                    dve.tensor_tensor(kn[u][0:n, 0, :], kn[u][0:n, 1, :], kb[0:n, :], ALU.add)
                    dve.drain()
                    dve.tensor_copy(kn[u][0:n, 1, :], kn[u][0:n, 0, :]).then_inc(norm_ready[u], 1)
                    dve.wait_ge(hi_ready[u], k + 1 + START)
                    dve.tensor_tensor(c_lo[:, bass.ds(j, n)], back[u][:, 0:n], f32(c_hi[:, bass.ds(j, n)]), ALU.subtract)
                    dve.tensor_tensor(ki_lo[:, bass.ds(j, n)], back[u][:, P:P + n], f32(ki_hi[:, bass.ds(j, n)]), ALU.subtract).then_inc(lo_ready[u], 1)

                tiles(dve, step)


def attention(nc, proj, v_nat, w_uk, w_uv, sinks, attn, keys):
    c_nat, c_hi, c_lo, ki_hi, ki_lo = keys
    with Scope(nc, "at") as s:
        ident = s.sb("ident", [P, P])
        wuk = s.sb("wuk", [P, HEADS, DH])
        wuk_t = s.sb("wuk_t", [P, HEADS // 2, P])
        wuv = s.sb("wuv", [P, HEADS, DH])
        query_key = s.sb("query_key", [P, L])
        limit = s.sb("limit", [P, L])
        base_a = s.sb("base_a", [P, WA])
        dist_a = s.sb("dist_a", [P, WA])
        pair_scale = s.sb("pair_scale", [P, HEADS // 2])
        slope, neg_slope, inv_slope = s.sb("slope", [P, HEADS]), s.sb("neg_slope", [P, HEADS]), s.sb("inv_slope", [P, HEADS])
        sink_u = s.sb("sink_u", [P, HEADS])
        minus_one = s.sb("minus_one", [P, HEADS])
        t_col, ti_col, first_col = s.sb("t_col", [P, 1]), s.sb("ti_col", [P, 1]), s.sb("first_col", [P, 1])
        qa, qb = s.sb("qa", [P, HEADS // 2, P]), s.sb("qb", [P, HEADS // 2, P])
        qa_s, qb_s = s.sb("qa_s", [P, HEADS // 2, P]), s.sb("qb_s", [P, HEADS // 2, P])
        qi = s.sb("qi", [P, HEADS, P])
        qi_2 = s.sb("qi_2", [P, HEADS, P], F32R)
        wi = s.sb("wi", [HEADS, P])
        w_idx = s.sb("w_idx", [P, HEADS])
        k_win = s.sb("k_win", [P, 2, WA])
        v_win = s.sb("v_win", [WH, 2, P])
        ql_hi, ql_lo = s.sb("ql_hi", [P, HEADS, P], F32R), s.sb("ql_lo", [P, HEADS, P], F32R)
        hidden = s.sb("hidden", [P, L])
        dist = s.sb("dist", [P, L])
        score = s.sb("score", [P, TPG, L])
        ints = score[:, 0, :].bitcast(I32)
        rel = [s.sb(f"rel{u}", [P, 1024]) for u in range(2)]
        rel_meta = s.sb("rel_meta", [P, HEADS, META])
        count, wanted, sign = s.sb("count", [P, TPG]), s.sb("wanted", [P, TPG]), s.sb("sign", [P, TPG])
        floor, rise, cand, neg_cand = s.sb("floor", [P, TPG]), s.sb("rise", [P, TPG]), s.sb("cand", [P, TPG]), s.sb("neg_cand", [P, TPG])
        kept = s.sb("kept", [P, TPG])
        below, nearest, more, left = s.sb("below", [P, TPG]), s.sb("nearest", [P, TPG]), s.sb("more", [P, TPG]), s.sb("left", [P, TPG])
        junk = [s.sb(f"junk{j}", [P, L], BF16) for j in range(TPG)]
        u_a = s.sb("u_a", [P, HEADS, WA])
        max_a, bias_a, sink_e = s.sb("max_a", [P, HEADS]), s.sb("bias_a", [P, HEADS]), s.sb("sink_e", [P, HEADS])
        den_a, rden_a = s.sb("den_a", [P, HEADS]), s.sb("rden_a", [P, HEADS])
        u_meta = s.sb("u_meta", [P, HEADS, META])
        u_b = [s.sb(f"u_b{u}", [P, L]) for u in range(2)]
        max_b, max_1, bias_b = s.sb("max_b", [P, HEADS, 4]), s.sb("max_1", [P, HEADS]), s.sb("bias_b", [P, HEADS])
        den_b, rden_b = s.sb("den_b", [P, HEADS]), s.sb("rden_b", [P, HEADS])
        p_t = [s.sb(f"p_t{u}", [P, 4, P]) for u in range(2)]
        ctx_t = s.sb("ctx_t", [P, HEADS, P])
        o_nat = [s.sb(f"o_nat{b}", [P, HEADS * DH]) for b in range(2)]
        o_t = [s.sb(f"o_t{b}", [P, 4, P]) for b in range(2)]

        big = [s.ps(f"big{u}", [P, 1024]) for u in range(2)]
        turn = [s.ps(f"turn{u}", [P, 512]) for u in range(2)]
        misc, ctx = s.ps("misc", [P, 512]), s.ps("ctx", [P, 512])

        id_ready, const_ready, w_loaded = s.sem("id_ready"), s.sem("const_ready"), s.sem("w_loaded")
        iota_ready, iota_used, wukt_ready = s.sem("iota_ready"), s.sem("iota_used"), s.sem("wukt_ready")
        q_loaded, q_scaled, qi_hi, qi_lo = s.sem("q_loaded"), s.sem("q_scaled"), s.sem("qi_hi"), s.sem("qi_lo")
        win_done, qi_loaded, qi_done = s.sem("win_done"), s.sem("qi_loaded"), s.sem("qi_done")
        flipped = s.sem("flipped")
        cand_ready, count_ready, count_seen = s.sems("cand_ready", TPG), s.sems("count_ready", TPG), s.sem("count_seen")
        wi_ready = s.sem("wi_ready")
        t_ready, dist_ready, dist_full = s.sem("t_ready"), s.sem("dist_ready"), s.sem("dist_full")
        big_ready, big_free = s.sems("big_ready"), s.sems("big_free")
        turn_ready, turn_free = s.sems("turn_ready"), s.sems("turn_free")
        pt_ready, pt_free = s.sems("pt_ready"), s.sems("pt_free")
        rel_ready, rel_free = s.sems("rel_ready"), s.sems("rel_free")
        misc_ready, misc_free = s.sem("misc_ready"), s.sem("misc_free")
        relm_ready, ql_hi_ready, ql_lo_ready = s.sem("relm_ready"), s.sem("ql_hi_ready"), s.sem("ql_lo_ready")
        stats_a, exp_a, rden_ready = s.sem("stats_a"), s.sem("exp_a"), s.sem("rden_ready")
        u_ready, p_ready, u_free = s.sem("u_ready"), s.sem("p_ready"), s.sems("u_free")
        ctx_ready, ctx_free = s.sem("ctx_ready"), s.sem("ctx_free")
        logits_seen = s.sem("logits_seen")
        o_ready, attn_stored = s.sem("o_ready"), s.sem("attn_stored")

        class Group:

            def __init__(self, g):
                self.g = g
                self.real = GROUP * (g + 1)
                self.width = META + self.real
                self.blocks = [(b, min(1024, self.real - b)) for b in range(0, self.real, 1024)]
                self.key_tiles = [(a, min(P, self.width - a)) for a in range(0, self.width, P)]
                self.key_fours = [self.key_tiles[a:a + 4] for a in range(0, len(self.key_tiles), 4)]
                nb, nf = len(self.blocks), len(self.key_fours)
                index = {"big": HEADS * nb // 2, "rel": HEADS * nb // 2, "turn": 0, "pt": 0}
                attend = {"big": 1 + HEADS * nb // 2, "rel": 0, "turn": (2 + 4 + 1 + HEADS * nf + 1) // 2,
                          "pt": (4 + HEADS * nf) // 2}
                before = {r: sum(Group(e).per_tile[r] * TPG for e in range(g)) for r in index}
                self.per_tile = {r: index[r] + attend[r] for r in index}
                self.stages = {"index": (before, index),
                               "attend": ({r: before[r] + TPG * index[r] for r in index}, attend)}

            def use(self, ring, n):
                at_start, per_tile = self.stages[self.stage]
                return n % 2, self.i * per_tile[ring] + (at_start[ring] + n // 2)

        groups = [Group(g) for g in range(NG)]
        MISC_OA, MISC_META, MISC_OB = 0, 1, 2

        def misc_use(grp, n):
            return grp.i + 4 * TPG * grp.g if grp.stage == "index" else 3 * grp.i + (4 * TPG * grp.g + TPG + n)

        def of_parity(tile, n):
            return tile[:, :, :].rearrange("p (j e) q -> p j e q", e=2)[:, :, n, :]

        def for_groups(eng, index, select, attend):
            for grp in groups:
                grp.stage = "index"
                if index:
                    with eng.Fori(0, TPG) as i:
                        grp.i = i
                        index(grp, i + TPG * grp.g)
                if select:
                    select(grp)
                grp.stage = "attend"
                with eng.Fori(0, TPG) as i:
                    grp.i = i
                    attend(grp, i + TPG * grp.g)

        with nc.Block() as block:
            @block.sync
            def _(sp):
                s.begin(sp)
                sp.dma_start(wuk[:, :, :], w_uk[0].rearrange("h r d -> r h d")).then_inc(w_loaded, 16)
                sp.dma_start(wuv[:, :, :], w_uv[0].rearrange("h r d -> r h d")).then_inc(w_loaded, 16)
                sp.dma_start(sink_u[:, :], sinks.to_broadcast([P, HEADS])).then_inc(w_loaded, 16)
                for half in range(2):
                    sp.dma_start(k_win[half * DH:half * DH + DH, :, 0:META],
                                 proj[R_KA:R_KA + P, PAD:PAD + META].rearrange("(k d) c -> d k c", d=DH)).then_inc(w_loaded, 16)
                sp.dma_start(v_win[0:META, 0, :], v_nat[PAD:PAD + META, :]).then_inc(w_loaded, 16)

                def load_index(grp, t):
                    sp.wait_ge(qi_done, t + START)
                    cols = bass.ds(t * P + (PAD + META), P)
                    for half in range(2):
                        sp.dma_start(qi[half * DH:half * DH + DH, :, :],
                                     proj[R_QI:R_QI + 512, cols].rearrange("(h d) c -> d h c", d=DH)).then_inc(qi_loaded, 16)
                    sp.dma_start(wi[:, :], proj[R_WI:R_WI + HEADS, cols]).then_inc(qi_loaded, 16)

                def load(grp, t):
                    sp.wait_ge(win_done, t + START)
                    q0 = t * P + (PAD + META)
                    w0 = t * P + META
                    cols = bass.ds(q0, P)
                    win = bass.ds(w0, WIN)
                    sp.dma_start(qa[:, :, :], proj[R_QA:R_QA + 512, cols].rearrange("(j p) c -> p j c", p=P)).then_inc(q_loaded, 16)
                    sp.dma_start(qb[:, :, :], proj[R_QB:R_QB + 512, cols].rearrange("(j p) c -> p j c", p=P)).then_inc(q_loaded, 16)
                    for half in range(2):
                        sp.dma_start(k_win[half * DH:half * DH + DH, :, META:WA],
                                     proj[R_KA:R_KA + P, win].rearrange("(k d) c -> d k c", d=DH)).then_inc(q_loaded, 16)
                    sp.dma_start(v_win[META:WH, 0, :], v_nat[bass.ds(w0, WH - META), :]).then_inc(q_loaded, 16)
                    sp.dma_start(v_win[:, 1, :], v_nat[bass.ds(w0 + (WH - META), WH), :]).then_inc(q_loaded, 16)

                for_groups(sp, load_index, None, load)
            q_dmas, qi_dmas = 6, 3

            @block.gpsimd
            def _(pool):
                make_identity(nc, pool, ident, id_ready)
                pool.iota(ints, pattern=[[-1, L]], base=META, channel_multiplier=1).then_inc(iota_ready, 1)
                pool.memset(minus_one[:, :], -1.0)
                for h in range(HEADS):
                    pool.memset(slope[:, h:h + 1], 2.0 ** -(h + 1))
                    pool.memset(neg_slope[:, h:h + 1], -2.0 ** -(h + 1))
                    pool.memset(inv_slope[:, h:h + 1], 2.0 ** (h + 1))
                pool.wait_ge(iota_used, 1 + START)
                for half in range(2):
                    pool.drain()
                    last = pool.iota(ints[half * DH:half * DH + DH, :], pattern=[[1, L]], base=-(META + CHUNK) - CHUNK * half,
                                     channel_multiplier=0)
                last.then_inc(iota_ready, 1)
                pool.drain()
                pool.wait_ge(iota_used, 2 + START)
                pool.iota(ints[:, 0:WIN], pattern=[[-1, WIN]], base=CHUNK, channel_multiplier=1).then_inc(iota_ready, 1)
                pool.drain()
                pool.wait_ge(const_ready, 1 + START)

                def index(grp, t):
                    pool.drain()
                    pool.wait_ge(qi_hi, t + 1 + START)
                    pool.tensor_tensor(qi_2[DH:P, :, :], qi[DH:P, :, :], f32(qi_2[DH:P, :, :]), ALU.subtract).then_inc(qi_lo, 1)
                    pool.drain()

                def one(tile, j):
                    return tile[:, j:j + 1]

                def judge(j, n):
                    pool.wait_ge(count_ready[j], n + 1 + START)
                    pool.sem_inc(count_seen, 1)
                    pool.tensor_scalar(one(kept, j), one(count, j), one(wanted, j), one(rise, j), ALU.is_ge, ALU.mult)
                    pool.drain()
                    pool.tensor_tensor(one(floor, j), one(floor, j), one(kept, j), ALU.add)

                def next_power(j, scales):
                    pool.drain()
                    if len(scales) == 2:
                        pool.tensor_scalar(one(cand, j), one(floor, j), scales[0], scales[1], ALU.mult, ALU.mult)
                    else:
                        pool.tensor_scalar(one(cand, j), one(floor, j), scales[0], TOP, ALU.mult, ALU.min)
                    pool.drain()
                    pool.tensor_scalar(one(neg_cand, j), one(cand, j), -1.0, None, ALU.mult)
                    pool.tensor_tensor(one(rise, j), one(cand, j), one(floor, j), ALU.subtract)
                    pool.drain()
                    pool.sem_inc(cand_ready[j], 1)

                def next_step(j, source):
                    if source is floor:
                        pool.drain()
                    pool.tensor_scalar(one(rise, j), one(source, j), 0.5, None, ALU.mult)
                    pool.drain()
                    if j < DVE_TILES:
                        last = pool.tensor_tensor(one(cand, j), one(floor, j), one(rise, j), ALU.add)
                    else:
                        last = pool.tensor_scalar(one(neg_cand, j), one(floor, j), -1.0, one(rise, j), ALU.mult, ALU.subtract)
                    last.then_inc(cand_ready[j], 1)

                def select(grp):
                    rounds = grp.g * ROUNDS
                    pool.wait_ge(flipped, grp.g + 1 + START)
                    pool.memset(floor[:, :], 0.0)
                    pool.memset(rise[:, :], TINY)
                    pool.memset(cand[:, :], TINY)
                    pool.memset(neg_cand[:, :], -TINY)
                    pool.drain()
                    for j in ORDER:
                        pool.sem_inc(cand_ready[j], 1)
                    for n, scales in enumerate([(2.0 ** 64, 2.0 ** 64)] + [(2.0 ** 2 ** e,) for e in range(6, -1, -1)]):
                        for j in ORDER:
                            judge(j, rounds + n)
                            next_power(j, scales)
                    for j in ORDER:
                        judge(j, rounds + 8)
                        next_step(j, floor)
                    with pool.Fori(0, MANTISSA - 1) as i:
                        for j in ORDER:
                            judge(j, i + (rounds + 9))
                            next_step(j, rise)
                    for j in ORDER:
                        judge(j, rounds + ROUNDS - 1)
                    pool.drain()
                    for j in ORDER:
                        pool.sem_inc(cand_ready[j], 1)

                def attend(grp, t):
                    w = grp.width
                    pool.wait_ge(q_loaded, 16 * q_dmas * (t + 1) + START)
                    scale = pair_scale[:, :].rearrange("p (j a) -> p j a", a=1).to_broadcast([P, HEADS // 2, P])
                    pool.tensor_tensor(qa_s[:, :, :], qa[:, :, :], scale, ALU.mult).then_inc(q_scaled, 1)
                    pool.tensor_tensor(qb_s[:, :, :], qb[:, :, :], scale, ALU.mult).then_inc(q_scaled, 1)
                    pool.wait_ge(dist_ready, t + 1 + START)
                    pool.tensor_tensor(dist[:, 0:w], dist[:, 0:w], hidden[:, 0:w], ALU.add).then_inc(dist_full, 1)
                    pool.wait_ge(exp_a, t + 1 + START)
                    pool.tensor_tensor(rden_a[:, :], den_a[:, :], sink_e[:, :], ALU.add)
                    pool.drain()
                    pool.tensor_tensor(rden_a[:, :], rden_a[:, :], minus_one[:, :], ALU.pow).then_inc(rden_ready, 1)
                    pool.wait_ge(p_ready, HEADS * (t + 1) + START)
                    pool.tensor_tensor(rden_b[:, :], den_b[:, :], minus_one[:, :], ALU.pow).then_inc(rden_ready, 1)

                for_groups(pool, index, select, attend)

            @block.tensor
            def _(pe):
                pe.wait_ge(id_ready, 1 + START)
                pe.wait_ge(w_loaded, 96 + START)
                for j in range(HEADS // 2):
                    last = pe.transpose(ctx[:, j * P:j * P + P], wuk[:, 2 * j:2 * j + 2, :].rearrange("r a d -> r (a d)"), ident[:, :])
                last.then_inc(wukt_ready, 1)
                pe.wait_ge(wukt_ready, 2 + START)
                pe.wait_ge(const_ready, 1 + START)

                def index(grp, t):
                    nb = len(grp.blocks)

                    pe.wait_ge(misc_free, misc_use(grp, 0) + START)
                    pe.wait_ge(qi_lo, t + 1 + START)
                    for h in range(HEADS):
                        out = misc[:, h * META:h * META + META]
                        pe.matmul(out, qi_2[:, h, :], ki_hi[:, 0:META], start=True, stop=False)
                        pe.matmul(out, qi_2[:, h, :], ki_lo[:, 0:META], start=False, stop=True)
                    pe.drain()
                    pe.transpose(misc[:, 128:128 + HEADS], wi[:, :], ident[0:HEADS, 0:HEADS]).then_inc(misc_ready, 1)

                    for h in range(HEADS):
                        for b, (a0, wb) in enumerate(grp.blocks):
                            u, k = grp.use("big", h * nb + b)
                            pe.wait_ge(big_free[u], k + START)
                            for a in range(0, wb, 512):
                                cols = slice(META + a0 + a, META + a0 + a + 512)
                                pe.matmul(big[u][:, a:a + 512], qi_2[:, h, :], ki_hi[:, cols], start=True, stop=False)
                                last = pe.matmul(big[u][:, a:a + 512], qi_2[:, h, :], ki_lo[:, cols], start=False, stop=True)
                            last.then_inc(big_ready[u], 1)
                    pe.drain()
                    pe.sem_inc(qi_done, 1)

                def attend(grp, t):
                    w = grp.width
                    nb, nf = len(grp.blocks), len(grp.key_fours)

                    pe.wait_ge(q_loaded, 16 * q_dmas * (t + 1) + START)
                    pe.wait_ge(q_scaled, 2 * t + 1 + START)
                    for n in range(2):
                        u, k = grp.use("big", n)
                        pe.wait_ge(big_free[u], k + START)
                        for h in range(4 * n, 4 * n + 4):
                            r = slice(h % 2 * DH, h % 2 * DH + DH)
                            at = h % 2 * 512 + h // 2 % 2 * 256
                            last = pe.matmul(big[u][:, at:at + WA], qa_s[r, h // 2, :], k_win[r, n, :],
                                             start=True, stop=True)
                        last.then_inc(big_ready[u], 1)

                    pe.wait_ge(q_scaled, 2 * t + 2 + START)
                    for n in range(2):
                        u, k = grp.use("turn", n)
                        pe.wait_ge(turn_free[u], k + START)
                        r = slice(n * DH, n * DH + DH)
                        for j in range(HEADS // 2):
                            last = pe.matmul(turn[u][:, j * P:j * P + P], wuk_t[r, j, :], qb_s[r, j, :],
                                             start=True, stop=True)
                        last.then_inc(turn_ready[u], 1)

                    def turn_a(n):
                        u, k = grp.use("turn", 2 + n)
                        pe.wait_ge(turn_free[u], k + START)
                        for m in range(4):
                            h, b = 2 * n + m // 2, m % 2
                            last = pe.transpose(turn[u][0:WH, m * P:m * P + P], u_a[:, h, b * WH:b * WH + WH], ident[:, :])
                        last.then_inc(turn_ready[u], 1)

                    pe.wait_ge(exp_a, t + 1 + START)
                    turn_a(0)
                    pe.wait_ge(misc_free, misc_use(grp, MISC_OA) + START)
                    for n in range(4):
                        if n < 3:
                            turn_a(n + 1)
                        u, k = grp.use("pt", n)
                        pe.wait_ge(pt_ready[u], k + 1 + START)
                        for m in range(4):
                            h, b = 2 * n + m // 2, m % 2
                            kv = h // 4
                            last = pe.matmul(misc[:, h * DH:h * DH + DH], p_t[u][0:WH, m, :], v_win[:, b, kv * DH:kv * DH + DH],
                                             start=(b == 0), stop=(b == 1))
                        last.then_inc(pt_free[u], 1)
                    pe.drain()
                    pe.sem_inc(misc_ready, 1)
                    pe.sem_inc(win_done, 1)

                    def turn_output(branch, n):
                        u, k = grp.use("turn", n)
                        pe.wait_ge(o_ready, 2 * t + 1 + branch + START)
                        pe.wait_ge(turn_free[u], k + START)
                        for j in range(4):
                            last = pe.transpose(turn[u][:, j * P:j * P + P], o_nat[branch][:, j * P:j * P + P], ident[:, :])
                        last.then_inc(turn_ready[u], 1)

                    turn_output(0, 6)

                    pe.wait_ge(misc_free, misc_use(grp, MISC_META) + START)
                    pe.wait_ge(ql_lo_ready, 2 * t + 2 + START)
                    for h in range(HEADS):
                        last = matmul3(pe, misc[:, h * META:h * META + META], ql_hi[:, h, :], ql_lo[:, h, :], c_hi[:, 0:META],
                                       c_lo[:, 0:META], True, True)
                    last.then_inc(misc_ready, 1)

                    def logits(h):
                        for b, (a0, wb) in enumerate(grp.blocks):
                            u, k = grp.use("big", 2 + h * nb + b)
                            pe.wait_ge(big_free[u], k + START)
                            for a in range(0, wb, 512):
                                cols = slice(META + a0 + a, META + a0 + a + 512)
                                last = matmul3(pe, big[u][:, a:a + 512], ql_hi[:, h, :], ql_lo[:, h, :], c_hi[:, cols], c_lo[:, cols], True, True)
                            last.then_inc(big_ready[u], 1)

                    def turn_b(h, f):
                        u, k = grp.use("turn", 7 + h * nf + f)
                        pe.wait_ge(turn_free[u], k + START)
                        for m, (a, n) in enumerate(grp.key_fours[f]):
                            last = pe.transpose(turn[u][0:n, m * P:m * P + P], u_b[h % 2][:, a:a + n], ident[:, :])
                        last.then_inc(turn_ready[u], 1)

                    def weigh(h):
                        pe.wait_ge(p_ready, HEADS * t + h + 1 + START)
                        turn_b(h, 0)
                        pe.wait_ge(ctx_free, HEADS * t + h + START)
                        for f in range(nf):
                            if f + 1 < nf:
                                turn_b(h, f + 1)
                                if f + 2 == nf:
                                    pe.drain()
                                    pe.sem_inc(u_free[h % 2], 1)
                            u, k = grp.use("pt", 4 + h * nf + f)
                            pe.wait_ge(pt_ready[u], k + 1 + START)
                            for m, (a, n) in enumerate(grp.key_fours[f]):
                                last = pe.matmul(ctx[:, 0:P], c_nat[0:n, a:a + P], p_t[u][0:n, m, :],
                                                 start=(a == 0), stop=(a + n == w))
                            last.then_inc(pt_free[u], 1)
                        pe.drain()
                        pe.sem_inc(ctx_ready, 1)

                    logits(0)
                    for h in range(HEADS):
                        if h + 1 < HEADS:
                            logits(h + 1)
                        weigh(h)
                    pe.wait_ge(misc_free, misc_use(grp, MISC_OB) + START)
                    pe.wait_ge(ctx_free, HEADS * (t + 1) + START)
                    for h in range(HEADS):
                        last = pe.matmul(misc[:, h * DH:h * DH + DH], ctx_t[:, h, :], wuv[:, h, :], start=True, stop=True)
                    last.then_inc(misc_ready, 1)
                    turn_output(1, 7 + HEADS * nf)

                for_groups(pe, index, None, attend)

            @block.scalar
            def _(act):
                act.wait_ge(wukt_ready, 1 + START)
                act.activation(wuk_t[:, :, :], ctx[:, :].rearrange("p (j r) -> p j r", j=4), ACT.Copy).then_inc(wukt_ready, 1)
                act.wait_ge(iota_ready, 3 + START)
                act.activation(base_a[:, META:WA], ints[:, 0:WIN], ACT.Abs).then_inc(iota_used, 1)
                act.wait_ge(const_ready, 1 + START)

                def index(grp, t):
                    nb = len(grp.blocks)
                    act.wait_ge(qi_loaded, 16 * qi_dmas * (t + 1) + START)
                    act.wait_ge(qi_done, t + START)
                    act.activation(qi_2[:, :, :], qi[:, :, :], ACT.Copy).then_inc(qi_hi, 1)
                    act.wait_ge(misc_ready, misc_use(grp, 0) + 1 + START)
                    act.wait_ge(wi_ready, t + START)
                    act.activation(w_idx[:, :], misc[:, 128:128 + HEADS], ACT.Copy, scale=HEADS ** -0.5 * DH ** -0.5)
                    act.activation(rel_meta[:, :, :], misc[:, 0:128].rearrange("p (h m) -> p h m", h=HEADS), ACT.Relu)
                    act.drain()
                    act.sem_inc(relm_ready, 1)
                    act.sem_inc(misc_free, 1)
                    for h in range(HEADS):
                        for b, (a0, wb) in enumerate(grp.blocks):
                            u, k = grp.use("big", h * nb + b)
                            v, kv = grp.use("rel", h * nb + b)
                            act.wait_ge(big_ready[u], k + 1 + START)
                            act.wait_ge(rel_free[v], kv + START)
                            act.activation(rel[v][:, 0:wb], big[u][:, 0:wb], ACT.Relu)
                            act.drain()
                            act.sem_inc(rel_ready[v], 1)
                            act.sem_inc(big_free[u], 1)

                def select(grp):
                    with act.Fori(0, ROUNDS) as i:
                        for j in range(DVE_TILES, TPG):
                            act.wait_ge(cand_ready[j], i + (grp.g * (ROUNDS + 1) + 1) + START)
                            act.activation(junk[j][:, 0:grp.width], score[:, j, 0:grp.width], ACT.Sign, bias=neg_cand[:, j:j + 1],
                                           accum_out=count[:, j:j + 1]).then_inc(count_ready[j], 1)

                def attend(grp, t):
                    w = grp.width
                    nb, nf = len(grp.blocks), len(grp.key_fours)
                    act.wait_ge(t_ready, t + 1 + START)
                    act.activation(dist[:, 0:w], query_key[:, 0:w], ACT.Abs, bias=t_col[:, :]).then_inc(dist_ready, 1)
                    for n in range(2):
                        u, k = grp.use("turn", n)
                        act.wait_ge(turn_ready[u], k + 1 + START)
                        act.activation(of_parity(ql_hi, n), turn[u][:, :].rearrange("p (j q) -> p j q", j=4), ACT.Copy).then_inc(ql_hi_ready, 1)
                    act.wait_ge(stats_a, t + 1 + START)
                    for h in range(HEADS):
                        act.activation(u_a[:, h, :], u_a[:, h, :], ACT.Exp, bias=bias_a[:, h:h + 1], scale=2.0 ** -(h + 1),
                                       accum_out=den_a[:, h:h + 1])
                    act.activation(sink_e[:, :], sink_e[:, :], ACT.Exp).then_inc(exp_a, 1)

                    def evacuate(n, m, rows, count):
                        u, k = grp.use("turn", n)
                        v, kv = grp.use("pt", m)
                        act.wait_ge(turn_ready[u], k + 1 + START)
                        act.wait_ge(pt_free[v], kv + START)
                        act.activation(p_t[v][0:rows, 0:count, :], turn[u][0:rows, 0:count * P].rearrange("p (m q) -> p m q", m=count), ACT.Copy)
                        act.drain()
                        act.sem_inc(pt_ready[v], 1)
                        act.sem_inc(turn_free[u], 1)

                    def output(branch, use_misc, n):
                        act.wait_ge(rden_ready, 2 * t + 1 + branch + START)
                        act.wait_ge(misc_ready, misc_use(grp, use_misc) + 1 + START)
                        rden = rden_a if branch == 0 else rden_b
                        for h in range(HEADS):
                            act.activation(o_nat[branch][:, h * DH:h * DH + DH], misc[:, h * DH:h * DH + DH], ACT.Copy, scale=rden[:, h:h + 1])
                        act.drain()
                        act.sem_inc(o_ready, 1)
                        act.sem_inc(misc_free, 1)
                        u, k = grp.use("turn", n)
                        act.wait_ge(turn_ready[u], k + 1 + START)
                        act.wait_ge(attn_stored, 32 * t + START)
                        act.activation(o_t[branch][:, :, :], turn[u][:, :].rearrange("p (j q) -> p j q", j=4), ACT.Copy).then_inc(turn_free[u], 1)
                        act.drain()
                        act.dma_start(attn[branch * 512:branch * 512 + 512, bass.ds(t * P, P)].rearrange("(j p) c -> p j c", p=P),
                                      o_t[branch][:, :, :]).then_inc(attn_stored, 16)

                    for n in range(4):
                        evacuate(2 + n, n, WH, 4)
                    output(0, MISC_OA, 6)
                    for h in range(HEADS):
                        act.wait_ge(u_ready, HEADS * t + h + 1 + START)
                        act.activation(u_b[h % 2][:, 0:w], u_b[h % 2][:, 0:w], ACT.Exp, bias=bias_b[:, h:h + 1], scale=2.0 ** -(h + 1),
                                       accum_out=den_b[:, h:h + 1]).then_inc(p_ready, 1)
                        for f in range(nf):
                            four = grp.key_fours[f]
                            evacuate(7 + h * nf + f, 4 + h * nf + f, four[0][1], len(four))
                        act.wait_ge(ctx_ready, HEADS * t + h + 1 + START)
                        act.activation(ctx_t[:, h, :], ctx[:, 0:P], ACT.Copy).then_inc(ctx_free, 1)
                    output(1, MISC_OB, 7 + HEADS * nf)

                for_groups(act, index, select, attend)
                act.wait_ge(attn_stored, 32 * SEQ // P + START)

            @block.vector
            def _(dve):
                dve.wait_ge(iota_ready, 1 + START)
                dve.tensor_copy(query_key[:, :], ints).then_inc(iota_used, 1)
                dve.wait_ge(iota_ready, 2 + START)
                dve.tensor_copy(limit[:, :], ints).then_inc(iota_used, 1)
                dve.memset(t_col[:, :], -float(P))
                dve.memset(ti_col[:, :], -float(P))
                for h in range(HEADS):
                    dve.memset(pair_scale[h % 2 * DH:h % 2 * DH + DH, h // 2:h // 2 + 1], DH ** -0.5 * 2.0 ** (h + 1))
                dve.wait_ge(iota_used, 3 + START)
                dve.wait_ge(w_loaded, 96 + START)
                dve.memset(base_a[0:DH, META + 2 * CHUNK:WA], BIG)
                dve.memset(base_a[DH:P, META:META + CHUNK], BIG)
                dve.drain()
                dve.tensor_copy(dist_a[:, META:WA], base_a[:, META:WA])
                dve.tensor_tensor(sink_u[:, :], sink_u[:, :], inv_slope[:, :], ALU.mult)
                dve.drain()
                dve.sem_inc(const_ready, 1)

                def index(grp, t):
                    w = grp.width
                    nb = len(grp.blocks)

                    def dst(a, b):
                        return score[:, bass.ds(grp.i, 1), a:b].rearrange("p a c -> p (a c)")

                    def src(h, a, b):
                        return dst(a, b) if h else hidden[:, a:b]

                    dve.drain()
                    dve.tensor_scalar(ti_col[:, :], ti_col[:, :], float(P), None, ALU.add)
                    dve.drain()
                    dve.tensor_scalar(hidden[:, 0:w], limit[:, 0:w], ti_col[:, :], BIG, ALU.is_ge, ALU.mult)
                    for h in range(HEADS):
                        def add(out, rel_h, prev, op, free=None):
                            ins = dve.scalar_tensor_tensor(out=out, in0=rel_h, scalar=w_idx[:, h:h + 1], in1=prev, op0=ALU.mult, op1=op)
                            if free is not None:
                                ins.then_inc(free, 1)
                        op = ALU.add if h else ALU.subtract
                        dve.drain()
                        if h == 0:
                            dve.wait_ge(relm_ready, t + 1 + START)
                        add(dst(0, META), rel_meta[:, h, :], src(h, 0, META), op)
                        for b, (a0, wb) in enumerate(grp.blocks):
                            v, kv = grp.use("rel", h * nb + b)
                            dve.wait_ge(rel_ready[v], kv + 1 + START)
                            add(dst(META + a0, META + a0 + wb), rel[v][:, 0:wb], src(h, META + a0, META + a0 + wb), op, rel_free[v])
                    dve.drain()
                    dve.sem_inc(wi_ready, 1)

                def select(grp):
                    w = grp.width

                    def one(tile, j):
                        return tile[:, j:j + 1]

                    for j in range(TPG):
                        dve.tensor_scalar(junk[j][:, 0:w], score[:, j, 0:w], 0.0, None, ALU.is_ge, ALU.add, accum_out=one(count, j))
                    dve.drain()
                    dve.tensor_scalar(sign[:, :], count[:, :], float(TOPK), 2.0, ALU.is_ge, ALU.mult)
                    dve.drain()
                    dve.tensor_scalar(sign[:, :], sign[:, :], -1.0, None, ALU.add)
                    dve.drain()
                    for j in range(TPG):
                        slope_k = (2 * TOPK - 1 - w) * (0.5 if j < DVE_TILES else 1.0)
                        offset = (w + 1) * 0.5 if j < DVE_TILES else 0.0
                        dve.tensor_scalar(one(wanted, j), one(sign, j), slope_k, offset, ALU.mult, ALU.add)
                        dve.tensor_scalar(score[:, j, 0:w], score[:, j, 0:w], one(sign, j), None, ALU.mult)
                    dve.drain()
                    dve.sem_inc(flipped, 1)
                    with dve.Fori(0, ROUNDS) as i:
                        for j in range(DVE_TILES):
                            dve.wait_ge(cand_ready[j], i + (grp.g * (ROUNDS + 1) + 1) + START)
                            dve.tensor_scalar(junk[j][:, 0:w], score[:, j, 0:w], one(cand, j), None, ALU.is_ge, ALU.add,
                                              accum_out=one(count, j)).then_inc(count_ready[j], 1)
                    for j in range(TPG):
                        dve.wait_ge(cand_ready[j], (grp.g + 1) * (ROUNDS + 1) + START)
                    for j in range(TPG):
                        x = score[:, j, 0:w]
                        spare, other = hidden[:, 0:w], dist[:, 0:w]
                        dve.tensor_scalar(spare, x, one(floor, j), None, ALU.is_le, ALU.add, accum_out=one(below, j))
                        dve.drain()
                        dve.tensor_scalar(spare, spare, TOP, None, ALU.mult)
                        dve.drain()
                        dve.tensor_tensor_reduce(other, x, spare, 1.0, TOP, ALU.add, ALU.min, one(nearest, j))
                        if j >= DVE_TILES:
                            dve.tensor_scalar(one(wanted, j), one(wanted, j), 0.5, (w + 1) * 0.5, ALU.mult, ALU.add)
                        dve.tensor_scalar(one(more, j), one(below, j), -1.0, float(w), ALU.mult, ALU.add)
                        dve.drain()
                        dve.tensor_tensor(one(more, j), one(more, j), one(wanted, j), ALU.is_ge)
                        dve.tensor_tensor(one(nearest, j), one(nearest, j), one(floor, j), ALU.subtract)
                        dve.drain()
                        dve.tensor_tensor(one(nearest, j), one(nearest, j), one(more, j), ALU.mult)
                        dve.drain()
                        dve.tensor_tensor(one(floor, j), one(floor, j), one(nearest, j), ALU.add)
                        dve.drain()
                        dve.tensor_tensor(one(floor, j), one(floor, j), one(sign, j), ALU.mult)
                        dve.tensor_scalar(x, x, one(sign, j), None, ALU.mult)
                        dve.drain()
                        dve.tensor_scalar(other, x, one(floor, j), None, ALU.is_gt, ALU.add, accum_out=one(left, j))
                        dve.tensor_scalar(spare, x, one(floor, j), None, ALU.is_equal)
                        dve.drain()
                        dve.tensor_scalar(one(left, j), one(left, j), -1.0, float(TOPK), ALU.mult, ALU.add)
                        dve.tensor_tensor_scan(x, spare, spare, 0.0, ALU.add, ALU.max)
                        dve.drain()
                        dve.scalar_tensor_tensor(out=x, in0=x, scalar=one(left, j), in1=spare, op0=ALU.is_le, op1=ALU.mult)
                        dve.drain()
                        dve.tensor_tensor(x, x, other, ALU.add)
                        dve.drain()
                        dve.tensor_scalar(x, x, 0.5, BIG, ALU.is_lt, ALU.mult)
                        dve.drain()

                def attend(grp, t):
                    w = grp.width
                    nb = len(grp.blocks)
                    dve.tensor_scalar(t_col[:, :], t_col[:, :], float(P), None, ALU.add)
                    dve.drain()
                    dve.tensor_scalar(hidden[:, 0:w], limit[:, 0:w], t_col[:, :], BIG, ALU.is_ge, ALU.mult)
                    dve.tensor_scalar(first_col[:, :], t_col[:, :], 1.0, BIG, ALU.is_lt, ALU.mult)
                    dve.tensor_scalar(dist_a[:, 0:META], query_key[:, 0:META], t_col[:, :], None, ALU.add)
                    dve.drain()
                    dve.tensor_scalar(dist_a[:, META:META + CHUNK], base_a[:, META:META + CHUNK], first_col[:, :], None, ALU.max)
                    dve.drain()
                    dve.sem_inc(t_ready, 1)
                    for n in range(2):
                        u, k = grp.use("big", n)
                        dve.wait_ge(big_ready[u], k + 1 + START)
                        dve.tensor_tensor(u_a[:, 4 * n:4 * n + 4, :].rearrange("p (j e) c -> p e j c", e=2),
                                          big[u][:, :].rearrange("p (e j c) -> p e j c", e=2, j=2)[:, :, :, 0:WA],
                                          dist_a[:, :].rearrange("p (a b c) -> p a b c", a=1, b=1).to_broadcast([P, 2, 2, WA]),
                                          ALU.subtract).then_inc(big_free[u], 1)
                    dve.drain()
                    dve.tensor_reduce(max_a[:, :], u_a[:, :, :], AX, ALU.max)
                    dve.drain()
                    dve.tensor_tensor(max_a[:, :], max_a[:, :], sink_u[:, :], ALU.max)
                    dve.drain()
                    dve.tensor_tensor(bias_a[:, :], max_a[:, :], neg_slope[:, :], ALU.mult)
                    dve.tensor_tensor(sink_e[:, :], sink_u[:, :], max_a[:, :], ALU.subtract)
                    dve.drain()
                    dve.tensor_tensor(sink_e[:, :], sink_e[:, :], slope[:, :], ALU.mult).then_inc(stats_a, 1)
                    for n in range(2):
                        u, k = grp.use("turn", n)
                        dve.wait_ge(ql_hi_ready, 2 * t + n + 1 + START)
                        dve.tensor_tensor(of_parity(ql_lo, n), turn[u][:, :].rearrange("p (j q) -> p j q", j=4),
                                          f32(of_parity(ql_hi, n)), ALU.subtract)
                        dve.drain()
                        dve.sem_inc(turn_free[u], 1)
                        dve.sem_inc(ql_lo_ready, 1)

                    dve.wait_ge(dist_full, t + 1 + START)
                    dve.tensor_tensor(dist[:, 0:w], dist[:, 0:w], score[:, bass.ds(grp.i, 1), 0:w].rearrange("p a c -> p (a c)"), ALU.max)
                    dve.drain()

                    dve.wait_ge(misc_ready, misc_use(grp, MISC_META) + 1 + START)
                    dve.tensor_tensor(u_meta[:, :, :], misc[:, 0:128].rearrange("p (h m) -> p h m", h=HEADS),
                                      dist[:, 0:META].rearrange("p (a m) -> p a m", a=1).to_broadcast([P, HEADS, META]), ALU.subtract).then_inc(misc_free, 1)
                    dve.drain()
                    for h in range(HEADS):
                        dve.wait_ge(u_free[h % 2], HEADS // 2 * t + h // 2 + START)
                        dve.tensor_scalar(u_b[h % 2][:, 0:META], u_meta[:, h, :], 1.0, None, ALU.mult, ALU.max, accum_out=max_b[:, h, 0:1])
                        for b, (a0, wb) in enumerate(grp.blocks):
                            u, k = grp.use("big", 2 + h * nb + b)
                            dve.wait_ge(big_ready[u], k + 1 + START)
                            dve.sem_inc(logits_seen, 1)
                            cols = slice(META + a0, META + a0 + wb)
                            dve.tensor_tensor_reduce(u_b[h % 2][:, cols], big[u][:, 0:wb], dist[:, cols], 1.0, MARK,
                                                     ALU.subtract, ALU.max, max_b[:, h, b + 1:b + 2]).then_inc(big_free[u], 1)
                        dve.drain()
                        dve.tensor_reduce(max_1[:, h:h + 1], max_b[:, h, 0:nb + 1], AX, ALU.max)
                        dve.drain()
                        dve.tensor_scalar(bias_b[:, h:h + 1], max_1[:, h:h + 1], -2.0 ** -(h + 1), None, ALU.mult).then_inc(u_ready, 1)

                for_groups(dve, index, select, attend)


def mix_and_ffn(nc, proj, attn, h0, w_o_a, w_o_b, w_out, ln1_g, ln1_b, w_gate, w_up, w_down, ln2_g, ln2_b, out):
    with Scope(nc, "ff") as s:
        ident, half = s.sb("ident", [P, P]), s.sb("half", [P, 1])
        ln = [s.sb(f"ln{n}", [P, D]) for n in range(4)]
        raw = [s.sb(f"raw{u}", [P, D]) for u in range(2)]
        w_hi, w_lo = [s.sb(f"w_hi{u}", [P, D], F32R) for u in range(2)], [s.sb(f"w_lo{u}", [P, D], F32R) for u in range(2)]
        resid = s.sb("resid", [P, TPG, D])
        h1_hi, h1_lo = s.sb("h1_hi", [P, KT, GROUP], F32R), s.sb("h1_lo", [P, KT, GROUP], F32R)
        f_hi, f_lo = s.sb("f_hi", [P, FT, GROUP], F32R), s.sb("f_lo", [P, FT, GROUP], F32R)
        gates = [s.sb(f"gates{u}", [P, 2, GROUP]) for u in range(2)]
        part_a, part_b, mixed = s.sb("part_a", [P, GROUP]), s.sb("part_b", [P, GROUP]), s.sb("mixed", [P, GROUP])
        silu = s.sb("silu", [P, GROUP])
        feature = s.sb("feature", [P, GROUP])
        stats, mean_var, var_eps, rstd = s.sb("stats", [P, 2, 6]), s.sb("mv", [P, 2]), s.sb("ve", [P, 1]), s.sb("rstd", [P, 1])
        bank = s.ps("bank", [P, 8, GROUP])

        const_ready, ln_loaded = s.sem("const_ready"), s.sem("ln_loaded")
        w_loaded, hi_ready, lo_ready, w_used = s.sems("w_loaded"), s.sems("hi_ready"), s.sems("lo_ready"), s.sems("w_used")
        att_loaded, att_hi, att_lo, h0_loaded = s.sem("att_loaded"), s.sem("att_hi"), s.sem("att_lo"), s.sem("h0_loaded")
        gates_loaded, gates_used = s.sems("gates_loaded"), s.sems("gates_used")
        mix_ready, mix_hi, mix_lo = s.sem("mix_ready"), s.sem("mix_hi"), s.sem("mix_lo")
        acc_free = s.sem("acc_free")
        var_ready, rstd_ready = s.sem("var_ready"), s.sem("rstd_ready")
        h1_ready, h1_turned, h1_hi_ready, h1_lo_ready = s.sem("h1_ready"), s.sem("h1_turned"), s.sem("h1_hi_ready"), s.sem("h1_lo_ready")
        silu_ready, feat_ready, feat_hi, feat_lo = s.sem("silu_ready"), s.sem("feat_ready"), s.sem("feat_hi"), s.sem("feat_lo")
        h2_ready, out_stored = s.sem("h2_ready"), s.sem("out_stored")

        Y, M, F, Z = 0, 4, 8, 8 + FT
        PAIRS = Z + FT // 2

        with nc.Block() as block:
            @block.sync
            def _(sp):
                s.begin(sp)
                for n, v in enumerate((ln1_g, ln1_b, ln2_g, ln2_b)):
                    sp.dma_start(ln[n][:, :], v.to_broadcast([P, D])).then_inc(ln_loaded, 16)
                cols = lambda w, c: w.rearrange("(k p) c -> p k c", p=P)[:, :, bass.ds(c * P, P)]
                rows = lambda w, c: w[bass.ds(c * P, P), :]
                as_k = lambda t: t[:, :].rearrange("p (k c) -> p k c", c=P)
                with sp.Fori(0, NG) as g:
                    sp.wait_ge(out_stored, 16 * TPG * g + START)
                    sp.dma_start(resid[:, :, :].rearrange("p a (b c) -> p (a b) c", c=GROUP),
                                 attn.rearrange("(k p) c -> p k c", p=P)[:, :, bass.ds(g * GROUP, GROUP)]).then_inc(att_loaded, 16)

                    def chunk(u, k, parts):
                        sp.wait_ge(lo_ready[u], g * PAIRS + k + START)
                        for dst, src in parts:
                            sp.dma_start(dst, src).then_inc(w_loaded[u], 16)

                    with sp.Fori(0, 4) as i:
                        for u in range(2):
                            c = 2 * i + u
                            chunk(u, Y + i, [(as_k(raw[u])[:, 0:4, :], cols(w_o_a, c)), (as_k(raw[u])[:, 4:8, :], cols(w_o_b, c))])
                            sp.wait_ge(gates_used[u], 4 * g + i + START)
                            for b in range(2):
                                sp.dma_start(gates[u][:, b, :], proj[bass.ds(c * P + R_GATE + b * D, P), bass.ds(g * GROUP + PAD + META, GROUP)]).then_inc(gates_loaded[u], 16)
                    sp.wait_ge(att_lo, g + 1 + START)
                    sp.dma_start(resid[:, :, :], h0[bass.ds(g * GROUP + META, GROUP), :].rearrange("(a p) d -> p a d", p=P)).then_inc(h0_loaded, 16)
                    with sp.Fori(0, 4) as i:
                        for u in range(2):
                            chunk(u, M + i, [(raw[u][:, :], rows(w_out, 2 * i + u))])
                    with sp.Fori(0, FT) as i:
                        chunk(0, F + i, [(as_k(raw[0]), cols(w_gate, i))])
                        chunk(1, F + i, [(as_k(raw[1]), cols(w_up, i))])
                    with sp.Fori(0, FT // 2) as i:
                        for u in range(2):
                            chunk(u, Z + i, [(raw[u][:, :], rows(w_down, 2 * i + u))])

            @block.gpsimd
            def _(pool):
                pool.memset(half[:, :], -0.5)
                make_identity(nc, pool, ident, const_ready)
                pool.drain()
                with pool.Fori(0, NG) as g:
                    def low_part(u, k):
                        pool.wait_ge(hi_ready[u], g * PAIRS + k + 1 + START)
                        pool.tensor_tensor(w_lo[u][:, :], raw[u][:, :], f32(w_hi[u][:, :]), ALU.subtract).then_inc(lo_ready[u], 1)

                    def inverse_roots(n):
                        with pool.Fori(0, TPG) as a:
                            pool.wait_ge(var_ready, 2 * TPG * g + n * TPG + a + 1 + START)
                            pool.tensor_tensor(rstd[:, :], var_eps[:, :], half[:, :], ALU.pow).then_inc(rstd_ready, 1)

                    pool.wait_ge(att_hi, g + 1 + START)
                    pool.tensor_tensor(f_lo[:, 0:8, :], resid[:, :, :].rearrange("p a (b c) -> p (a b) c", c=GROUP), f32(f_hi[:, 0:8, :]),
                                       ALU.subtract).then_inc(att_lo, 1)
                    with pool.Fori(0, F) as i:
                        for u in range(2):
                            low_part(u, i)
                    inverse_roots(0)
                    with pool.Fori(F, PAIRS) as i:
                        for u in range(2):
                            low_part(u, i)
                    inverse_roots(1)

            @block.scalar
            def _(act):
                with act.Fori(0, NG) as g:
                    def high_part(u, k, double=False):
                        act.wait_ge(w_loaded[u], (16 * (PAIRS + 4) * g + (32 * (k + 1) if double else 16 * (k + 1) + 64)) + START)
                        act.wait_ge(w_used[u], g * PAIRS + k + START)
                        act.activation(w_hi[u][:, :], raw[u][:, :], ACT.Copy).then_inc(hi_ready[u], 1)

                    act.wait_ge(att_loaded, 16 * (g + 1) + START)
                    act.wait_ge(w_used[1], g * PAIRS + START)
                    act.activation(f_hi[:, 0:8, :], resid[:, :, :].rearrange("p a (b c) -> p (a b) c", c=GROUP), ACT.Copy).then_inc(att_hi, 1)
                    with act.Fori(0, 4) as i:
                        for u in range(2):
                            high_part(u, Y + i, True)
                            act.wait_ge(mix_ready, 8 * g + 2 * i + u + 1 + START)
                            act.activation(f_hi[:, bass.ds(8 + 2 * i + u, 1), :], mixed[:, :].rearrange("p (a c) -> p a c", a=1), ACT.Copy).then_inc(mix_hi, 1)
                    with act.Fori(0, 4) as i:
                        for u in range(2):
                            high_part(u, M + i)
                    with act.Fori(0, TPG) as a:
                        for b in range(2):
                            act.wait_ge(h1_turned, 2 * TPG * g + 2 * a + b + 1 + START)
                            act.activation(h1_hi[:, 4 * b:4 * b + 4, bass.ds(a * P, P)], bank[:, b, :].rearrange("p (k c) -> p k c", c=P),
                                           ACT.Copy).then_inc(h1_hi_ready, 1)

                    def gate(n, i):
                        act.wait_ge(w_used[0], g * PAIRS + F + i + 1 + START)
                        act.wait_ge(feat_ready, FT * g + i + START)
                        act.activation(silu[:, :], bank[:, 4 * n, :], ACT.Silu).then_inc(silu_ready, 1)
                        act.wait_ge(feat_ready, FT * g + i + 1 + START)
                        act.activation(f_hi[:, bass.ds(i, 1), :], feature[:, :].rearrange("p (a c) -> p a c", a=1), ACT.Copy).then_inc(feat_hi, 1)

                    high_part(0, F)
                    high_part(1, F)
                    with act.Fori(0, FT // 2 - 1) as i:
                        for n in range(2):
                            high_part(0, F + 2 * i + n + 1)
                            gate(n, 2 * i + n)
                            high_part(1, F + 2 * i + n + 1)
                    high_part(0, F + FT - 1)
                    gate(0, FT - 2)
                    high_part(1, F + FT - 1)
                    high_part(0, Z)
                    gate(1, FT - 1)
                    high_part(1, Z)
                    with act.Fori(1, FT // 2) as i:
                        for u in range(2):
                            high_part(u, Z + i)
                    with act.Fori(0, TPG) as a:
                        act.wait_ge(h2_ready, TPG * g + a + 1 + START)
                        act.dma_start(out[0, bass.ds(g * GROUP + a * P, P), :], resid[:, bass.ds(a, 1), :].rearrange("p a d -> p (a d)")).then_inc(out_stored, 16)
                act.wait_ge(out_stored, 16 * TPG * NG + START)

            @block.vector
            def _(dve):
                dve.wait_ge(ln_loaded, 64 + START)

                with dve.Fori(0, NG) as g:
                    def one(ap):
                        return ap.rearrange("p a c -> p (a c)")

                    with dve.Fori(0, 4) as i:
                        for u in range(2):
                            n = 2 * i + u
                            dve.wait_ge(gates_loaded[u], 32 * (4 * g + i + 1) + START)
                            dve.wait_ge(w_used[u], g * PAIRS + Y + i + 1 + START)
                            dve.tensor_tensor(part_a[:, :], bank[:, 2 * u, :], gates[u][:, 0, :], ALU.mult)
                            dve.tensor_tensor(part_b[:, :], bank[:, 2 * u + 1, :], gates[u][:, 1, :], ALU.mult)
                            dve.drain()
                            dve.sem_inc(gates_used[u], 1)
                            dve.sem_inc(acc_free, 1)
                            dve.tensor_tensor(mixed[:, :], part_a[:, :], part_b[:, :], ALU.add).then_inc(mix_ready, 1)
                            dve.wait_ge(mix_hi, 8 * g + n + 1 + START)
                            dve.tensor_tensor(one(f_lo[:, bass.ds(8 + n, 1), :]), mixed[:, :], f32(one(f_hi[:, bass.ds(8 + n, 1), :])), ALU.subtract).then_inc(mix_lo, 1)
                            dve.drain()

                    def layer_norm(stage, n, done):
                        for a in range(TPG):
                            x = resid[:, a, :]
                            for b in range(2):
                                dve.scalar_tensor_tensor(out=resid[:, a, b * 512:b * 512 + 512], in0=resid[:, a, b * 512:b * 512 + 512],
                                                         scalar=ALPHA, in1=bank[:, 2 * a + b, :], op0=ALU.mult, op1=ALU.add)
                            dve.drain()
                            dve.sem_inc(acc_free, 1)
                            for b in range(2):
                                dve.bn_stats(stats[:, b, :], resid[:, a, b * 512:b * 512 + 512])
                            dve.drain()
                            dve.bn_aggr(mean_var[:, :], stats[:, :, :])
                            dve.drain()
                            dve.tensor_scalar(var_eps[:, :], mean_var[:, 1:2], 1e-5, None, ALU.add).then_inc(var_ready, 1)
                            dve.wait_ge(rstd_ready, 2 * TPG * g + TPG * stage + a + 1 + START)
                            dve.tensor_scalar(x, x, mean_var[:, 0:1], rstd[:, :], ALU.subtract, ALU.mult)
                            dve.drain()
                            dve.tensor_tensor(x, x, ln[n][:, :], ALU.mult)
                            dve.drain()
                            dve.tensor_tensor(x, x, ln[n + 1][:, :], ALU.add).then_inc(done, 1)

                    dve.wait_ge(h0_loaded, 16 * (g + 1) + START)
                    dve.wait_ge(w_used[1], g * PAIRS + F + START)
                    layer_norm(0, 0, h1_ready)
                    with dve.Fori(0, TPG) as a:
                        for b in range(2):
                            dve.wait_ge(h1_hi_ready, 2 * TPG * g + 2 * a + b + 1 + START)
                            dve.tensor_tensor(h1_lo[:, 4 * b:4 * b + 4, bass.ds(a * P, P)], bank[:, b, :].rearrange("p (k c) -> p k c", c=P),
                                              f32(h1_hi[:, 4 * b:4 * b + 4, bass.ds(a * P, P)]), ALU.subtract).then_inc(h1_lo_ready, 1)
                    with dve.Fori(0, FT // 2) as i:
                        for n in range(2):
                            t = 2 * i + n
                            dve.wait_ge(silu_ready, FT * g + t + 1 + START)
                            dve.wait_ge(w_used[1], g * PAIRS + F + t + 1 + START)
                            dve.tensor_tensor(feature[:, :], silu[:, :], bank[:, 4 * n + 1, :], ALU.mult).then_inc(feat_ready, 1)
                            dve.wait_ge(feat_hi, FT * g + t + 1 + START)
                            dve.tensor_tensor(one(f_lo[:, bass.ds(t, 1), :]), feature[:, :], f32(one(f_hi[:, bass.ds(t, 1), :])), ALU.subtract).then_inc(feat_lo, 1)
                            dve.drain()
                    dve.wait_ge(w_used[1], g * PAIRS + PAIRS + START)
                    layer_norm(1, 2, h2_ready)

            @block.tensor
            def _(pe):
                pe.wait_ge(const_ready, 1 + START)
                ACC = 8 + 2 * TPG
                with pe.Fori(0, NG) as g:
                    def weights(u, k):
                        pe.wait_ge(hi_ready[u], g * PAIRS + k + 1 + START)
                        pe.wait_ge(lo_ready[u], g * PAIRS + k + 1 + START)

                    def turned(dst, u, first, count, hi, lo, hi_first):
                        for c in range(count):
                            w = slice((first + c) * P, (first + c) * P + P)
                            last = matmul3(pe, dst, w_hi[u][:, w], w_lo[u][:, w], hi[:, hi_first + c, :], lo[:, hi_first + c, :],
                                           c == 0, c == count - 1)
                        return last

                    with pe.Fori(0, 4) as i:
                        for u in range(2):
                            pe.wait_ge(att_lo, g + 1 + START)
                            pe.wait_ge(acc_free, ACC * g + START)
                            weights(u, Y + i)
                            pe.wait_ge(mix_ready, 8 * g + 2 * i + START)
                            turned(bank[:, 2 * u, :], u, 0, 4, f_hi, f_lo, 0)
                            turned(bank[:, 2 * u + 1, :], u, 4, 4, f_hi, f_lo, 4).then_inc(w_used[u], 1)

                    def natural(u, first, last_one, hi, lo, at):
                        for a in range(TPG):
                            for b in range(2):
                                q, c = slice(a * P, a * P + P), slice(b * 512, b * 512 + 512)
                                last = matmul3(pe, bank[:, 2 * a + b, :], hi[:, at, q], lo[:, at, q], w_hi[u][:, c], w_lo[u][:, c],
                                               first, last_one)
                        last.then_inc(w_used[u], 1)

                    pe.wait_ge(acc_free, ACC * g + 8 + START)
                    for c in range(8):
                        weights(c % 2, M + c // 2)
                        pe.wait_ge(mix_lo, 8 * g + 8 + START)
                        natural(c % 2, c == 0, c == 7, f_hi, f_lo, 8 + c)
                    pe.wait_ge(acc_free, ACC * g + 8 + TPG + START)
                    for a in range(TPG):
                        pe.wait_ge(h1_ready, TPG * g + a + 1 + START)
                        for b in range(2):
                            if a:
                                pe.wait_ge(h1_lo_ready, 2 * TPG * g + 2 * (a - 1) + b + 1 + START)
                            for c in range(4):
                                last = pe.transpose(bank[:, b, c * P:c * P + P], resid[:, a, (4 * b + c) * P:(4 * b + c) * P + P], ident[:, :])
                            last.then_inc(h1_turned, 1)
                    with pe.Fori(0, FT // 2) as i:
                        for n in range(2):
                            pe.wait_ge(h1_lo_ready, 2 * TPG * (g + 1) + START)
                            pe.wait_ge(feat_ready, FT * g + 2 * i + START)
                            for u in range(2):
                                weights(u, F + 2 * i + n)
                                turned(bank[:, 4 * n + u, :], u, 0, 8, h1_hi, h1_lo, 0).then_inc(w_used[u], 1)
                    pe.wait_ge(feat_lo, FT * (g + 1) + START)
                    for c in range(FT):
                        weights(c % 2, Z + c // 2)
                        natural(c % 2, c == 0, c == FT - 1, f_hi, f_lo, c)


def build(nc, x, meta_tokens, ln0_g, ln0_b, w_in, b_gate, kv_norm_g, w_uk, w_uv, k_idx_g, k_idx_b, sinks, w_o_a, w_o_b,
          w_out, ln1_g, ln1_b, w_ff_gate, w_ff_up, w_ff_down, ln2_g, ln2_b, out, phases=4):
    h0 = nc.dram_tensor("h0", (L, D), F32, kind="Internal").ap()
    proj = nc.dram_tensor("proj", (4096, LP), F32, kind="Internal").ap()
    v_nat = nc.dram_tensor("v_nat", (LP, P), F32, kind="Internal").ap()
    attn = nc.dram_tensor("attn", (D, SEQ), F32, kind="Internal").ap()
    project(nc, x, meta_tokens, ln0_g, ln0_b, w_in, b_gate, h0, proj, v_nat)
    if phases > 1:
        with Scope(nc, "keys") as s:
            keys = (s.sb("c_nat", [P, 17 * P]), s.sb("c_hi", [P, L], F32R), s.sb("c_lo", [P, L], F32R),
                    s.sb("ki_hi", [P, L], F32R), s.sb("ki_lo", [P, L], F32R))
            prepare_keys(nc, proj, kv_norm_g, k_idx_g, k_idx_b, v_nat, keys)
            if phases > 2:
                attention(nc, proj, v_nat, w_uk, w_uv, sinks, attn, keys)
    if phases > 3:
        mix_and_ffn(nc, proj, attn, h0, w_o_a[0], w_o_b[0], w_out[0], ln1_g, ln1_b, w_ff_gate[0], w_ff_up[0], w_ff_down[0],
                    ln2_g, ln2_b, out)


_INS = ["x", "meta_tokens", "ln0_g", "ln0_b", "w_in", "b_gate", "kv_norm_g", "w_uk", "w_uv", "k_idx_g", "k_idx_b", "sinks",
        "w_o_a", "w_o_b", "w_out", "ln1_g", "ln1_b", "w_ff_gate", "w_ff_up", "w_ff_down", "ln2_g", "ln2_b"]


def kernel(**inputs):
    import numpy as np
    import concourse.bacc as bacc
    from concourse.bass_utils import run_bass_kernel_spmd

    nc = bacc.Bacc("TRN2", target_bir_lowering=False, num_devices=1)
    arrays, args = {}, []
    for name in _INS:
        a = np.ascontiguousarray(inputs[name])
        arrays[f"in_{name}"] = a
        args.append(nc.dram_tensor(f"in_{name}", a.shape, mybir.dt.from_np(a.dtype), kind="ExternalInput").ap())
    args.append(nc.dram_tensor("out_0", (1, SEQ, D), F32, kind="ExternalOutput").ap())
    build(nc, *args)
    r = run_bass_kernel_spmd(nc, [arrays], core_ids=[0])
    return r.results[0]["out_0"]
```

```python
from contextlib import ExitStack

import concourse.bass as bass
from concourse import mybir

ALU = mybir.AluOpType
ACT = mybir.ActivationFunctionType
AX = mybir.AxisListType.X
F32 = mybir.dt.float32
F32R = mybir.dt.float32r
I32 = mybir.dt.int32
BF16 = mybir.dt.bfloat16

P = 128
D = 1024
KT = D // P
SEQ = 2048
META = 16
L = SEQ + META
CHUNK = 64
HEADS = 8
DH = 64
TOPK = 256
DFF = 2816
FT = DFF // P
GROUP = 512
NG = SEQ // GROUP
TPG = GROUP // P
ALPHA = 2.0 ** 0.25
PAD = CHUNK
LP = L + PAD
BIG = 1e37
START = 1
MARK = -3e38
R_QA, R_KA, R_VA, R_QB, R_CB, R_QI, R_KI, R_WI, R_GATE = 0, 512, 640, 768, 1280, 1408, 1920, 1984, 2048
SPLIT_CHUNKS = 16
GATE_COL = 1992
WIN = 2 * CHUNK + CHUNK
WA = META + WIN
TINY, TOP = 2.0 ** -126, 3e38
MANTISSA = 23
ROUNDS = 1 + 8 + MANTISSA
DVE_TILES = 2
ACT_TILES = range(DVE_TILES, 4)
POWERS = [(2.0 ** 64, 2.0 ** 64)] + [(2.0 ** 2 ** e,) for e in range(6, -1, -1)]
WH = WA // 2


def f32(ap):
    return ap.bitcast(F32)


class Scope(ExitStack):

    def __init__(self, nc, tag):
        super().__init__()
        self.nc, self.tag, self.all_sems = nc, tag, []

    def sb(self, name, shape, dt=F32):
        return self.enter_context(self.nc.sbuf_tensor(f"{self.tag}_{name}", shape, dt))

    def ps(self, name, shape):
        return self.enter_context(self.nc.psum_tensor(f"{self.tag}_{name}", shape, F32))

    def sem(self, name):
        self.all_sems.append(self.enter_context(self.nc.semaphore(f"{self.tag}_{name}")))
        return self.all_sems[-1]

    def begin(self, sp):
        for sem in self.all_sems:
            sp.sem_inc(sem, START)

    def sems(self, name, n=2):
        return [self.sem(f"{name}{i}") for i in range(n)]


def matmul3(pe, out, lhs_hi, lhs_lo, rhs_hi, rhs_lo, start, stop):
    pe.matmul(out, lhs_lo, rhs_hi, start=start, stop=False)
    pe.matmul(out, lhs_hi, rhs_hi, start=False, stop=False)
    return pe.matmul(out, lhs_hi, rhs_lo, start=False, stop=stop)


def make_identity(nc, pool, ident, ready):
    pool.memset(ident[:, :], 0.0)
    pool.drain()
    pool.affine_select(out=ident[:, :], in_=ident[:, :], compare_op=ALU.not_equal, fill=1.0, base=0,
                       pattern=[[-1, P]], channel_multiplier=1).then_inc(ready, 1)


def project(nc, x, meta_tokens, ln0_g, ln0_b, w_in, b_gate, h0, proj, v_nat):
    with Scope(nc, "pj") as s:
        h_hi, h_lo = s.sb("h_hi", [P, KT, L], F32R), s.sb("h_lo", [P, KT, L], F32R)
        ident = s.sb("ident", [P, P])
        zeros = s.sb("zeros", [P, PAD])
        half = s.sb("half", [P, 1])
        id_ready, zero_ready, zero_stored = s.sem("id_ready"), s.sem("zero_ready"), s.sem("zero_stored")
        with Scope(nc, "ln") as a:
            xt = [a.sb(f"x{u}", [P, D]) for u in range(2)]
            hb = [a.sb(f"h{u}", [P, D]) for u in range(2)]
            gain, shift = a.sb("gain", [P, D]), a.sb("shift", [P, D])
            stats = [a.sb(f"stats{u}", [P, 2, 6]) for u in range(2)]
            mean_var = [a.sb(f"mv{u}", [P, 2]) for u in range(2)]
            var_eps = [a.sb(f"ve{u}", [P, 1]) for u in range(2)]
            rstd = [a.sb(f"rstd{u}", [P, 1]) for u in range(2)]
            turned = [a.ps(f"turned{u}", [P, KT, P]) for u in range(2)]
            gb_loaded = a.sem("gb_loaded")
            x_loaded, x_free = a.sems("x_loaded"), a.sems("x_free")
            var_ready, rstd_ready = a.sem("var_ready"), a.sem("rstd_ready")
            h_ready, h_stored = a.sems("h_ready"), a.sems("h_stored")
            turned_ready, hi_ready, turned_free = a.sems("turned_ready"), a.sems("hi_ready"), a.sems("turned_free")

            def tiles(eng, step):
                step(0, 0, META, None)
                with eng.Fori(0, SEQ // P // 2) as i:
                    step(1, i, P, 2 * P * i)
                    step(0, i + 1, P, 2 * P * i + P)

            with nc.Block() as block:
                @block.sync
                def _(sp):
                    s.begin(sp)
                    a.begin(sp)
                    sp.dma_start(gain[:, :], ln0_g.rearrange("(a d) -> a d", a=1).to_broadcast([P, D])).then_inc(gb_loaded, 16)
                    sp.dma_start(shift[:, :], ln0_b.rearrange("(a d) -> a d", a=1).to_broadcast([P, D])).then_inc(gb_loaded, 16)

                    def load(u, k, n, r):
                        sp.wait_ge(x_free[u], k + START)
                        src = meta_tokens if r is None else x[0, bass.ds(r, P), :]
                        sp.dma_start(xt[u][0:n, :], src).then_inc(x_loaded[u], 16)

                    tiles(sp, load)
                    sp.wait_ge(zero_ready, 1 + START)
                    sp.dma_start(proj[R_KA:R_KA + P, 0:PAD], zeros[:, :]).then_inc(zero_stored, 16)
                    for half_cols in range(2):
                        sp.dma_start(v_nat[0:PAD, half_cols * 64:half_cols * 64 + 64], zeros[0:PAD, :]).then_inc(zero_stored, 16)
                    sp.wait_ge(zero_stored, 48 + START)

                @block.gpsimd
                def _(pool):
                    make_identity(nc, pool, ident, id_ready)
                    pool.memset(half[:, :], -0.5)
                    pool.memset(zeros[:, :], 0.0).then_inc(zero_ready, 1)
                    pool.drain()

                    def inverse_root(u, k, n, r):
                        pool.wait_ge(var_ready, 2 * k + u + 1 + START)
                        pool.tensor_tensor(rstd[u][0:n, :], var_eps[u][0:n, :], half[0:n, :], ALU.pow).then_inc(rstd_ready, 1)

                    tiles(pool, inverse_root)

                @block.vector
                def _(dve):
                    def statistics(u, k, n):
                        dve.wait_ge(x_loaded[u], 16 * (k + 1) + START)
                        for c in range(2):
                            dve.bn_stats(stats[u][0:n, c, :], xt[u][0:n, c * 512:c * 512 + 512])
                        dve.drain()
                        dve.bn_aggr(mean_var[u][0:n, :], stats[u][0:n, :, :])
                        dve.drain()
                        dve.tensor_scalar(var_eps[u][0:n, :], mean_var[u][0:n, 1:2], 1e-5, None, ALU.add).then_inc(var_ready, 1)
                        dve.wait_ge(turned_ready[u], k + START)
                        dve.wait_ge(h_stored[u], 16 * k + START)
                        dve.scalar_tensor_tensor(out=hb[u][0:n, :], in0=xt[u][0:n, :], scalar=mean_var[u][0:n, 0:1], in1=gain[0:n, :],
                                                 op0=ALU.subtract, op1=ALU.mult).then_inc(x_free[u], 1)

                    def low_part(u, k, n, col):
                        dve.wait_ge(hi_ready[u], k + 1 + START)
                        dve.tensor_tensor(h_lo[:, :, bass.ds(col, n)], turned[u][:, :, 0:n],
                                          f32(h_hi[:, :, bass.ds(col, n)]), ALU.subtract).then_inc(turned_free[u], 1)

                    def finish(u, k, n):
                        dve.drain()
                        dve.wait_ge(rstd_ready, 2 * k + u + 1 + START)
                        dve.scalar_tensor_tensor(out=hb[u][0:n, :], in0=hb[u][0:n, :], scalar=rstd[u][0:n, :], in1=shift[0:n, :],
                                                 op0=ALU.mult, op1=ALU.add).then_inc(h_ready[u], 1)

                    dve.wait_ge(gb_loaded, 32 + START)
                    statistics(0, 0, META)
                    finish(0, 0, META)
                    statistics(1, 0, P)
                    low_part(0, 0, META, 0)
                    finish(1, 0, P)
                    with dve.Fori(0, SEQ // P // 2 - 1) as i:
                        statistics(0, i + 1, P)
                        low_part(1, i, P, META + 2 * P * i)
                        finish(0, i + 1, P)
                        statistics(1, i + 1, P)
                        low_part(0, i + 1, P, META + 2 * P * i + P)
                        finish(1, i + 1, P)
                    last = SEQ // P // 2
                    statistics(0, last, P)
                    low_part(1, last - 1, P, L - 2 * P)
                    finish(0, last, P)
                    low_part(0, last, P, L - P)

                @block.tensor
                def _(pe):
                    pe.wait_ge(id_ready, 1 + START)

                    def turn(u, k, n, r):
                        pe.wait_ge(h_ready[u], k + 1 + START)
                        pe.wait_ge(turned_free[u], k + START)
                        for c in range(KT):
                            last = pe.transpose(turned[u][:, c, 0:n], hb[u][0:n, c * P:c * P + P], ident[0:n, 0:n])
                        last.then_inc(turned_ready[u], 1)

                    tiles(pe, turn)

                @block.scalar
                def _(act):
                    def high_part(u, k, n, r):
                        act.wait_ge(h_ready[u], k + 1 + START)
                        dst = h0[0:META, :] if r is None else h0[bass.ds(r + META, P), :]
                        act.dma_start(dst, hb[u][0:n, :]).then_inc(h_stored[u], 16)
                        act.wait_ge(turned_ready[u], k + 1 + START)
                        col = 0 if r is None else r + META
                        act.activation(h_hi[:, :, bass.ds(col, n)], turned[u][:, :, 0:n], ACT.Copy).then_inc(hi_ready[u], 1)

                    tiles(act, high_part)
                    act.wait_ge(h_stored[0], 16 * 9 + START)
                    act.wait_ge(h_stored[1], 16 * 8 + START)

        with Scope(nc, "in") as a:
            raw = [a.sb(f"raw{u}", [P, KT, P]) for u in range(2)]
            w_hi = [a.sb(f"w_hi{u}", [P, KT, P], F32R) for u in range(2)]
            w_lo = [a.sb(f"w_lo{u}", [P, KT, P], F32R) for u in range(2)]
            row = [a.sb(f"row{u}", [P, L]) for u in range(2)]
            bias = [a.sb(f"bias{u}", [P, 1]) for u in range(2)]
            acc = [a.ps(f"acc{g}", [P, GROUP]) for g in range(NG)]
            acc_meta = [a.ps(f"acc_meta{u}", [P, GROUP]) for u in range(2)]
            w_loaded, hi_ready, lo_ready, w_free = a.sems("w_loaded"), a.sems("hi_ready"), a.sems("lo_ready"), a.sems("w_free")
            acc_ready = a.sems("acc_ready", NG)
            acc_free = a.sems("acc_free", NG + 1)
            stored = a.sems("stored")
            half_plain, half_all = SPLIT_CHUNKS // 2, SPLIT_CHUNKS

            with nc.Block() as block:
                @block.sync
                def _(sp):
                    a.begin(sp)
                    def load(u, k, gates):
                        sp.wait_ge(lo_ready[u], k + START)
                        first = (2 * k + u) * P
                        if gates:
                            first = first - (R_GATE - GATE_COL)
                        sp.dma_start(raw[u][:, :, :], w_in[0].rearrange("(k p) c -> p k c", p=P)[:, :, bass.ds(first, P)]).then_inc(w_loaded[u], 16)
                        if gates:
                            sp.wait_ge(acc_free[NG], 2 * k + u - 1 + START)
                            sp.dma_start(bias[u][:, :], b_gate[0].rearrange("(a b) -> a b", b=1)[bass.ds((2 * k + u) * P - R_GATE, P), :]).then_inc(w_loaded[u], 16)

                    def store(u, k):
                        for n in range(NG + 1):
                            sp.wait_ge(acc_free[n], 2 * k + u + 1 + START)
                        sp.dma_start(proj[bass.ds((2 * k + u) * P, P), PAD:LP], row[u][:, :]).then_inc(stored[u], 16)

                    load(0, 0, False)
                    load(1, 0, False)
                    with sp.Fori(0, half_plain - 1) as k:
                        for u in range(2):
                            store(u, k)
                            load(u, k + 1, False)
                    with sp.Fori(half_plain - 1, half_all - 1) as k:
                        for u in range(2):
                            store(u, k)
                            load(u, k + 1, True)
                    for u in range(2):
                        store(u, half_all - 1)
                    for u in range(2):
                        sp.wait_ge(stored[u], 16 * half_all + START)

                def loaded(eng, u, k, gates):
                    eng.wait_ge(w_loaded[u], (32 * (k + 1) - 16 * half_plain if gates else 16 * (k + 1)) + START)

                @block.gpsimd
                def _(pool):
                    with pool.Fori(0, half_all) as k:
                        for u in range(2):
                            pool.wait_ge(hi_ready[u], k + 1 + START)
                            pool.tensor_tensor(w_lo[u][:, :, :], raw[u][:, :, :], f32(w_hi[u][:, :, :]), ALU.subtract).then_inc(lo_ready[u], 1)

                @block.scalar
                def _(act):
                    def high_part(u, k, gates):
                        loaded(act, u, k, gates)
                        act.wait_ge(w_free[u], k + START)
                        act.activation(w_hi[u][:, :, :], raw[u][:, :, :], ACT.Copy).then_inc(hi_ready[u], 1)

                    def evacuate(u, k):
                        act.wait_ge(stored[u], 16 * k + START)
                        for g in (1, 3):
                            act.wait_ge(acc_ready[g], 2 * k + u + 1 + START)
                            act.activation(row[u][:, META + g * GROUP:META + (g + 1) * GROUP], acc[g][:, :], ACT.Copy).then_inc(acc_free[g], 1)

                    def gate(u, k):
                        act.wait_ge(stored[u], 16 * k + START)
                        for g in range(NG):
                            act.wait_ge(acc_ready[g], 2 * k + u + 1 + START)
                            act.activation(row[u][:, META + g * GROUP:META + (g + 1) * GROUP], acc[g][:, :], ACT.Sigmoid,
                                           bias=bias[u][:, :]).then_inc(acc_free[g], 1)
                        act.wait_ge(w_free[u], k + 1 + START)
                        act.activation(row[u][:, 0:META], acc_meta[u][:, 0:META], ACT.Sigmoid, bias=bias[u][:, :]).then_inc(acc_free[NG], 1)

                    high_part(0, 0, False)
                    with act.Fori(0, half_plain - 1) as k:
                        high_part(1, k, False)
                        evacuate(0, k)
                        high_part(0, k + 1, False)
                        evacuate(1, k)
                    high_part(1, half_plain - 1, False)
                    evacuate(0, half_plain - 1)
                    high_part(0, half_plain, True)
                    evacuate(1, half_plain - 1)
                    with act.Fori(half_plain, half_all - 1) as k:
                        high_part(1, k, True)
                        gate(0, k)
                        high_part(0, k + 1, True)
                        gate(1, k)
                    high_part(1, half_all - 1, True)
                    gate(0, half_all - 1)
                    gate(1, half_all - 1)

                @block.vector
                def _(dve):
                    with dve.Fori(0, half_plain) as k:
                        for u in range(2):
                            dve.wait_ge(stored[u], 16 * k + START)
                            for g in (0, 2):
                                dve.wait_ge(acc_ready[g], 2 * k + u + 1 + START)
                                dve.tensor_copy(row[u][:, META + g * GROUP:META + (g + 1) * GROUP], acc[g][:, :]).then_inc(acc_free[g], 1)
                            dve.wait_ge(w_free[u], k + 1 + START)
                            dve.tensor_copy(row[u][:, 0:META], acc_meta[u][:, 0:META]).then_inc(acc_free[NG], 1)

                @block.tensor
                def _(pe):
                    with pe.Fori(0, half_all) as k:
                        for u in range(2):
                            pe.wait_ge(hi_ready[u], k + 1 + START)
                            pe.wait_ge(lo_ready[u], k + 1 + START)
                            for g in range(NG + 1):
                                pe.wait_ge(acc_free[g], 2 * k + u + START)
                                out = acc[g][:, :] if g < NG else acc_meta[u][:, 0:META]
                                c0, c1 = (META + g * GROUP, META + (g + 1) * GROUP) if g < NG else (0, META)
                                for c in range(KT):
                                    last = matmul3(pe, out, w_hi[u][:, c, :], w_lo[u][:, c, :], h_hi[:, c, c0:c1],
                                                   h_lo[:, c, c0:c1], c == 0, c == KT - 1)
                                last.then_inc(acc_ready[g] if g < NG else w_free[u], 1)


def prepare_keys(nc, proj, kv_norm_g, k_idx_g, k_idx_b, v_nat, keys):
    c_nat, c_hi, c_lo, ki_hi, ki_lo = keys
    with Scope(nc, "ky") as s:
        ident, half = s.sb("ident", [P, P]), s.sb("half", [P, 2])
        cg, kg, kb = s.sb("cg", [P, P]), s.sb("kg", [P, DH]), s.sb("kb", [P, DH])
        cin = [s.sb(f"cin{u}", [P, P]) for u in range(2)]
        kin = [s.sb(f"kin{u}", [DH, P]) for u in range(2)]
        vin = [s.sb(f"vin{u}", [P, P]) for u in range(2)]
        junk = s.sb("junk", [P, P])
        stats = [s.sb(f"stats{u}", [P, 6]) for u in range(2)]
        mean_var = [s.sb(f"mv{u}", [P, 2]) for u in range(2)]
        square = [s.sb(f"square{u}", [P, 1]) for u in range(2)]
        var_eps = [s.sb(f"ve{u}", [P, 2]) for u in range(2)]
        rstd = [s.sb(f"rstd{u}", [P, 2]) for u in range(2)]
        cn = [s.sb(f"cn{u}", [P, P]) for u in range(2)]
        kn = [s.sb(f"kn{u}", [P, 2, DH]) for u in range(2)]
        vn = [s.sb(f"vn{u}", [P, P]) for u in range(2)]
        nat = [s.ps(f"nat{u}", [P, 512]) for u in range(2)]
        nat_k = [s.ps(f"nat_k{u}", [P, 512]) for u in range(2)]
        back = [s.ps(f"back{u}", [P, 512]) for u in range(2)]
        const_ready, g_loaded = s.sem("const_ready"), s.sem("g_loaded")
        loaded, nat_ready, square_ready = s.sems("loaded"), s.sems("nat_ready"), s.sems("square_ready")
        var_ready, rstd_ready, norm_ready, copied = s.sems("var_ready"), s.sems("rstd_ready"), s.sems("norm_ready"), s.sems("copied")
        back_ready, hi_ready, lo_ready, v_stored = s.sems("back_ready"), s.sems("hi_ready"), s.sems("lo_ready"), s.sems("v_stored")

        def tiles(eng, step):
            with eng.Fori(0, L // P // 2) as i:
                for u in range(2):
                    step(u, i, P, (2 * i + u) * P)
            step(0, L // P // 2, L % P, L - L % P)

        with nc.Block() as block:
            @block.sync
            def _(sp):
                s.begin(sp)
                sp.dma_start(cg[:, :], kv_norm_g.to_broadcast([P, P])).then_inc(g_loaded, 16)
                sp.dma_start(kg[:, :], k_idx_g.to_broadcast([P, DH])).then_inc(g_loaded, 16)
                sp.dma_start(kb[:, :], k_idx_b.to_broadcast([P, DH])).then_inc(g_loaded, 16)

                def load(u, k, n, j):
                    sp.wait_ge(nat_ready[u], k + START)
                    for dst, row, rows in ((cin, R_CB, P), (kin, R_KI, DH), (vin, R_VA, P)):
                        sp.dma_start(dst[u][0:rows, 0:n], proj[row:row + rows, bass.ds(j + PAD, n)]).then_inc(loaded[u], 16)

                tiles(sp, load)

            @block.gpsimd
            def _(pool):
                pool.memset(half[:, :], -0.5)
                make_identity(nc, pool, ident, const_ready)
                pool.drain()

                def step(u, k, n, j):
                    pool.wait_ge(var_ready[u], k + 1 + START)
                    pool.tensor_tensor(rstd[u][0:n, :], var_eps[u][0:n, :], half[0:n, :], ALU.pow).then_inc(rstd_ready[u], 1)
                    pool.wait_ge(norm_ready[u], k + 1 + START)
                    pool.tensor_copy(c_nat[0:n, bass.ds(j, P)], cn[u][0:n, :]).then_inc(copied[u], 1)

                tiles(pool, step)

            @block.tensor
            def _(pe):
                pe.wait_ge(const_ready, 1 + START)

                def step(u, k, n, j):
                    pe.wait_ge(loaded[u], 48 * (k + 1) + START)
                    pe.wait_ge(norm_ready[u], k + START)
                    pe.transpose(nat[u][0:n, 0:P], cin[u][:, 0:n], ident[:, :])
                    pe.transpose(nat_k[u][0:n, 0:DH], kin[u][:, 0:n], ident[0:DH, 0:DH])
                    pe.transpose(nat[u][0:n, P:2 * P], vin[u][:, 0:n], ident[:, :]).then_inc(nat_ready[u], 1)
                    pe.wait_ge(norm_ready[u], k + 1 + START)
                    pe.wait_ge(lo_ready[u], k + START)
                    pe.transpose(back[u][:, 0:n], cn[u][0:n, :], ident[0:n, 0:n])
                    pe.transpose(back[u][:, P:P + n], kn[u][0:n, :, :].rearrange("p a d -> p (a d)"), ident[0:n, 0:n]).then_inc(back_ready[u], 1)

                tiles(pe, step)

            @block.scalar
            def _(act):
                def step(u, k, n, j):
                    act.wait_ge(nat_ready[u], k + 1 + START)
                    act.wait_ge(v_stored[u], 16 * k + START)
                    act.activation(junk[0:n, :], nat[u][0:n, 0:P], ACT.Square, accum_out=square[u][0:n, :])
                    act.activation(vn[u][0:n, :], nat[u][0:n, P:2 * P], ACT.Copy).then_inc(square_ready[u], 1)
                    act.drain()
                    act.dma_start(v_nat[bass.ds(j + PAD, n), :], vn[u][0:n, :]).then_inc(v_stored[u], 16)
                    act.wait_ge(back_ready[u], k + 1 + START)
                    act.activation(c_hi[:, bass.ds(j, n)], back[u][:, 0:n], ACT.Copy)
                    act.activation(ki_hi[:, bass.ds(j, n)], back[u][:, P:P + n], ACT.Copy).then_inc(hi_ready[u], 1)

                tiles(act, step)
                act.wait_ge(v_stored[0], 16 * 9 + START)
                act.wait_ge(v_stored[1], 16 * 8 + START)

            @block.vector
            def _(dve):
                dve.wait_ge(g_loaded, 48 + START)

                def step(u, k, n, j):
                    dve.wait_ge(nat_ready[u], k + 1 + START)
                    dve.bn_stats(stats[u][0:n, :], nat_k[u][0:n, 0:DH])
                    dve.drain()
                    dve.bn_aggr(mean_var[u][0:n, :], stats[u][0:n, :])
                    dve.drain()
                    dve.tensor_scalar(var_eps[u][0:n, 1:2], mean_var[u][0:n, 1:2], 1e-5, None, ALU.add)
                    dve.wait_ge(square_ready[u], k + 1 + START)
                    dve.tensor_scalar(var_eps[u][0:n, 0:1], square[u][0:n, :], 1.0 / P, 1e-6, ALU.mult, ALU.add).then_inc(var_ready[u], 1)
                    dve.wait_ge(rstd_ready[u], k + 1 + START)
                    dve.wait_ge(back_ready[u], k + START)
                    dve.wait_ge(copied[u], k + START)
                    dve.scalar_tensor_tensor(out=cn[u][0:n, :], in0=nat[u][0:n, 0:P], scalar=rstd[u][0:n, 0:1], in1=cg[0:n, :], op0=ALU.mult, op1=ALU.mult)
                    dve.tensor_scalar(kn[u][0:n, 1, :], nat_k[u][0:n, 0:DH], mean_var[u][0:n, 0:1], rstd[u][0:n, 1:2], ALU.subtract, ALU.mult)
                    dve.drain()
                    dve.tensor_tensor(kn[u][0:n, 1, :], kn[u][0:n, 1, :], kg[0:n, :], ALU.mult)
                    dve.drain()
                    dve.tensor_tensor(kn[u][0:n, 0, :], kn[u][0:n, 1, :], kb[0:n, :], ALU.add)
                    dve.drain()
                    dve.tensor_copy(kn[u][0:n, 1, :], kn[u][0:n, 0, :]).then_inc(norm_ready[u], 1)
                    dve.wait_ge(hi_ready[u], k + 1 + START)
                    dve.tensor_tensor(c_lo[:, bass.ds(j, n)], back[u][:, 0:n], f32(c_hi[:, bass.ds(j, n)]), ALU.subtract)
                    dve.tensor_tensor(ki_lo[:, bass.ds(j, n)], back[u][:, P:P + n], f32(ki_hi[:, bass.ds(j, n)]), ALU.subtract).then_inc(lo_ready[u], 1)

                tiles(dve, step)


def attention(nc, proj, v_nat, w_uk, w_uv, sinks, attn, keys):
    c_nat, c_hi, c_lo, ki_hi, ki_lo = keys
    with Scope(nc, "at") as s:
        ident = s.sb("ident", [P, P])
        wuk = s.sb("wuk", [P, HEADS, DH])
        wuk_t = s.sb("wuk_t", [P, HEADS // 2, P])
        wuv = s.sb("wuv", [P, HEADS, DH])
        query_key = s.sb("query_key", [P, L])
        limit = s.sb("limit", [P, L])
        base_a = s.sb("base_a", [P, WA])
        dist_a = s.sb("dist_a", [P, WA])
        pair_scale = s.sb("pair_scale", [P, HEADS // 2])
        slope, neg_slope, inv_slope = s.sb("slope", [P, HEADS]), s.sb("neg_slope", [P, HEADS]), s.sb("inv_slope", [P, HEADS])
        sink_u = s.sb("sink_u", [P, HEADS])
        minus_one = s.sb("minus_one", [P, HEADS])
        t_col, neg_t_col, ti_col, first_col = s.sb("t_col", [P, 1]), s.sb("neg_t_col", [P, 1]), s.sb("ti_col", [P, 1]), s.sb("first_col", [P, 1])
        qa, qb = s.sb("qa", [P, HEADS // 2, P]), s.sb("qb", [P, HEADS // 2, P])
        qa_s = s.sb("qa_s", [P, HEADS // 2, P])
        qi = s.sb("qi", [P, HEADS, P])
        qi_2 = s.sb("qi_2", [P, HEADS, P], F32R)
        wi = s.sb("wi", [HEADS, P])
        w_idx = s.sb("w_idx", [P, HEADS])
        k_win = s.sb("k_win", [P, 2, WA])
        v_win = s.sb("v_win", [WH, 2, P])
        ql_hi, ql_lo = s.sb("ql_hi", [P, HEADS, P], F32R), s.sb("ql_lo", [P, HEADS, P], F32R)
        hidden = s.sb("hidden", [P, L])
        dist = s.sb("dist", [P, L])
        score = s.sb("score", [P, TPG, L])
        ints = score[:, 0, :].bitcast(I32)
        rel = [s.sb(f"rel{u}", [P, 1024]) for u in range(2)]
        rel_meta = s.sb("rel_meta", [P, HEADS, META])
        count, wanted, sign = s.sb("count", [P, TPG]), s.sb("wanted", [P, TPG]), s.sb("sign", [P, TPG])
        floor, rise, cand, neg_cand = s.sb("floor", [P, TPG]), s.sb("rise", [P, TPG]), s.sb("cand", [P, TPG]), s.sb("neg_cand", [P, TPG])
        kept = s.sb("kept", [P, TPG])
        below, nearest, more, left = s.sb("below", [P, TPG]), s.sb("nearest", [P, TPG]), s.sb("more", [P, TPG]), s.sb("left", [P, TPG])
        u_a = s.sb("u_a", [P, HEADS, WA])
        max_a, bias_a, sink_e = s.sb("max_a", [P, HEADS]), s.sb("bias_a", [P, HEADS]), s.sb("sink_e", [P, HEADS])
        den_a, rden_a = s.sb("den_a", [P, HEADS]), s.sb("rden_a", [P, HEADS])
        u_meta = s.sb("u_meta", [P, HEADS, META])
        u_b = [s.sb(f"u_b{u}", [P, L]) for u in range(3)]
        spare_halves = u_b[2][:, :].bitcast(BF16)
        junk = [spare_halves[:, 0:L], spare_halves[:, L:2 * L]] + [s.sb(f"junk{j}", [P, L], BF16) for j in range(DVE_TILES, TPG)]
        max_b, max_1, bias_b = s.sb("max_b", [P, HEADS, 4]), s.sb("max_1", [P, HEADS]), s.sb("bias_b", [P, HEADS])
        den_b, rden_b = s.sb("den_b", [P, HEADS]), s.sb("rden_b", [P, HEADS])
        p_t = [s.sb(f"p_t{u}", [P, 4, P]) for u in range(2)]
        ctx_t = s.sb("ctx_t", [P, HEADS, P])
        o_nat = [s.sb(f"o_nat{b}", [P, HEADS * DH]) for b in range(2)]
        o_t = [s.sb(f"o_t{b}", [P, 4, P]) for b in range(2)]

        big = [s.ps(f"big{u}", [P, 1024]) for u in range(2)]
        turn = [s.ps(f"turn{u}", [P, 512]) for u in range(2)]
        misc, ctx = s.ps("misc", [P, 512]), s.ps("ctx", [P, 512])

        id_ready, const_ready, w_loaded = s.sem("id_ready"), s.sem("const_ready"), s.sem("w_loaded")
        iota_ready, iota_used, wukt_ready = s.sem("iota_ready"), s.sem("iota_used"), s.sem("wukt_ready")
        q_loaded, q_scaled, qi_hi, qi_lo = s.sem("q_loaded"), s.sem("q_scaled"), s.sem("qi_hi"), s.sem("qi_lo")
        raw_ready = s.sem("raw_ready")
        win_done, qi_loaded, qi_done = s.sem("win_done"), s.sem("qi_loaded"), s.sem("qi_done")
        flipped = s.sem("flipped")
        cand_ready, count_ready, count_seen = s.sems("cand_ready", TPG - DVE_TILES), s.sems("count_ready", TPG - DVE_TILES), s.sem("count_seen")
        cand_ready, count_ready = dict(zip(ACT_TILES, cand_ready)), dict(zip(ACT_TILES, count_ready))
        wi_ready = s.sem("wi_ready")
        big_ready, big_free = s.sems("big_ready"), s.sems("big_free")
        turn_ready, turn_free = s.sems("turn_ready"), s.sems("turn_free")
        pt_free = s.sems("pt_free")
        rel_free = s.sems("rel_free")
        misc_ready, misc_free = s.sem("misc_ready"), s.sem("misc_free")
        relm_ready, ql_hi_ready = s.sem("relm_ready"), s.sem("ql_hi_ready")
        stats_a, exp_a, rden_ready = s.sem("stats_a"), s.sem("exp_a"), s.sem("rden_ready")
        u_ready, p_ready, ctx_free = s.sem("u_ready"), s.sem("p_ready"), s.sem("ctx_free")
        logits_seen = s.sem("logits_seen")
        o_ready, attn_stored = s.sem("o_ready"), s.sem("attn_stored")

        class Part:

            def __init__(self, g, half):
                self.g, self.half = g, half
                self.real = GROUP * g + GROUP // 2 * (half + 1)
                self.width = META + self.real
                self.blocks = [(b, min(1024, self.real - b)) for b in range(0, self.real, 1024)]
                full = [(a, P) for a in range(0, self.real, P)]
                self.key_fours = [full[a:a + 4] for a in range(0, len(full), 4)] + [[(self.real, META)]]
                nb, nf = len(self.blocks), len(self.key_fours)
                self.per_tile = {"index": {"big": HEADS * nb // 2, "rel": HEADS * nb // 2},
                                 "attend": {"big": 1 + HEADS * nb // 2, "turn": (2 + 4 + 2 + HEADS * nf) // 2,
                                            "pt": (4 + HEADS * nf) // 2}}
                self.at_start = {}
                self.big_order = ([("logits", h, b) for h in range(2) for b in range(nb)] + [("window", 0), ("window", 1)]
                                  + [("logits", h, b) for h in range(2, HEADS) for b in range(nb)])
                self.pt_order = [item for h in range(HEADS) for item in self.turns(h)]
                self.turn_order = [("absorbed", 0), ("absorbed", 1)] + self.pt_order + [("out", 0), ("out", 1)]

            def turns(self, h):
                return [("window", h - 3)] * (3 <= h < 7) + [("latent", h, f) for f in range(len(self.key_fours))]

            def use(self, ring, n):
                if isinstance(n, tuple):
                    n = {"big": self.big_order, "pt": self.pt_order, "turn": self.turn_order}[ring].index(n)
                return n % 2, self.i * self.per_tile[self.stage][ring] + (self.at_start[self.stage][ring] + n // 2)

        class Group:

            def __init__(self, g):
                self.g = g
                self.parts = [Part(g, half) for half in range(2)]
                self.seen = [max(META + GROUP * g + P * (j + 1), META + TOPK) for j in range(TPG)]

        groups = [Group(g) for g in range(NG)]
        used = dict.fromkeys(("big", "rel", "turn", "pt"), 0)
        for group in groups:
            for stage in ("index", "attend"):
                for part in group.parts:
                    part.at_start[stage] = dict(used)
                    for ring, n in part.per_tile[stage].items():
                        used[ring] += TPG // 2 * n
        MISC_META, MISC_OA, MISC_OB = 0, 1, 2

        def misc_use(grp, n):
            tiles = TPG // 2 * grp.half
            return grp.i + (4 * TPG * grp.g + tiles) if grp.stage == "index" else 3 * grp.i + (4 * TPG * grp.g + TPG + 3 * tiles + n)

        def of_parity(tile, n):
            return tile[:, :, :].rearrange("p (j e) q -> p j e q", e=2)[:, :, n, :]

        def for_groups(eng, index, select, attend):
            def for_parts(group, stage, body):
                for part in group.parts:
                    part.stage = stage
                    with eng.Fori(0, TPG // 2) as i:
                        part.i = i
                        body(part, i + (TPG * group.g + TPG // 2 * part.half))

            for group in groups:
                if index:
                    for_parts(group, "index", index)
                if select:
                    select(group)
                for_parts(group, "attend", attend)

        with nc.Block() as block:
            @block.sync
            def _(sp):
                s.begin(sp)
                sp.dma_start(wuk[:, :, :], w_uk[0].rearrange("h r d -> r h d")).then_inc(w_loaded, 16)
                sp.dma_start(wuv[:, :, :], w_uv[0].rearrange("h r d -> r h d")).then_inc(w_loaded, 16)
                sp.dma_start(sink_u[:, :], sinks.to_broadcast([P, HEADS])).then_inc(w_loaded, 16)
                for half in range(2):
                    sp.dma_start(k_win[half * DH:half * DH + DH, :, 0:META],
                                 proj[R_KA:R_KA + P, PAD:PAD + META].rearrange("(k d) c -> d k c", d=DH)).then_inc(w_loaded, 16)
                sp.dma_start(v_win[0:META, 0, :], v_nat[PAD:PAD + META, :]).then_inc(w_loaded, 16)

                def load_index(grp, t):
                    sp.wait_ge(qi_done, t + START)
                    cols = bass.ds(t * P + (PAD + META), P)
                    for half in range(2):
                        sp.dma_start(qi[half * DH:half * DH + DH, :, :],
                                     proj[R_QI:R_QI + 512, cols].rearrange("(h d) c -> d h c", d=DH)).then_inc(qi_loaded, 16)
                    sp.dma_start(wi[:, :], proj[R_WI:R_WI + HEADS, cols]).then_inc(qi_loaded, 16)

                def load(grp, t):
                    sp.wait_ge(win_done, t + START)
                    q0 = t * P + (PAD + META)
                    w0 = t * P + META
                    cols = bass.ds(q0, P)
                    win = bass.ds(w0, WIN)
                    sp.dma_start(qa[:, :, :], proj[R_QA:R_QA + 512, cols].rearrange("(j p) c -> p j c", p=P)).then_inc(q_loaded, 16)
                    sp.dma_start(qb[:, :, :], proj[R_QB:R_QB + 512, cols].rearrange("(j p) c -> p j c", p=P)).then_inc(q_loaded, 16)
                    for half in range(2):
                        sp.dma_start(k_win[half * DH:half * DH + DH, :, META:WA],
                                     proj[R_KA:R_KA + P, win].rearrange("(k d) c -> d k c", d=DH)).then_inc(q_loaded, 16)
                    sp.dma_start(v_win[META:WH, 0, :], v_nat[bass.ds(w0, WH - META), :]).then_inc(q_loaded, 16)
                    sp.dma_start(v_win[:, 1, :], v_nat[bass.ds(w0 + (WH - META), WH), :]).then_inc(q_loaded, 16)

                for_groups(sp, load_index, None, load)
            q_dmas, qi_dmas = 6, 3

            @block.gpsimd
            def _(pool):
                make_identity(nc, pool, ident, id_ready)
                pool.iota(ints, pattern=[[-1, L]], base=META, channel_multiplier=1).then_inc(iota_ready, 1)
                pool.memset(minus_one[:, :], -1.0)
                for h in range(HEADS):
                    pool.memset(slope[:, h:h + 1], 2.0 ** -(h + 1))
                    pool.memset(neg_slope[:, h:h + 1], -2.0 ** -(h + 1))
                    pool.memset(inv_slope[:, h:h + 1], 2.0 ** (h + 1))
                pool.wait_ge(iota_used, 1 + START)
                for half in range(2):
                    pool.drain()
                    last = pool.iota(ints[half * DH:half * DH + DH, :], pattern=[[1, L]], base=-(META + CHUNK) - CHUNK * half,
                                     channel_multiplier=0)
                last.then_inc(iota_ready, 1)
                pool.drain()
                pool.wait_ge(iota_used, 2 + START)
                pool.iota(ints[:, 0:WIN], pattern=[[-1, WIN]], base=CHUNK, channel_multiplier=1).then_inc(iota_ready, 1)
                pool.drain()
                pool.wait_ge(const_ready, 1 + START)
                scale = pair_scale[:, :].rearrange("p (j a) -> p j a", a=1).to_broadcast([P, HEADS // 2, P])
                pool.wait_ge(wukt_ready, 2 + START)
                pool.tensor_tensor(wuk_t[:, :, :], wuk_t[:, :, :], scale, ALU.mult).then_inc(wukt_ready, 1)

                def index(grp, t):
                    pool.drain()
                    pool.wait_ge(qi_hi, t + 1 + START)
                    pool.tensor_tensor(qi_2[DH:P, :, :], qi[DH:P, :, :], f32(qi_2[DH:P, :, :]), ALU.subtract).then_inc(qi_lo, 1)
                    pool.drain()

                def one(tile, j):
                    return tile[:, j:j + 1]

                def judge(j, n):
                    pool.wait_ge(count_ready[j], n + 1 + START)
                    pool.sem_inc(count_seen, 1)
                    pool.tensor_scalar(one(kept, j), one(count, j), one(wanted, j), one(rise, j), ALU.is_ge, ALU.mult)
                    pool.drain()
                    pool.tensor_tensor(one(floor, j), one(floor, j), one(kept, j), ALU.add)

                def next_power(j, scales):
                    pool.drain()
                    if len(scales) == 2:
                        pool.tensor_scalar(one(cand, j), one(floor, j), scales[0], scales[1], ALU.mult, ALU.mult)
                    else:
                        pool.tensor_scalar(one(cand, j), one(floor, j), scales[0], TOP, ALU.mult, ALU.min)
                    pool.drain()
                    pool.tensor_scalar(one(neg_cand, j), one(cand, j), -1.0, None, ALU.mult)
                    pool.tensor_tensor(one(rise, j), one(cand, j), one(floor, j), ALU.subtract)
                    pool.drain()
                    pool.sem_inc(cand_ready[j], 1)

                def next_step(j, source):
                    if source is floor:
                        pool.drain()
                    pool.tensor_scalar(one(rise, j), one(source, j), 0.5, None, ALU.mult)
                    pool.drain()
                    pool.tensor_scalar(one(neg_cand, j), one(floor, j), -1.0, one(rise, j), ALU.mult, ALU.subtract).then_inc(cand_ready[j], 1)

                def select(grp):
                    rounds = grp.g * ROUNDS
                    pool.wait_ge(flipped, grp.g + 1 + START)
                    for tile, value in ((floor, 0.0), (rise, TINY), (neg_cand, -TINY)):
                        pool.memset(tile[:, DVE_TILES:TPG], value)
                    pool.drain()
                    for j in ACT_TILES:
                        pool.sem_inc(cand_ready[j], 1)
                    for n, scales in enumerate(POWERS):
                        for j in ACT_TILES:
                            judge(j, rounds + n)
                            next_power(j, scales)
                    for j in ACT_TILES:
                        judge(j, rounds + 8)
                        next_step(j, floor)
                    with pool.Fori(0, MANTISSA - 1) as i:
                        for j in ACT_TILES:
                            judge(j, i + (rounds + 9))
                            next_step(j, rise)
                    for j in ACT_TILES:
                        judge(j, rounds + ROUNDS - 1)
                    pool.drain()
                    for j in ACT_TILES:
                        pool.sem_inc(cand_ready[j], 1)

                def attend(grp, t):
                    pool.wait_ge(q_loaded, 16 * q_dmas * (t + 1) + START)
                    pool.tensor_tensor(qa_s[:, :, :], qa[:, :, :], scale, ALU.mult).then_inc(q_scaled, 1)

                    def divide(branch, rden):
                        pool.drain()
                        pool.wait_ge(raw_ready, 2 * t + 1 + branch + START)
                        o = o_nat[branch][:, :].rearrange("p (h d) -> p h d", h=HEADS)
                        pool.tensor_tensor(o, o, rden[:, :].rearrange("p (h a) -> p h a", a=1).to_broadcast([P, HEADS, DH]), ALU.mult).then_inc(o_ready, 1)

                    pool.wait_ge(exp_a, 4 * (t + 1) + START)
                    pool.tensor_tensor(rden_a[:, :], den_a[:, :], sink_e[:, :], ALU.add)
                    pool.drain()
                    pool.tensor_tensor(rden_a[:, :], rden_a[:, :], minus_one[:, :], ALU.pow)
                    divide(0, rden_a)
                    pool.wait_ge(p_ready, HEADS * (t + 1) + START)
                    pool.tensor_tensor(rden_b[:, :], den_b[:, :], minus_one[:, :], ALU.pow)
                    divide(1, rden_b)

                for_groups(pool, index, select, attend)

            @block.tensor
            def _(pe):
                pe.wait_ge(id_ready, 1 + START)
                pe.wait_ge(w_loaded, 96 + START)
                for j in range(HEADS // 2):
                    last = pe.transpose(ctx[:, j * P:j * P + P], wuk[:, 2 * j:2 * j + 2, :].rearrange("r a d -> r (a d)"), ident[:, :])
                last.then_inc(wukt_ready, 1)
                pe.wait_ge(wukt_ready, 3 + START)
                pe.wait_ge(const_ready, 1 + START)

                def index(grp, t):
                    nb = len(grp.blocks)

                    pe.wait_ge(misc_free, misc_use(grp, 0) + START)
                    pe.wait_ge(qi_lo, t + 1 + START)
                    for h in range(HEADS):
                        out = misc[:, h * META:h * META + META]
                        pe.matmul(out, qi_2[:, h, :], ki_hi[:, 0:META], start=True, stop=False)
                        pe.matmul(out, qi_2[:, h, :], ki_lo[:, 0:META], start=False, stop=True)
                    pe.drain()
                    pe.transpose(misc[:, 128:128 + HEADS], wi[:, :], ident[0:HEADS, 0:HEADS]).then_inc(misc_ready, 1)

                    for h in range(HEADS):
                        for b, (a0, wb) in enumerate(grp.blocks):
                            u, k = grp.use("big", h * nb + b)
                            pe.wait_ge(big_free[u], k + START)
                            for a in range(0, wb, 512):
                                n = min(512, wb - a)
                                cols = slice(META + a0 + a, META + a0 + a + n)
                                pe.matmul(big[u][:, a:a + n], qi_2[:, h, :], ki_hi[:, cols], start=True, stop=False)
                                last = pe.matmul(big[u][:, a:a + n], qi_2[:, h, :], ki_lo[:, cols], start=False, stop=True)
                            last.then_inc(big_ready[u], 1)
                    pe.drain()
                    pe.sem_inc(qi_done, 1)

                def attend(grp, t):
                    w = grp.width

                    pe.wait_ge(q_loaded, 16 * q_dmas * (t + 1) + START)
                    for n in range(2):
                        u, k = grp.use("turn", ("absorbed", n))
                        pe.wait_ge(turn_free[u], k + START)
                        r = slice(n * DH, n * DH + DH)
                        for j in range(HEADS // 2):
                            last = pe.matmul(turn[u][:, j * P:j * P + P], wuk_t[r, j, :], qb[r, j, :],
                                             start=True, stop=True)
                        last.then_inc(turn_ready[u], 1)

                    pe.wait_ge(misc_free, misc_use(grp, MISC_META) + START)
                    for n in range(2):
                        u, k = grp.use("turn", ("absorbed", n))
                        pe.wait_ge(turn_free[u], k + 1 + START)
                    for h in range(HEADS):
                        last = matmul3(pe, misc[:, h * META:h * META + META], ql_hi[:, h, :], ql_lo[:, h, :], c_hi[:, 0:META],
                                       c_lo[:, 0:META], True, True)
                    last.then_inc(misc_ready, 1)

                    def logits(h):
                        for b, (a0, wb) in enumerate(grp.blocks):
                            u, k = grp.use("big", ("logits", h, b))
                            pe.wait_ge(big_free[u], k + START)
                            for a in range(0, wb, 512):
                                n = min(512, wb - a)
                                cols = slice(META + a0 + a, META + a0 + a + n)
                                last = matmul3(pe, big[u][:, a:a + n], ql_hi[:, h, :], ql_lo[:, h, :], c_hi[:, cols], c_lo[:, cols], True, True)
                            last.then_inc(big_ready[u], 1)

                    def window_logits(n):
                        u, k = grp.use("big", ("window", n))
                        pe.wait_ge(big_free[u], k + START)
                        pe.wait_ge(q_scaled, t + 1 + START)
                        for h in range(4 * n, 4 * n + 4):
                            r = slice(h % 2 * DH, h % 2 * DH + DH)
                            at = h % 2 * 512 + h // 2 % 2 * 256
                            last = pe.matmul(big[u][:, at:at + WA], qa_s[r, h // 2, :], k_win[r, n, :],
                                             start=True, stop=True)
                        last.then_inc(big_ready[u], 1)

                    def transpose(item):
                        u, k = grp.use("turn", item)
                        if item[0] == "window":
                            pe.wait_ge(exp_a, 4 * t + item[1] + 1 + START)
                        elif item[2] == 0:
                            pe.wait_ge(p_ready, HEADS * t + item[1] + 1 + START)
                        pe.wait_ge(turn_free[u], k + START)
                        if item[0] == "window":
                            for m in range(4):
                                h, b = 2 * item[1] + m // 2, m % 2
                                last = pe.transpose(turn[u][0:WH, m * P:m * P + P], u_a[:, h, b * WH:b * WH + WH], ident[:, :])
                        else:
                            for m, (a, n) in enumerate(grp.key_fours[item[2]]):
                                last = pe.transpose(turn[u][0:n, m * P:m * P + P], u_b[item[1] % 3][:, a:a + n], ident[:, :])
                        last.then_inc(turn_ready[u], 1)

                    def weigh(item):
                        u, k = grp.use("turn", item)
                        v, _ = grp.use("pt", item)
                        if item == ("window", 0):
                            pe.wait_ge(misc_free, misc_use(grp, MISC_OA) + START)
                        if item[0] == "latent" and item[2] == 0:
                            pe.wait_ge(ctx_free, HEADS * t + item[1] + START)
                        pe.wait_ge(turn_free[u], k + 1 + START)
                        if item[0] == "window":
                            for m in range(4):
                                h, b = 2 * item[1] + m // 2, m % 2
                                kv = h // 4
                                last = pe.matmul(misc[:, h * DH:h * DH + DH], p_t[v][0:WH, m, :], v_win[:, b, kv * DH:kv * DH + DH],
                                                 start=(b == 0), stop=(b == 1))
                        else:
                            for m, (a, n) in enumerate(grp.key_fours[item[2]]):
                                last = pe.matmul(ctx[:, 0:P], c_nat[0:n, a:a + P], p_t[v][0:n, m, :],
                                                 start=(a == 0), stop=(a + n == w))
                        last.then_inc(pt_free[v], 1)
                        if item == ("window", 3):
                            pe.drain()
                            pe.sem_inc(misc_ready, 1)
                            pe.sem_inc(win_done, 1)

                    def transpose_output(branch):
                        u, k = grp.use("turn", ("out", branch))
                        pe.wait_ge(o_ready, 2 * t + 1 + branch + START)
                        pe.wait_ge(turn_free[u], k + START)
                        for j in range(4):
                            last = pe.transpose(turn[u][:, j * P:j * P + P], o_nat[branch][:, j * P:j * P + P], ident[:, :])
                        last.then_inc(turn_ready[u], 1)

                    logits(0)
                    logits(1)
                    for h in range(HEADS):
                        items = grp.turns(h)
                        transpose(items[0])
                        transpose(items[1])
                        if h == 0:
                            window_logits(0)
                            window_logits(1)
                        if h + 2 < HEADS:
                            logits(h + 2)
                        for f, item in enumerate(items):
                            weigh(item)
                            if f + 2 < len(items):
                                transpose(items[f + 2])
                    transpose_output(0)
                    pe.wait_ge(misc_free, misc_use(grp, MISC_OB) + START)
                    pe.wait_ge(ctx_free, HEADS * (t + 1) + START)
                    for h in range(HEADS):
                        last = pe.matmul(misc[:, h * DH:h * DH + DH], ctx_t[:, h, :], wuv[:, h, :], start=True, stop=True)
                    last.then_inc(misc_ready, 1)
                    transpose_output(1)

                for_groups(pe, index, None, attend)

            @block.scalar
            def _(act):
                act.wait_ge(wukt_ready, 1 + START)
                act.activation(wuk_t[:, :, :], ctx[:, :].rearrange("p (j r) -> p j r", j=4), ACT.Copy).then_inc(wukt_ready, 1)
                act.wait_ge(iota_ready, 3 + START)
                act.activation(base_a[:, META:WA], ints[:, 0:WIN], ACT.Abs).then_inc(iota_used, 1)
                act.wait_ge(const_ready, 1 + START)

                def index(grp, t):
                    nb = len(grp.blocks)
                    act.wait_ge(qi_loaded, 16 * qi_dmas * (t + 1) + START)
                    act.wait_ge(qi_done, t + START)
                    act.activation(qi_2[:, :, :], qi[:, :, :], ACT.Copy).then_inc(qi_hi, 1)
                    act.wait_ge(misc_ready, misc_use(grp, 0) + 1 + START)
                    act.wait_ge(wi_ready, t + START)
                    act.activation(w_idx[:, :], misc[:, 128:128 + HEADS], ACT.Copy, scale=HEADS ** -0.5 * DH ** -0.5)
                    act.activation(rel_meta[:, :, :], misc[:, 0:128].rearrange("p (h m) -> p h m", h=HEADS), ACT.Relu)
                    act.drain()
                    act.sem_inc(relm_ready, 1)
                    act.sem_inc(misc_free, 1)
                    for h in range(HEADS):
                        for b, (a0, wb) in enumerate(grp.blocks):
                            u, k = grp.use("big", h * nb + b)
                            v, kv = grp.use("rel", h * nb + b)
                            act.wait_ge(big_ready[u], k + 1 + START)
                            act.wait_ge(rel_free[v], kv + START)
                            act.activation(rel[v][:, 0:wb], big[u][:, 0:wb], ACT.Relu).then_inc(big_free[u], 1)

                def select(grp):
                    with act.Fori(0, ROUNDS) as i:
                        for j in ACT_TILES:
                            act.wait_ge(cand_ready[j], i + (grp.g * (ROUNDS + 1) + 1) + START)
                            act.activation(junk[j][:, 0:grp.seen[j]], score[:, j, 0:grp.seen[j]], ACT.Sign, bias=neg_cand[:, j:j + 1],
                                           accum_out=count[:, j:j + 1]).then_inc(count_ready[j], 1)

                def attend(grp, t):
                    w = grp.width
                    for n in range(2):
                        u, k = grp.use("turn", ("absorbed", n))
                        act.wait_ge(turn_ready[u], k + 1 + START)
                        act.activation(of_parity(ql_hi, n), turn[u][:, :].rearrange("p (j q) -> p j q", j=4), ACT.Copy).then_inc(ql_hi_ready, 1)

                    def latent_exp(h):
                        act.wait_ge(u_ready, HEADS * t + h + 1 + START)
                        act.activation(u_b[h % 3][:, 0:w], u_b[h % 3][:, 0:w], ACT.Exp, bias=bias_b[:, h:h + 1], scale=2.0 ** -(h + 1),
                                       accum_out=den_b[:, h:h + 1]).then_inc(p_ready, 1)

                    def window_exp(n):
                        if n == 0:
                            act.wait_ge(stats_a, t + 1 + START)
                            act.activation(sink_e[:, :], sink_e[:, :], ACT.Exp)
                        for h in (2 * n, 2 * n + 1):
                            last = act.activation(u_a[:, h, :], u_a[:, h, :], ACT.Exp, bias=bias_a[:, h:h + 1], scale=2.0 ** -(h + 1),
                                                  accum_out=den_a[:, h:h + 1])
                        last.then_inc(exp_a, 1)

                    def evacuate(item):
                        u, k = grp.use("turn", item)
                        v, kv = grp.use("pt", item)
                        four = grp.key_fours[item[2]] if item[0] == "latent" else [(0, WH)] * 4
                        rows, count = four[0][1], len(four)
                        act.wait_ge(turn_ready[u], k + 1 + START)
                        act.wait_ge(pt_free[v], kv + START)
                        act.activation(p_t[v][0:rows, 0:count, :], turn[u][0:rows, 0:count * P].rearrange("p (m q) -> p m q", m=count),
                                       ACT.Copy).then_inc(turn_free[u], 1)

                    def evacuate_context(h):
                        v, kv = grp.use("pt", ("latent", h, len(grp.key_fours) - 1))
                        act.wait_ge(pt_free[v], kv + 1 + START)
                        act.activation(ctx_t[:, h, :], ctx[:, 0:P], ACT.Copy).then_inc(ctx_free, 1)

                    def evacuate_product(branch, use_misc):
                        act.wait_ge(misc_ready, misc_use(grp, use_misc) + 1 + START)
                        act.activation(o_nat[branch][:, :], misc[:, :], ACT.Copy)
                        act.drain()
                        act.sem_inc(raw_ready, 1)
                        act.sem_inc(misc_free, 1)

                    def store(branch):
                        u, k = grp.use("turn", ("out", branch))
                        act.wait_ge(turn_ready[u], k + 1 + START)
                        act.wait_ge(attn_stored, 32 * t + START)
                        act.activation(o_t[branch][:, :, :], turn[u][:, :].rearrange("p (j q) -> p j q", j=4), ACT.Copy).then_inc(turn_free[u], 1)
                        act.drain()
                        act.dma_start(attn[branch * 512:branch * 512 + 512, bass.ds(t * P, P)].rearrange("(j p) c -> p j c", p=P),
                                      o_t[branch][:, :, :]).then_inc(attn_stored, 16)

                    latent_exp(0)
                    for h in range(HEADS):
                        if h + 1 < HEADS:
                            latent_exp(h + 1)
                        if h:
                            evacuate_context(h - 1)
                        if 2 <= h < 6:
                            window_exp(h - 2)
                        if h == HEADS - 1:
                            evacuate_product(0, MISC_OA)
                        for item in grp.turns(h):
                            evacuate(item)
                    evacuate_context(HEADS - 1)
                    store(0)
                    evacuate_product(1, MISC_OB)
                    store(1)

                for_groups(act, index, select, attend)
                act.wait_ge(attn_stored, 32 * SEQ // P + START)

            @block.vector
            def _(dve):
                dve.wait_ge(iota_ready, 1 + START)
                dve.tensor_copy(query_key[:, :], ints).then_inc(iota_used, 1)
                dve.wait_ge(iota_ready, 2 + START)
                dve.tensor_copy(limit[:, :], ints).then_inc(iota_used, 1)
                dve.memset(t_col[:, :], -float(P))
                dve.memset(neg_t_col[:, :], float(P))
                dve.memset(ti_col[:, :], -float(P))
                for h in range(HEADS):
                    dve.memset(pair_scale[h % 2 * DH:h % 2 * DH + DH, h // 2:h // 2 + 1], DH ** -0.5 * 2.0 ** (h + 1))
                dve.wait_ge(iota_used, 3 + START)
                dve.wait_ge(w_loaded, 96 + START)
                dve.memset(base_a[0:DH, META + 2 * CHUNK:WA], BIG)
                dve.memset(base_a[DH:P, META:META + CHUNK], BIG)
                dve.drain()
                dve.tensor_copy(dist_a[:, META:WA], base_a[:, META:WA])
                dve.tensor_tensor(sink_u[:, :], sink_u[:, :], inv_slope[:, :], ALU.mult)
                dve.drain()
                dve.sem_inc(const_ready, 1)

                def index(grp, t):
                    w = grp.width
                    nb = len(grp.blocks)

                    def dst(a, b):
                        return score[:, bass.ds(grp.i + TPG // 2 * grp.half, 1), a:b].rearrange("p a c -> p (a c)")

                    def src(h, a, b):
                        return dst(a, b) if h else hidden[:, a:b]

                    dve.drain()
                    dve.tensor_scalar(ti_col[:, :], ti_col[:, :], float(P), None, ALU.add)
                    dve.drain()
                    dve.tensor_scalar(hidden[:, 0:w], limit[:, 0:w], ti_col[:, :], BIG, ALU.is_ge, ALU.mult)
                    for h in range(HEADS):
                        def add(out, rel_h, prev, op, free=None):
                            ins = dve.scalar_tensor_tensor(out=out, in0=rel_h, scalar=w_idx[:, h:h + 1], in1=prev, op0=ALU.mult, op1=op)
                            if free is not None:
                                ins.then_inc(free, 1)
                        op = ALU.add if h else ALU.subtract
                        dve.drain()
                        if h == 0:
                            dve.wait_ge(relm_ready, t + 1 + START)
                        add(dst(0, META), rel_meta[:, h, :], src(h, 0, META), op)
                        for b, (a0, wb) in enumerate(grp.blocks):
                            u, k = grp.use("big", h * nb + b)
                            v, _ = grp.use("rel", h * nb + b)
                            dve.wait_ge(big_free[u], k + 1 + START)
                            add(dst(META + a0, META + a0 + wb), rel[v][:, 0:wb], src(h, META + a0, META + a0 + wb), op, rel_free[v])
                    dve.drain()
                    dve.sem_inc(wi_ready, 1)

                def select(grp):
                    def one(tile, j):
                        return tile[:, j:j + 1]

                    for j, w in enumerate(grp.seen):
                        dve.tensor_scalar(junk[j][:, 0:w], score[:, j, 0:w], 0.0, None, ALU.is_ge, ALU.add, accum_out=one(count, j))
                    dve.drain()
                    dve.tensor_scalar(sign[:, :], count[:, :], float(TOPK), 2.0, ALU.is_ge, ALU.mult)
                    dve.drain()
                    dve.tensor_scalar(sign[:, :], sign[:, :], -1.0, None, ALU.add)
                    dve.drain()
                    for j, w in enumerate(grp.seen):
                        slope_k = (2 * TOPK - 1 - w) * (0.5 if j < DVE_TILES else 1.0)
                        offset = (w + 1) * 0.5 if j < DVE_TILES else 0.0
                        dve.tensor_scalar(one(wanted, j), one(sign, j), slope_k, offset, ALU.mult, ALU.add)
                        dve.tensor_scalar(score[:, j, 0:w], score[:, j, 0:w], one(sign, j), None, ALU.mult)
                    dve.drain()
                    dve.sem_inc(flipped, 1)

                    def own(tile):
                        return tile[:, 0:DVE_TILES]

                    def judge():
                        for j, w in enumerate(grp.seen[:DVE_TILES]):
                            dve.tensor_scalar(junk[j][:, 0:w], score[:, j, 0:w], one(cand, j), None, ALU.is_ge, ALU.add,
                                              accum_out=one(count, j))
                        dve.drain()
                        for j in range(DVE_TILES):
                            dve.tensor_scalar(one(kept, j), one(count, j), one(wanted, j), one(rise, j), ALU.is_ge, ALU.mult)
                        dve.drain()
                        dve.tensor_tensor(own(floor), own(floor), own(kept), ALU.add)

                    def half_step(source):
                        dve.tensor_scalar(own(rise), own(source), 0.5, None, ALU.mult)
                        dve.drain()
                        dve.tensor_tensor(own(cand), own(floor), own(rise), ALU.add)
                        dve.drain()

                    for tile, value in ((floor, 0.0), (rise, TINY), (cand, TINY)):
                        dve.memset(own(tile), value)
                    dve.drain()
                    for scales in POWERS:
                        judge()
                        dve.drain()
                        if len(scales) == 2:
                            dve.tensor_scalar(own(cand), own(floor), scales[0], scales[1], ALU.mult, ALU.mult)
                        else:
                            dve.tensor_scalar(own(cand), own(floor), scales[0], TOP, ALU.mult, ALU.min)
                        dve.drain()
                        dve.tensor_tensor(own(rise), own(cand), own(floor), ALU.subtract)
                    judge()
                    dve.drain()
                    half_step(floor)
                    with dve.Fori(0, MANTISSA - 1):
                        judge()
                        half_step(rise)
                    judge()
                    dve.drain()
                    for j in ACT_TILES:
                        dve.wait_ge(cand_ready[j], (grp.g + 1) * (ROUNDS + 1) + START)
                    for j, w in enumerate(grp.seen):
                        x = score[:, j, 0:w]
                        spare, other = hidden[:, 0:w], dist[:, 0:w]
                        dve.tensor_scalar(spare, x, one(floor, j), None, ALU.is_le, ALU.add, accum_out=one(below, j))
                        dve.drain()
                        dve.tensor_scalar(spare, spare, TOP, None, ALU.mult)
                        dve.drain()
                        dve.tensor_tensor_reduce(other, x, spare, 1.0, TOP, ALU.add, ALU.min, one(nearest, j))
                        if j in ACT_TILES:
                            dve.tensor_scalar(one(wanted, j), one(wanted, j), 0.5, (w + 1) * 0.5, ALU.mult, ALU.add)
                        dve.tensor_scalar(one(more, j), one(below, j), -1.0, float(w), ALU.mult, ALU.add)
                        dve.drain()
                        dve.tensor_tensor(one(more, j), one(more, j), one(wanted, j), ALU.is_ge)
                        dve.tensor_tensor(one(nearest, j), one(nearest, j), one(floor, j), ALU.subtract)
                        dve.drain()
                        dve.tensor_tensor(one(nearest, j), one(nearest, j), one(more, j), ALU.mult)
                        dve.drain()
                        dve.tensor_tensor(one(floor, j), one(floor, j), one(nearest, j), ALU.add)
                        dve.drain()
                        dve.tensor_tensor(one(floor, j), one(floor, j), one(sign, j), ALU.mult)
                        dve.tensor_scalar(x, x, one(sign, j), None, ALU.mult)
                        dve.drain()
                        dve.tensor_scalar(other, x, one(floor, j), None, ALU.is_gt, ALU.add, accum_out=one(left, j))
                        dve.tensor_scalar(spare, x, one(floor, j), None, ALU.is_equal)
                        dve.drain()
                        dve.tensor_scalar(one(left, j), one(left, j), -1.0, float(TOPK), ALU.mult, ALU.add)
                        dve.tensor_tensor_scan(x, spare, spare, 0.0, ALU.add, ALU.max)
                        dve.drain()
                        dve.scalar_tensor_tensor(out=x, in0=x, scalar=one(left, j), in1=spare, op0=ALU.is_le, op1=ALU.mult)
                        dve.drain()
                        dve.tensor_tensor(x, x, other, ALU.add)
                        dve.drain()
                        dve.tensor_scalar(x, x, 0.5, BIG, ALU.is_lt, ALU.mult)
                        part = grp.parts[j // (TPG // 2)]
                        if w < part.width:
                            dve.memset(score[:, j, w:part.width], BIG)
                        if grp.g == 0:
                            dve.tensor_scalar(spare, limit[:, 0:w], float(P * j), BIG, ALU.is_ge, ALU.mult)
                            dve.drain()
                            dve.tensor_tensor(x, x, spare, ALU.max)
                        dve.drain()

                def attend(grp, t):
                    w = grp.width
                    dve.tensor_scalar(t_col[:, :], t_col[:, :], float(P), None, ALU.add)
                    dve.tensor_scalar(neg_t_col[:, :], neg_t_col[:, :], -float(P), None, ALU.add)
                    dve.drain()
                    dve.scalar_tensor_tensor(out=dist[:, 0:w], in0=query_key[:, 0:w], scalar=t_col[:, :],
                                             in1=score[:, bass.ds(grp.i + TPG // 2 * grp.half, 1), 0:w].rearrange("p a c -> p (a c)"), op0=ALU.add, op1=ALU.max)
                    dve.tensor_scalar(first_col[:, :], t_col[:, :], 1.0, BIG, ALU.is_lt, ALU.mult)
                    dve.tensor_scalar(dist_a[:, 0:META], query_key[:, 0:META], t_col[:, :], None, ALU.add)
                    dve.drain()
                    dve.scalar_tensor_tensor(out=dist[:, 0:w], in0=query_key[:, 0:w], scalar=neg_t_col[:, :], in1=dist[:, 0:w],
                                             op0=ALU.subtract, op1=ALU.max, reverse0=True)
                    dve.tensor_scalar(dist_a[:, META:META + CHUNK], base_a[:, META:META + CHUNK], first_col[:, :], None, ALU.max)
                    for n in range(2):
                        u, k = grp.use("turn", ("absorbed", n))
                        dve.wait_ge(ql_hi_ready, 2 * t + n + 1 + START)
                        dve.tensor_tensor(of_parity(ql_lo, n), turn[u][:, :].rearrange("p (j q) -> p j q", j=4),
                                          f32(of_parity(ql_hi, n)), ALU.subtract).then_inc(turn_free[u], 1)
                    dve.wait_ge(misc_ready, misc_use(grp, MISC_META) + 1 + START)
                    dve.tensor_tensor(u_meta[:, :, :], misc[:, 0:128].rearrange("p (h m) -> p h m", h=HEADS),
                                      dist[:, 0:META].rearrange("p (a m) -> p a m", a=1).to_broadcast([P, HEADS, META]), ALU.subtract).then_inc(misc_free, 1)
                    dve.drain()

                    def latent(h):
                        if h == 0:
                            u, k = grp.use("turn", 1)
                            dve.wait_ge(turn_ready[u], k + START)
                        if h > 2:
                            u, k = grp.use("turn", ("latent", h - 3, len(grp.key_fours) - 1))
                            dve.wait_ge(turn_ready[u], k + 1 + START)
                        out = u_b[h % 3]
                        dve.tensor_scalar(out[:, 0:META], u_meta[:, h, :], 1.0, None, ALU.mult, ALU.max, accum_out=max_b[:, h, 0:1])
                        for b, (a0, wb) in enumerate(grp.blocks):
                            u, k = grp.use("big", ("logits", h, b))
                            dve.wait_ge(big_ready[u], k + 1 + START)
                            dve.sem_inc(logits_seen, 1)
                            cols = slice(META + a0, META + a0 + wb)
                            dve.tensor_tensor_reduce(out[:, cols], big[u][:, 0:wb], dist[:, cols], 1.0, MARK,
                                                     ALU.subtract, ALU.max, max_b[:, h, b + 1:b + 2]).then_inc(big_free[u], 1)
                        dve.drain()
                        dve.tensor_reduce(max_1[:, h:h + 1], max_b[:, h, 0:len(grp.blocks) + 1], AX, ALU.max)
                        dve.drain()
                        dve.tensor_scalar(bias_b[:, h:h + 1], max_1[:, h:h + 1], -2.0 ** -(h + 1), None, ALU.mult).then_inc(u_ready, 1)

                    latent(0)
                    latent(1)
                    for n in range(2):
                        u, k = grp.use("big", ("window", n))
                        dve.wait_ge(big_ready[u], k + 1 + START)
                        dve.tensor_tensor(u_a[:, 4 * n:4 * n + 4, :].rearrange("p (j e) c -> p e j c", e=2),
                                          big[u][:, :].rearrange("p (e j c) -> p e j c", e=2, j=2)[:, :, :, 0:WA],
                                          dist_a[:, :].rearrange("p (a b c) -> p a b c", a=1, b=1).to_broadcast([P, 2, 2, WA]),
                                          ALU.subtract).then_inc(big_free[u], 1)
                    latent(2)
                    dve.tensor_reduce(max_a[:, :], u_a[:, :, :], AX, ALU.max)
                    dve.drain()
                    dve.tensor_tensor(max_a[:, :], max_a[:, :], sink_u[:, :], ALU.max)
                    dve.drain()
                    dve.tensor_tensor(bias_a[:, :], max_a[:, :], neg_slope[:, :], ALU.mult)
                    dve.tensor_tensor(sink_e[:, :], sink_u[:, :], max_a[:, :], ALU.subtract)
                    dve.drain()
                    dve.tensor_tensor(sink_e[:, :], sink_e[:, :], slope[:, :], ALU.mult).then_inc(stats_a, 1)
                    for h in range(3, HEADS):
                        latent(h)

                for_groups(dve, index, select, attend)


def mix_and_ffn(nc, proj, attn, h0, w_o_a, w_o_b, w_out, ln1_g, ln1_b, w_gate, w_up, w_down, ln2_g, ln2_b, out):
    with Scope(nc, "ff") as s:
        ident, half = s.sb("ident", [P, P]), s.sb("half", [P, 1])
        ln = [s.sb(f"ln{n}", [P, D]) for n in range(4)]
        raw = [s.sb(f"raw{u}", [P, D]) for u in range(2)]
        w_hi, w_lo = [s.sb(f"w_hi{u}", [P, D], F32R) for u in range(2)], [s.sb(f"w_lo{u}", [P, D], F32R) for u in range(2)]
        resid = s.sb("resid", [P, TPG, D])
        att = s.sb("att", [P, KT, GROUP])
        h1_hi, h1_lo = s.sb("h1_hi", [P, KT, GROUP], F32R), s.sb("h1_lo", [P, KT, GROUP], F32R)
        f_hi, f_lo = s.sb("f_hi", [P, FT, GROUP], F32R), s.sb("f_lo", [P, FT, GROUP], F32R)
        gates = [s.sb(f"gates{u}", [P, 2, GROUP]) for u in range(2)]
        part_a, part_b, mixed = s.sb("part_a", [P, GROUP]), s.sb("part_b", [P, GROUP]), s.sb("mixed", [P, GROUP])
        silu, feature = [part_a, part_b], mixed
        stats, mean_var = s.sb("stats", [P, TPG, 2, 6]), s.sb("mv", [P, TPG, 2])
        var_eps, rstd = s.sb("ve", [P, TPG]), s.sb("rstd", [P, TPG])
        bank = s.ps("bank", [P, 8, GROUP])

        const_ready, ln_loaded = s.sem("const_ready"), s.sem("ln_loaded")
        w_loaded, hi_ready, lo_ready, w_used = s.sems("w_loaded"), s.sems("hi_ready"), s.sems("lo_ready"), s.sems("w_used")
        att_loaded, att_hi, att_lo, h0_loaded = s.sem("att_loaded"), s.sem("att_hi"), s.sem("att_lo"), s.sem("h0_loaded")
        gates_loaded, gates_used = s.sems("gates_loaded"), s.sems("gates_used")
        mix_ready, mix_hi, mix_lo = s.sem("mix_ready"), s.sem("mix_hi"), s.sem("mix_lo")
        pair_free = s.sems("pair_free", TPG)
        sums_ready = s.sem("sums_ready")
        var_ready, rstd_ready = s.sem("var_ready"), s.sem("rstd_ready")
        h1_ready, h1_turned, h1_hi_ready, h1_lo_ready = s.sem("h1_ready"), s.sem("h1_turned"), s.sem("h1_hi_ready"), s.sem("h1_lo_ready")
        silu_ready, feat_ready, feat_hi, feat_lo = s.sem("silu_ready"), s.sems("feat_ready"), s.sem("feat_hi"), s.sem("feat_lo")
        h2_ready, out_stored = s.sem("h2_ready"), s.sem("out_stored")

        Y, M, F, Z = 0, 4, 8, 8 + FT
        PAIRS = Z + FT // 2
        ATT = Z + FT // 2 - KT
        MIXES = 4

        def piece(tile, k):
            return tile[:, bass.ds(k, 1), :].rearrange("p a c -> p (a c)")

        with nc.Block() as block:
            @block.sync
            def _(sp):
                s.begin(sp)
                for n, v in enumerate((ln1_g, ln1_b, ln2_g, ln2_b)):
                    sp.dma_start(ln[n][:, :], v.to_broadcast([P, D])).then_inc(ln_loaded, 16)
                cols = lambda w, c: w.rearrange("(k p) c -> p k c", p=P)[:, :, bass.ds(c * P, P)]
                rows = lambda w, c: w[bass.ds(c * P, P), :]
                as_k = lambda t: t[:, :].rearrange("p (k c) -> p k c", c=P)

                def load_att(g):
                    sp.wait_ge(att_lo, KT * g + START)
                    sp.dma_start(att[:, :, :], attn.rearrange("(k p) c -> p k c", p=P)[:, :, bass.ds(g * GROUP, GROUP)]).then_inc(att_loaded, 16)

                def group(g, more):
                    def chunk(u, k, parts):
                        sp.wait_ge(lo_ready[u], g * PAIRS + k + START)
                        for dst, src in parts:
                            sp.dma_start(dst, src).then_inc(w_loaded[u], 16)

                    with sp.Fori(0, 4) as i:
                        for u in range(2):
                            c = 2 * i + u
                            chunk(u, Y + i, [(as_k(raw[u])[:, 0:4, :], cols(w_o_a, c)), (as_k(raw[u])[:, 4:8, :], cols(w_o_b, c))])
                            sp.wait_ge(gates_used[u], 4 * g + i + START)
                            for b in range(2):
                                sp.dma_start(gates[u][:, b, :], proj[bass.ds(c * P + R_GATE + b * D, P), bass.ds(g * GROUP + PAD + META, GROUP)]).then_inc(gates_loaded[u], 16)
                    for u in range(2):
                        chunk(u, M, [(raw[u][:, :], rows(w_out, u))])
                    sp.wait_ge(out_stored, 16 * TPG * g + START)
                    sp.dma_start(resid[:, :, :], h0[bass.ds(g * GROUP + META, GROUP), :].rearrange("(a p) d -> p a d", p=P)).then_inc(h0_loaded, 16)
                    with sp.Fori(1, 4) as i:
                        for u in range(2):
                            chunk(u, M + i, [(raw[u][:, :], rows(w_out, 2 * i + u))])
                    with sp.Fori(0, FT) as i:
                        chunk(0, F + i, [(as_k(raw[0]), cols(w_gate, i))])
                        chunk(1, F + i, [(as_k(raw[1]), cols(w_up, i))])
                    if more:
                        load_att(g + 1)
                    with sp.Fori(0, FT // 2) as i:
                        for u in range(2):
                            chunk(u, Z + i, [(raw[u][:, :], rows(w_down, 2 * i + u))])

                load_att(0)
                with sp.Fori(0, NG - 1) as g:
                    group(g, True)
                group(NG - 1, False)

            @block.gpsimd
            def _(pool):
                pool.memset(half[:, :], -0.5)
                make_identity(nc, pool, ident, const_ready)
                pool.drain()

                def low_att(g, k):
                    pool.wait_ge(att_hi, KT * g + k + 1 + START)
                    pool.tensor_tensor(piece(h1_lo, k), piece(att, k), f32(piece(h1_hi, k)), ALU.subtract).then_inc(att_lo, 1)

                def low_part(g, u, k):
                    pool.wait_ge(hi_ready[u], g * PAIRS + k + 1 + START)
                    pool.tensor_tensor(w_lo[u][:, :], raw[u][:, :], f32(w_hi[u][:, :]), ALU.subtract).then_inc(lo_ready[u], 1)

                def inverse_root(g, n, a):
                    pool.wait_ge(var_ready, 2 * TPG * g + n * TPG + a + 1 + START)
                    pool.tensor_tensor(rstd[:, a:a + 1], var_eps[:, a:a + 1], half[:, :], ALU.pow).then_inc(rstd_ready, 1)

                def group(g, more):
                    with pool.Fori(2, F) as i:
                        for u in range(2):
                            low_part(g, u, i)
                    for a in range(TPG):
                        inverse_root(g, 0, a)
                    with pool.Fori(F, ATT) as i:
                        for u in range(2):
                            low_part(g, u, i)
                    with pool.Fori(ATT, PAIRS) as i:
                        for u in range(2):
                            low_part(g, u, i)
                        if more:
                            low_att(g + 1, i - ATT)
                    if more:
                        low_part(g + 1, 0, Y)
                    for a in range(TPG):
                        if more and a < 3:
                            low_part(g + 1, (a + 1) % 2, Y + (a + 1) // 2)
                        inverse_root(g, 1, a)

                with pool.Fori(0, KT) as k:
                    low_att(0, k)
                with pool.Fori(Y, Y + 2) as i:
                    for u in range(2):
                        low_part(0, u, i)
                with pool.Fori(0, NG - 1) as g:
                    group(g, True)
                group(NG - 1, False)

            @block.scalar
            def _(act):
                def high_att(g, k):
                    act.wait_ge(att_loaded, 16 * (g + 1) + START)
                    act.activation(piece(h1_hi, k), piece(att, k), ACT.Copy).then_inc(att_hi, 1)

                def high_part(g, u, k, double=False):
                    act.wait_ge(w_loaded[u], (16 * (PAIRS + 4) * g + (32 * (k + 1) if double else 16 * (k + 1) + 64)) + START)
                    act.wait_ge(w_used[u], g * PAIRS + k + START)
                    act.activation(w_hi[u][:, :], raw[u][:, :], ACT.Copy).then_inc(hi_ready[u], 1)

                def high_mix(g, n):
                    act.wait_ge(mix_ready, 8 * g + n + 1 + START)
                    act.activation(piece(f_hi, 8 + n), mixed[:, :], ACT.Copy).then_inc(mix_hi, 1)

                def mixes(g, first, last):
                    for n in range(first, last):
                        if n < 7:
                            high_part(g, (n + 1) % 2, Y + (n + 1) // 2, True)
                        else:
                            high_part(g, 0, M)
                        high_mix(g, n)

                def group(g, more):
                    mixes(g, 4, 8)
                    high_part(g, 1, M)
                    with act.Fori(1, 4) as i:
                        for u in range(2):
                            high_part(g, u, M + i)
                    high_part(g, 0, F)
                    high_part(g, 1, F)
                    with act.Fori(0, TPG) as a:
                        for b in range(2):
                            act.wait_ge(h1_turned, 2 * TPG * g + 2 * a + b + 1 + START)
                            act.activation(h1_hi[:, 4 * b:4 * b + 4, bass.ds(a * P, P)],
                                           bank[:, bass.ds(2 * a + b, 1), :].rearrange("p e (k c) -> p (e k) c", c=P), ACT.Copy).then_inc(h1_hi_ready, 1)

                    def gate(n, i):
                        act.wait_ge(w_used[0], g * PAIRS + F + 2 * i + n + 1 + START)
                        act.wait_ge(feat_ready[n], FT // 2 * g + i + START)
                        act.activation(silu[n][:, :], bank[:, 4 * n, :], ACT.Silu).then_inc(silu_ready, 1)
                        act.wait_ge(feat_ready[n], FT // 2 * g + i + 1 + START)
                        act.activation(piece(f_hi, 2 * i + n), feature[:, :], ACT.Copy).then_inc(feat_hi, 1)

                    with act.Fori(0, FT // 2 - 1) as i:
                        for n in range(2):
                            high_part(g, 0, F + 2 * i + n + 1)
                            gate(n, i)
                            high_part(g, 1, F + 2 * i + n + 1)
                    high_part(g, 0, F + FT - 1)
                    gate(0, FT // 2 - 1)
                    high_part(g, 1, F + FT - 1)
                    high_part(g, 0, Z)
                    gate(1, FT // 2 - 1)
                    high_part(g, 1, Z)
                    with act.Fori(Z + 1, ATT) as i:
                        for u in range(2):
                            high_part(g, u, i)
                    with act.Fori(ATT, PAIRS) as i:
                        for u in range(2):
                            high_part(g, u, i)
                        if more:
                            high_att(g + 1, i - ATT)
                    if more:
                        high_part(g + 1, 0, Y, True)
                        mixes(g + 1, 0, 4)
                    with act.Fori(0, TPG) as a:
                        act.wait_ge(h2_ready, TPG * g + a + 1 + START)
                        act.dma_start(out[0, bass.ds(g * GROUP + a * P, P), :], piece(resid, a)).then_inc(out_stored, 16)

                with act.Fori(0, KT) as k:
                    high_att(0, k)
                high_part(0, 0, Y, True)
                mixes(0, 0, 4)
                with act.Fori(0, NG - 1) as g:
                    group(g, True)
                group(NG - 1, False)
                act.wait_ge(out_stored, 16 * TPG * NG + START)

            @block.vector
            def _(dve):
                dve.wait_ge(ln_loaded, 64 + START)

                def mix(g, u, i):
                    n = 2 * i + u
                    dve.wait_ge(gates_loaded[u], 32 * (4 * g + i + 1) + START)
                    dve.wait_ge(w_used[u], g * PAIRS + Y + i + 1 + START)
                    dve.tensor_tensor(part_a[:, :], bank[:, 2 * u, :], gates[u][:, 0, :], ALU.mult)
                    dve.tensor_tensor(part_b[:, :], bank[:, 2 * u + 1, :], gates[u][:, 1, :], ALU.mult)
                    dve.drain()
                    dve.sem_inc(gates_used[u], 1)
                    dve.sem_inc(pair_free[u], 1)
                    dve.tensor_tensor(mixed[:, :], part_a[:, :], part_b[:, :], ALU.add).then_inc(mix_ready, 1)
                    dve.wait_ge(mix_hi, 8 * g + n + 1 + START)
                    dve.tensor_tensor(piece(f_lo, 8 + n), mixed[:, :], f32(piece(f_hi, 8 + n)), ALU.subtract).then_inc(mix_lo, 1)
                    dve.drain()

                def group(g, more):
                    with dve.Fori(2, 4) as i:
                        for u in range(2):
                            mix(g, u, i)

                    def layer_norm(stage, n, done, between):
                        def add(a):
                            if a < TPG - 1:
                                dve.wait_ge(sums_ready, (TPG - 1) * (2 * g + stage) + a + 1 + START)
                            else:
                                dve.wait_ge(w_used[1], g * PAIRS + (PAIRS if stage else F) + START)
                            for b in range(2):
                                last = dve.scalar_tensor_tensor(out=resid[:, a, b * 512:b * 512 + 512], in0=resid[:, a, b * 512:b * 512 + 512],
                                                                scalar=ALPHA, in1=bank[:, 2 * a + b, :], op0=ALU.mult, op1=ALU.add)
                            last.then_inc(pair_free[a], 1)
                            dve.drain()

                        def statistics(a):
                            for b in range(2):
                                dve.bn_stats(stats[:, a, b, :], resid[:, a, b * 512:b * 512 + 512])
                            dve.drain()
                            dve.bn_aggr(mean_var[:, a, :], stats[:, a, :, :])
                            dve.drain()
                            dve.tensor_scalar(var_eps[:, a:a + 1], mean_var[:, a, 1:2], 1e-5, None, ALU.add).then_inc(var_ready, 1)
                            dve.scalar_tensor_tensor(out=resid[:, a, :], in0=resid[:, a, :], scalar=mean_var[:, a, 0:1], in1=ln[n][:, :],
                                                     op0=ALU.subtract, op1=ALU.mult)

                        def finish(a):
                            dve.wait_ge(rstd_ready, 2 * TPG * g + TPG * stage + a + 1 + START)
                            dve.scalar_tensor_tensor(out=resid[:, a, :], in0=resid[:, a, :], scalar=rstd[:, a:a + 1], in1=ln[n + 1][:, :],
                                                     op0=ALU.mult, op1=ALU.add).then_inc(done, 1)

                        if between:
                            add(0)
                            add(1)
                        for a in range(TPG):
                            if a >= (2 if between else 0):
                                add(a)
                            statistics(a)
                            if a:
                                finish(a - 1)
                            if between:
                                between(a)
                        dve.drain()
                        finish(TPG - 1)

                    dve.wait_ge(h0_loaded, 16 * (g + 1) + START)
                    layer_norm(0, 0, h1_ready, None)
                    with dve.Fori(0, TPG) as a:
                        for b in range(2):
                            dve.wait_ge(h1_hi_ready, 2 * TPG * g + 2 * a + b + 1 + START)
                            dve.tensor_tensor(h1_lo[:, 4 * b:4 * b + 4, bass.ds(a * P, P)],
                                              bank[:, bass.ds(2 * a + b, 1), :].rearrange("p e (k c) -> p (e k) c", c=P),
                                              f32(h1_hi[:, 4 * b:4 * b + 4, bass.ds(a * P, P)]), ALU.subtract).then_inc(h1_lo_ready, 1)
                    with dve.Fori(0, FT // 2) as i:
                        for n in range(2):
                            t = 2 * i + n
                            dve.wait_ge(silu_ready, FT * g + t + 1 + START)
                            dve.wait_ge(w_used[1], g * PAIRS + F + t + 1 + START)
                            dve.tensor_tensor(feature[:, :], silu[n][:, :], bank[:, 4 * n + 1, :], ALU.mult).then_inc(feat_ready[n], 1)
                            dve.wait_ge(feat_hi, FT * g + t + 1 + START)
                            dve.tensor_tensor(piece(f_lo, t), feature[:, :], f32(piece(f_hi, t)), ALU.subtract).then_inc(feat_lo, 1)
                            dve.drain()
                    layer_norm(1, 2, h2_ready, (lambda a: mix(g + 1, a % 2, a // 2)) if more else None)

                for a in range(4):
                    mix(0, a % 2, a // 2)
                with dve.Fori(0, NG - 1) as g:
                    group(g, True)
                group(NG - 1, False)

            @block.tensor
            def _(pe):
                pe.wait_ge(const_ready, 1 + START)
                with pe.Fori(0, NG) as g:
                    def weights(u, k):
                        pe.wait_ge(hi_ready[u], g * PAIRS + k + 1 + START)
                        pe.wait_ge(lo_ready[u], g * PAIRS + k + 1 + START)

                    def bank_pair(a, norms):
                        mixes = MIXES if a < 2 else 0
                        pe.wait_ge(pair_free[a], (mixes + 2) * g + mixes + norms + START)

                    def turned(dst, u, first, count, hi, lo, hi_first):
                        for c in range(count):
                            w = slice((first + c) * P, (first + c) * P + P)
                            last = matmul3(pe, dst, w_hi[u][:, w], w_lo[u][:, w], hi[:, hi_first + c, :], lo[:, hi_first + c, :],
                                           c == 0, c == count - 1)
                        return last

                    with pe.Fori(0, 4) as i:
                        for u in range(2):
                            pe.wait_ge(att_lo, KT * (g + 1) + START)
                            weights(u, Y + i)
                            pe.wait_ge(pair_free[u], (MIXES + 2) * g + i + START)
                            turned(bank[:, 2 * u, :], u, 0, 4, h1_hi, h1_lo, 0)
                            turned(bank[:, 2 * u + 1, :], u, 4, 4, h1_hi, h1_lo, 4).then_inc(w_used[u], 1)

                    def natural(u, first, last_one, hi, lo, at, order=range(TPG), norms=None):
                        for a in order:
                            if norms is not None:
                                bank_pair(a, norms)
                            for b in range(2):
                                q, c = slice(a * P, a * P + P), slice(b * 512, b * 512 + 512)
                                last = matmul3(pe, bank[:, 2 * a + b, :], hi[:, at, q], lo[:, at, q], w_hi[u][:, c], w_lo[u][:, c],
                                               first, last_one)
                            if last_one and a < TPG - 1:
                                last.then_inc(sums_ready, 1)
                        last.then_inc(w_used[u], 1)

                    for c in range(8):
                        weights(c % 2, M + c // 2)
                        pe.wait_ge(mix_lo, 8 * g + c + 1 + START)
                        natural(c % 2, c == 0, c == 7, f_hi, f_lo, 8 + c, (2, 3, 0, 1) if c == 0 else range(TPG), 0 if c == 0 else None)
                    for a in range(TPG):
                        pe.wait_ge(h1_ready, TPG * g + a + 1 + START)
                        for b in range(2):
                            for c in range(4):
                                last = pe.transpose(bank[:, 2 * a + b, c * P:c * P + P], resid[:, a, (4 * b + c) * P:(4 * b + c) * P + P], ident[:, :])
                            last.then_inc(h1_turned, 1)
                    with pe.Fori(0, FT // 2) as i:
                        for n in range(2):
                            pe.wait_ge(h1_lo_ready, 2 * TPG * (g + 1) + START)
                            pe.wait_ge(feat_ready[n], FT // 2 * g + i + START)
                            for u in range(2):
                                weights(u, F + 2 * i + n)
                                turned(bank[:, 4 * n + u, :], u, 0, 8, h1_hi, h1_lo, 0).then_inc(w_used[u], 1)
                    for c in range(FT):
                        weights(c % 2, Z + c // 2)
                        pe.wait_ge(feat_lo, FT * g + c + 1 + START)
                        if c == 0:
                            pe.wait_ge(feat_ready[0], FT // 2 * (g + 1) + START)
                            pe.wait_ge(feat_ready[1], FT // 2 * (g + 1) + START)
                        natural(c % 2, c == 0, c == FT - 1, f_hi, f_lo, c)


def build(nc, x, meta_tokens, ln0_g, ln0_b, w_in, b_gate, kv_norm_g, w_uk, w_uv, k_idx_g, k_idx_b, sinks, w_o_a, w_o_b,
          w_out, ln1_g, ln1_b, w_ff_gate, w_ff_up, w_ff_down, ln2_g, ln2_b, out, phases=4):
    h0 = nc.dram_tensor("h0", (L, D), F32, kind="Internal").ap()
    proj = nc.dram_tensor("proj", (4096, LP), F32, kind="Internal").ap()
    v_nat = nc.dram_tensor("v_nat", (LP, P), F32, kind="Internal").ap()
    attn = nc.dram_tensor("attn", (D, SEQ), F32, kind="Internal").ap()
    project(nc, x, meta_tokens, ln0_g, ln0_b, w_in, b_gate, h0, proj, v_nat)
    if phases > 1:
        with Scope(nc, "keys") as s:
            keys = (s.sb("c_nat", [P, 17 * P]), s.sb("c_hi", [P, L], F32R), s.sb("c_lo", [P, L], F32R),
                    s.sb("ki_hi", [P, L], F32R), s.sb("ki_lo", [P, L], F32R))
            prepare_keys(nc, proj, kv_norm_g, k_idx_g, k_idx_b, v_nat, keys)
            if phases > 2:
                attention(nc, proj, v_nat, w_uk, w_uv, sinks, attn, keys)
    if phases > 3:
        mix_and_ffn(nc, proj, attn, h0, w_o_a[0], w_o_b[0], w_out[0], ln1_g, ln1_b, w_ff_gate[0], w_ff_up[0], w_ff_down[0],
                    ln2_g, ln2_b, out)


_INS = ["x", "meta_tokens", "ln0_g", "ln0_b", "w_in", "b_gate", "kv_norm_g", "w_uk", "w_uv", "k_idx_g", "k_idx_b", "sinks",
        "w_o_a", "w_o_b", "w_out", "ln1_g", "ln1_b", "w_ff_gate", "w_ff_up", "w_ff_down", "ln2_g", "ln2_b"]


def kernel(**inputs):
    import numpy as np
    import concourse.bacc as bacc
    from concourse.bass_utils import run_bass_kernel_spmd

    nc = bacc.Bacc("TRN2", target_bir_lowering=False, num_devices=1)
    arrays, args = {}, []
    for name in _INS:
        a = np.ascontiguousarray(inputs[name])
        arrays[f"in_{name}"] = a
        args.append(nc.dram_tensor(f"in_{name}", a.shape, mybir.dt.from_np(a.dtype), kind="ExternalInput").ap())
    args.append(nc.dram_tensor("out_0", (1, SEQ, D), F32, kind="ExternalOutput").ap())
    build(nc, *args)
    r = run_bass_kernel_spmd(nc, [arrays], core_ids=[0])
    return r.results[0]["out_0"]
```
